# Optimizing a Trainium2 kernel written in Bass

```python
import math
import jax
import jax.numpy as jnp
from jax import lax
import numpy as np

D_MODEL = 1024
BATCH = 1
SEQ = 1024
DEPTH = 2

GRID_W = 64
CTX_LEN = 256

NA_HEADS = 8
NA_HEAD_DIM = 64
NA_W = NA_HEADS * NA_HEAD_DIM
NA_KH = 8
NA_KW = 16

HY_W = 256
HY_ORDER = 2
HY_SHORT = 3
HY_BANDS = 8
HY_EMB = 1 + 2 * HY_BANDS
HY_FFN = 64
HY_FAST_DECAY = 0.3
HY_SLOW_DECAY = 1.5
HY_TARGET = 1e-2

RET_HEADS = 4
RET_HEAD_DIM = 64
RET_W = RET_HEADS * RET_HEAD_DIM
RET_CHUNK = 128

MIX_W = NA_W + HY_W + RET_W
IN_W = 4 * NA_W + 4 * HY_W + 4 * RET_W
ROPE_BASE = 10000.0
EPS = 1e-6
NEG_INF = -1e30
F32 = jnp.float32

kernel_name = 'hybrid_na_hyena_retention_dit_block'

def rms_norm(x, eps=EPS):
    xf = x.astype(F32)
    return (xf * lax.rsqrt(jnp.mean(xf * xf, axis=-1, keepdims=True) + eps)).astype(x.dtype)

def ada_modulation(cond, ada_w, ada_b):
    return jax.nn.silu(cond) @ ada_w + ada_b

def modulate(h, mod, norm_w):
    shift, scale, gate = jnp.split(mod, 3, axis=-1)
    return rms_norm(h) * norm_w * (1 + scale) + shift, gate

def split_projection(u):
    sizes = (3 * NA_W, NA_W, 3 * HY_W, HY_W, 3 * RET_W, RET_W)
    cuts = [int(s) for s in np.cumsum(sizes)[:-1]]
    return jnp.split(u, cuts, axis=-1)

def heads(u, n_heads, head_dim):
    return u.reshape(u.shape[0], u.shape[1], n_heads, head_dim)

def na_queries(u_na, q_gain):
    q = heads(u_na[..., :NA_W], NA_HEADS, NA_HEAD_DIM)
    return rms_norm(q) * q_gain * (NA_HEAD_DIM ** -0.5)

def na_keys_values(u_na, k_gain):
    k = heads(u_na[..., NA_W:2 * NA_W], NA_HEADS, NA_HEAD_DIM)
    v = heads(u_na[..., 2 * NA_W:], NA_HEADS, NA_HEAD_DIM)
    return rms_norm(k) * k_gain, v

def neighborhood_attention(q, k, v, k_ctx, v_ctx, rpb):
    B, L, H, Dh = q.shape
    rows = L // GRID_W
    kh = min(NA_KH, rows)
    r = jnp.arange(rows)
    row_idx = jnp.clip(r - kh // 2, 0, rows - kh)[:, None] + jnp.arange(kh)[None, :]
    cq = jnp.arange(GRID_W)
    ck = jnp.arange(GRID_W)
    col_start = jnp.clip(cq - NA_KW // 2, 0, GRID_W - NA_KW)
    col_ok = (ck[None, :] >= col_start[:, None]) & (ck[None, :] < col_start[:, None] + NA_KW)
    dr = row_idx - r[:, None] + (NA_KH - 1)
    dc = jnp.clip(ck[None, :] - cq[:, None] + (NA_KW - 1), 0, 2 * NA_KW - 2)
    bias = rpb[:, dr[:, None, :, None], dc[None, :, None, :]].astype(F32)

    qg = q.reshape(B, rows, GRID_W, H, Dh)
    kg = k.reshape(B, rows, GRID_W, H, Dh)[:, row_idx]
    vg = v.reshape(B, rows, GRID_W, H, Dh)[:, row_idx]
    s_loc = jnp.einsum('brqhd,brjkhd->bhrqjk', qg, kg).astype(F32) + bias[None]
    s_loc = jnp.where(col_ok[:, None, :], s_loc, NEG_INF)
    s_ctx = jnp.einsum('brqhd,bchd->bhrqc', qg, k_ctx).astype(F32)
    n_loc = kh * GRID_W
    s = jnp.concatenate([s_loc.reshape(B, H, rows, GRID_W, n_loc), s_ctx], axis=-1)
    p = jax.nn.softmax(s, axis=-1).astype(v.dtype)
    p_loc = p[..., :n_loc].reshape(B, H, rows, GRID_W, kh, GRID_W)
    p_ctx = p[..., n_loc:]
    o = jnp.einsum('bhrqjk,brjkhd->brqhd', p_loc, vg) + jnp.einsum('bhrqc,bchd->brqhd', p_ctx, v_ctx)
    return o.reshape(B, L, H * Dh)

def context_attention(q, k, v):
    B, Lc, H, Dh = q.shape
    s = jnp.einsum('bqhd,bkhd->bhqk', q, k).astype(F32)
    p = jax.nn.softmax(s, axis=-1).astype(v.dtype)
    return jnp.einsum('bhqk,bkhd->bqhd', p, v).reshape(B, Lc, H * Dh)

def hyena_filter_spectrum(L, w1, b1, w2, b2, w3, sin_freq):
    t = jnp.linspace(0.0, 1.0, L, dtype=F32)[:, None]
    omega = 2.0 * math.pi * jnp.arange(L, dtype=F32)[:, None] / L
    bands = jnp.linspace(1e-4, HY_BANDS - 1, HY_BANDS, dtype=F32)[None, :]
    z = jnp.concatenate([t, jnp.cos(bands * omega), -jnp.sin(bands * omega)], axis=-1)
    h = jnp.sin(sin_freq[0] * (z @ w1 + b1))
    h = jnp.sin(sin_freq[1] * (h @ w2 + b2))
    h = (h @ w3).astype(F32).reshape(L, HY_ORDER, 2, HY_W)
    deltas = jnp.abs(jnp.linspace(math.log(HY_TARGET) / HY_SLOW_DECAY,
                                  math.log(HY_TARGET) / HY_FAST_DECAY, HY_W, dtype=F32))
    h = h * jnp.exp(-t * deltas)[:, None, None, :]
    h_fwd = h[:, :, 0]
    h_bwd = h[1:, :, 1][::-1]
    filt = jnp.concatenate([h_fwd, jnp.zeros((1, HY_ORDER, HY_W), F32), h_bwd], axis=0)
    filt = filt / jnp.sum(jnp.abs(filt), axis=0, keepdims=True)
    return jnp.fft.rfft(filt, axis=0)

def fft_long_conv(u, filt_f, skip):
    L = u.shape[1]
    uf = u.astype(F32)
    y = jnp.fft.irfft(jnp.fft.rfft(uf, n=2 * L, axis=1) * filt_f[None], n=2 * L, axis=1)[:, :L]
    return (y + uf * skip).astype(u.dtype)

def short_conv(u, w, b):
    L = u.shape[1]
    pad = HY_SHORT // 2
    up = jnp.pad(u, ((0, 0), (pad, pad), (0, 0)))
    return sum(up[:, j:j + L] * w[j] for j in range(HY_SHORT)) + b

def hyena_mixer(u, conv_w, conv_b, filt_f, skip):
    z = short_conv(u, conv_w, conv_b)
    v, x1, x2 = jnp.split(z, 3, axis=-1)
    y = x1 * fft_long_conv(v, filt_f[:, 0], skip[0])
    return x2 * fft_long_conv(y, filt_f[:, 1], skip[1])

def retention_heads(u):
    q, k, v = [heads(a, RET_HEADS, RET_HEAD_DIM).astype(F32) for a in jnp.split(u, 3, axis=-1)]
    return q, k * (RET_HEAD_DIM ** -0.5), v

def axial_rope(x):
    L, D = x.shape[1], x.shape[-1]
    half = D // 2
    quarter = half // 2
    t = jnp.arange(L)
    pos = jnp.stack([t // GRID_W, t % GRID_W], axis=0).astype(F32)
    freqs = ROPE_BASE ** (-jnp.arange(quarter, dtype=F32) / quarter)
    ang = pos[:, :, None] * freqs
    outs = []
    for a in range(2):
        xa = x[..., a * half:(a + 1) * half]
        x1, x2 = xa[..., :quarter], xa[..., quarter:]
        cos = jnp.cos(ang[a])[None, :, None, :]
        sin = jnp.sin(ang[a])[None, :, None, :]
        outs += [x1 * cos - x2 * sin, x1 * sin + x2 * cos]
    return jnp.concatenate(outs, axis=-1).astype(x.dtype)

def retention_chunks(q, k, v, log_gamma, state0):
    B, L, H, Dk = q.shape
    Dv = v.shape[-1]
    n = L // RET_CHUNK
    qc = q.reshape(B, n, RET_CHUNK, H, Dk)
    kc = k.reshape(B, n, RET_CHUNK, H, Dk)
    vc = v.reshape(B, n, RET_CHUNK, H, Dv)
    pos = jnp.arange(RET_CHUNK, dtype=F32)
    diff = pos[:, None] - pos[None, :]
    decay_in = jnp.where(diff >= 0, jnp.exp(log_gamma[:, None, None] * jnp.maximum(diff, 0.0)), 0.0)
    scores = jnp.einsum('bnjhd,bnlhd->bnhjl', qc, kc) * decay_in
    o = jnp.einsum('bnhjl,bnlhe->bnjhe', scores, vc)
    zeta = jnp.exp(log_gamma[:, None] * (RET_CHUNK - 1 - pos))
    chunk_kv = jnp.einsum('bnlhd,hl,bnlhe->nbhde', kc, zeta, vc)
    chunk_decay = jnp.exp(log_gamma * RET_CHUNK)[None, :, None, None]

    def step(state, kv):
        return chunk_decay * state + kv, state

    _, prev = lax.scan(step, state0, chunk_kv)
    xi = jnp.exp(log_gamma[:, None] * (pos + 1.0))
    o = o + jnp.einsum('bnjhd,nbhde,hj->bnjhe', qc, prev, xi)
    return o.reshape(B, L, H, Dv)

def bidir_retention(q, k, v, log_gamma, state_fwd, state_bwd):
    flip = lambda a: a[:, ::-1]
    o_fwd = retention_chunks(q, k, v, log_gamma[0], state_fwd)
    o_bwd = retention_chunks(flip(q), flip(k), flip(v), log_gamma[1], state_bwd)
    return o_fwd + flip(o_bwd)

def context_final_states(k, v, log_gamma):
    Lc = k.shape[1]
    pos = jnp.arange(Lc, dtype=F32)
    w_fwd = jnp.exp(log_gamma[0][:, None] * (Lc - 1 - pos))
    w_bwd = jnp.exp(log_gamma[1][:, None] * pos)
    s_fwd = jnp.einsum('bmhd,hm,bmhe->bhde', k, w_fwd, v)
    s_bwd = jnp.einsum('bmhd,hm,bmhe->bhde', k, w_bwd, v)
    return s_fwd, s_bwd

def merge_branches(a, g_a, y, g_y, r, g_r, w_out):
    B, L, _ = a.shape
    r = rms_norm(r).reshape(B, L, RET_W).astype(a.dtype)
    z = jnp.concatenate([a * jax.nn.silu(g_a), y * jax.nn.silu(g_y), r * jax.nn.silu(g_r)], axis=-1)
    return z @ w_out

def hybrid_layer(x, ctx, mod_x, mod_c, norm_w, w_in, w_out, q_gain, k_gain, rpb,
                 conv_w, conv_b, hw1, hb1, hw2, hb2, hw3, sin_freq, skip, ret_log_rate,
                 with_ctx_out):
    B, L, _ = x.shape
    Lc = ctx.shape[1]
    hx, gate_x = modulate(x, mod_x[:, None, :], norm_w)
    hc, gate_c = modulate(ctx, mod_c, norm_w)
    na_x, ga_x, hy_x, gh_x, re_x, gr_x = split_projection(hx @ w_in)
    na_c, ga_c, hy_c, gh_c, re_c, gr_c = split_projection(hc @ w_in)
    log_gamma = -jnp.exp(ret_log_rate.astype(F32))

    k_c, v_c = na_keys_values(na_c, k_gain)
    k_x, v_x = na_keys_values(na_x, k_gain)
    a_x = neighborhood_attention(na_queries(na_x, q_gain), k_x, v_x, k_c, v_c, rpb)
    y_x = hyena_mixer(hy_x, conv_w, conv_b,
                      hyena_filter_spectrum(L, hw1, hb1, hw2, hb2, hw3, sin_freq), skip)
    rq_c, rk_c, rv_c = retention_heads(re_c)
    s_fwd, s_bwd = context_final_states(rk_c, rv_c, log_gamma)
    rq_x, rk_x, rv_x = retention_heads(re_x)
    r_x = bidir_retention(axial_rope(rq_x), axial_rope(rk_x), rv_x, log_gamma, s_fwd, s_bwd)

    x_new = x + gate_x * merge_branches(a_x, ga_x, y_x, gh_x, r_x, gr_x, w_out)
    if not with_ctx_out:
        return x_new, None

    a_c = context_attention(na_queries(na_c, q_gain), k_c, v_c)
    y_c = hyena_mixer(hy_c, conv_w, conv_b,
                      hyena_filter_spectrum(Lc, hw1, hb1, hw2, hb2, hw3, sin_freq), skip)
    zero_state = jnp.zeros((B, RET_HEADS, RET_HEAD_DIM, RET_HEAD_DIM), F32)
    r_c = bidir_retention(rq_c, rk_c, rv_c, log_gamma, zero_state, zero_state)
    ctx_new = ctx + gate_c * merge_branches(a_c, ga_c, y_c, gh_c, r_c, gr_c, w_out)
    return x_new, ctx_new

def setup_inputs(seed: int = 0) -> dict:
    key = jax.random.key(seed)
    ks = jax.random.split(key, 24)
    nrm = lambda k, shape, s: jax.random.normal(k, shape, F32) * s
    base_rate = jnp.log(-jnp.log1p(-(2.0 ** (-5.0 - jnp.arange(RET_HEADS, dtype=F32)))))
    return {
        'x': nrm(ks[0], (BATCH, SEQ, D_MODEL), 1.0),
        'c': nrm(ks[1], (BATCH, D_MODEL), 1.0),
        'ctx': nrm(ks[2], (BATCH, CTX_LEN, D_MODEL), 1.0),
        'c_ctx': nrm(ks[3], (D_MODEL,), 1.0),
        'norm_w': 1.0 + nrm(ks[4], (DEPTH, D_MODEL), 0.02),
        'ada_w': nrm(ks[5], (DEPTH, D_MODEL, 3 * D_MODEL), 0.5 * D_MODEL ** -0.5),
        'ada_b': nrm(ks[6], (DEPTH, 3 * D_MODEL), 0.02),
        'w_in': nrm(ks[7], (DEPTH, D_MODEL, IN_W), D_MODEL ** -0.5),
        'w_out': nrm(ks[8], (DEPTH, MIX_W, D_MODEL), MIX_W ** -0.5),
        'na_q_gain': 1.0 + nrm(ks[9], (DEPTH, NA_HEAD_DIM), 0.02),
        'na_k_gain': 1.0 + nrm(ks[10], (DEPTH, NA_HEAD_DIM), 0.02),
        'na_rpb': nrm(ks[11], (DEPTH, NA_HEADS, 2 * NA_KH - 1, 2 * NA_KW - 1), 0.05),
        'hy_conv_w': nrm(ks[12], (DEPTH, HY_SHORT, 3 * HY_W), HY_SHORT ** -0.5),
        'hy_conv_b': nrm(ks[13], (DEPTH, 3 * HY_W), 0.02),
        'hy_w1': nrm(ks[14], (DEPTH, HY_EMB, HY_FFN), HY_EMB ** -0.5),
        'hy_b1': nrm(ks[15], (DEPTH, HY_FFN), 0.02),
        'hy_w2': nrm(ks[16], (DEPTH, HY_FFN, HY_FFN), HY_FFN ** -0.5),
        'hy_b2': nrm(ks[17], (DEPTH, HY_FFN), 0.02),
        'hy_w3': nrm(ks[18], (DEPTH, HY_FFN, HY_ORDER * 2 * HY_W), HY_FFN ** -0.5),
        'hy_sin_freq': 1.0 + nrm(ks[19], (DEPTH, 2, HY_FFN), 0.05),
        'hy_skip': nrm(ks[20], (DEPTH, HY_ORDER, HY_W), 1.0),
        'ret_log_rate': base_rate[None, None, :] + nrm(ks[21], (DEPTH, 2, RET_HEADS), 0.05),
    }

def reference(x, c, ctx, c_ctx, norm_w, ada_w, ada_b, w_in, w_out, na_q_gain, na_k_gain, na_rpb,
              hy_conv_w, hy_conv_b, hy_w1, hy_b1, hy_w2, hy_b2, hy_w3, hy_sin_freq, hy_skip,
              ret_log_rate):
    for i in range(DEPTH):
        mod_x = ada_modulation(c, ada_w[i], ada_b[i])
        mod_c = ada_modulation(c_ctx, ada_w[i], ada_b[i])
        x, ctx = hybrid_layer(x, ctx, mod_x, mod_c, norm_w[i], w_in[i], w_out[i],
                              na_q_gain[i], na_k_gain[i], na_rpb[i],
                              hy_conv_w[i], hy_conv_b[i], hy_w1[i], hy_b1[i], hy_w2[i], hy_b2[i],
                              hy_w3[i], hy_sin_freq[i], hy_skip[i], ret_log_rate[i],
                              i < DEPTH - 1)
    return x


_drawn_inputs = setup_inputs


def setup_inputs(seed=0):
    import zlib

    import numpy as np

    out = dict(_drawn_inputs(seed))
    spreads = {}
    factors = {'norm_w': 7.619,
     'ada_b': 2.952,
     'na_q_gain': 39.924,
     'na_k_gain': 31.219,
     'na_rpb': 64.0,
     'hy_conv_b': 8.0,
     'hy_w1': 2.92,
     'hy_b1': 8.0,
     'hy_w2': 2.872,
     'hy_b2': 8.0,
     'hy_w3': 2.976,
     'hy_sin_freq': 8.0,
     'ret_log_rate': 8.0}
    for name, (base, spread) in spreads.items():
        noise = np.random.default_rng([zlib.crc32(name.encode()), seed]).standard_normal(out[name].shape)
        drawn = base * np.exp(spread * noise) if base else spread * noise
        out[name] = jnp.asarray(drawn.astype(out[name].dtype))
    for name, factor in factors.items():
        out[name] = (out[name] * factor).astype(out[name].dtype)
    return out
```

```python
from contextlib import ExitStack
import math

import numpy as np

import concourse.bass as bass
from concourse import mybir

F32 = mybir.dt.float32
ALU = mybir.AluOpType
ACT = mybir.ActivationFunctionType
AX = mybir.AxisListType

P = 128
D = 1024
KC = D // P
L = 1024
LC = 256
DEPTH = 2
TC = LC // P
TILES = TC + L // P
TOK = LC + L
GRID = 64
NA_HEADS, HD = 8, 64
NA_W = NA_HEADS * HD
KH, KW = 8, 16
HW = 256
FFN = 64
EMB = 17
RH = 4
RW = RH * HD
IN_W = 4 * (NA_W + HW + RW)
EPS = 1e-6
NEG = -1e30
NF = 2 * L
T2 = 16
T1 = L // T2
NR = L // P
GROUPS = 16
HT = 8
WCH = 512
HY0 = 4 * NA_W
RE0 = HY0 + 4 * HW
MAGIC = 1.5 * 2.0 ** 23
TWO_PI_HI = 6.28125
TWO_PI_LO = 2.0 * math.pi - TWO_PI_HI
PI_F = 3.1415925


def constants():
    c = {}
    c["ident"] = np.eye(P)
    t1 = np.arange(T1)[:, None]
    slot = np.arange(64)
    time = np.zeros((T1, 64, 2))
    ang = 2 * np.pi * t1 * slot / 128
    time[:, :, 0] = np.cos(ang)
    time[:, :, 1] = -np.sin(ang)
    time[:, 0, 0] = 1.0
    time[:, 0, 1] = (-1.0) ** t1[:, 0]
    time = time.reshape(T1, P)
    both = np.zeros((P, 2, P))
    for b in range(2):
        both[b::2, b] = time
    c["dft_time"] = both
    c["idft_time"] = both.transpose(2, 1, 0)
    fine = np.zeros((P, 2, GROUPS, 64))
    inv = np.zeros((P, HT, 2, P))
    t2 = np.arange(T2)
    for g in range(GROUPS):
        for s in range(4):
            sl = 4 * g + s
            for f2 in range(16):
                col = s * 16 + f2
                irow = 64 * (g % 2) + col
                w = 2.0 / NF
                if sl > 0:
                    th = 2 * np.pi * t2 * (sl + 128 * f2) / NF
                    r0, r1 = s * 32 + t2, s * 32 + 16 + t2
                    fine[r0, 0, g, col], fine[r1, 0, g, col] = np.cos(th), np.sin(th)
                    fine[r0, 1, g, col], fine[r1, 1, g, col] = -np.sin(th), np.cos(th)
                    inv[irow, g // 2, 0, r0], inv[irow, g // 2, 0, r1] = w * np.cos(th), w * np.sin(th)
                    inv[irow, g // 2, 1, r0], inv[irow, g // 2, 1, r1] = -w * np.sin(th), w * np.cos(th)
                else:
                    f = 128 * f2 if f2 < 8 else 64 + 128 * (f2 - 8)
                    r = t2 if f2 < 8 else 16 + t2
                    th = 2 * np.pi * t2 * f / NF
                    if f2 == 0:
                        fine[r, 0, g, col], fine[r, 1, g, col] = 1.0, np.cos(np.pi * t2)
                        inv[irow, 0, 0, r], inv[irow, 0, 1, r] = 1.0 / NF, np.cos(np.pi * t2) / NF
                    else:
                        fine[r, 0, g, col], fine[r, 1, g, col] = np.cos(th), -np.sin(th)
                        inv[irow, 0, 0, r], inv[irow, 0, 1, r] = w * np.cos(th), -w * np.sin(th)
    c["dft_fine"] = fine
    c["idft_fine"] = inv
    special = np.zeros((P, 2, 64))
    special[:, 0] = fine[:, 0, 0]
    special[:, 0, 0] = fine[:, 1, 0, 0]
    special[:, 1] = fine[:, 1, 0]
    special[:, 1, 0] = 0.0
    c["fine_special"] = special
    t = np.arange(LC)
    f = np.arange(LC)
    th = 2 * np.pi * np.outer(t, f) / (2 * LC)
    re, im = np.cos(th), -np.sin(th)
    im[:, 0] = np.cos(np.pi * t)
    h, g = re.copy(), im.copy()
    h[:, 0] = im[:, 0]
    g[:, 0] = 0.0
    rows = lambda m: m.reshape(2, P, -1).transpose(1, 0, 2)
    c["cdft"] = np.stack([rows(re), rows(im)], 1)
    c["cdft_special"] = np.stack([rows(h)[:, :, :P], rows(g)[:, :, :P]], 1)
    w = np.full(LC, 2.0 / (2 * LC))
    w[0] = 1.0 / (2 * LC)
    c["cidft"] = np.stack([rows(re.T * w[:, None]), rows(im.T * w[:, None])], 1)
    px = (NR * np.arange(P)[None] + np.arange(NR)[:, None]).ravel()
    emb, dec = [], []
    for n, pos in ((L, px), (LC, np.arange(LC))):
        tn = np.linspace(0.0, 1.0, n).astype(np.float32).astype(np.float64)[pos][:, None]
        om = 2 * np.pi * pos[:, None] / n
        bands = np.linspace(1e-4, 7.0, 8).astype(np.float32).astype(np.float64)[None]
        emb.append(np.concatenate([tn, np.cos(bands * om), -np.sin(bands * om)], 1))
        deltas = np.abs(np.linspace(math.log(1e-2) / 1.5, math.log(1e-2) / 0.3, HW))
        dec.append(np.exp(-tn * deltas))
    c["emb"] = np.concatenate(emb, 0).T
    c["decay"] = np.concatenate(dec, 0).reshape(TILES, P, HW).transpose(1, 0, 2)
    tok = np.arange(L)
    fr = 10000.0 ** (-np.arange(16) / 16.0)
    ang = np.stack([tok // GRID, tok % GRID], 1)[:, :, None] * fr
    rope = np.zeros((TOK, 2, 2, 16))
    rope[:LC, 0] = 1.0
    rope[LC:, 0] = np.cos(ang)
    rope[LC:, 1] = np.sin(ang)
    c["rope"] = rope.reshape(TILES, P, 64).transpose(1, 0, 2)
    l, j = np.arange(P)[:, None], np.arange(P)[None]
    c["dist"] = np.stack([np.maximum(j - l, 0), np.maximum(l - j, 0), (j >= l) * 0.125, (l >= j) * 0.125], 1)
    c["age"] = np.broadcast_to(np.stack([np.arange(P) + 1, P - np.arange(P)])[None], (P, 2, P))
    c["rest"] = np.stack([P - 1 - np.arange(P), np.arange(P)], 1)[:, :, None].repeat(RH, 2)
    cq, ck = np.arange(GRID)[:, None], np.arange(GRID)[None]
    cs = np.clip(cq - KW // 2, 0, GRID - KW)
    ok = (ck >= cs) & (ck < cs + KW)
    c["colmask"] = np.concatenate([np.where(ok, 0.0, NEG)] * 2, 0)
    return {k: np.ascontiguousarray(v, np.float32) for k, v in c.items()}


class Ring:

    def __init__(self, name, banks, sem):
        self.banks, self.full, self.free = banks, sem(name + "_full"), sem(name + "_free")
        self.put, self.got = 0, 0

    def fill(self, pe):
        if self.put >= len(self.banks):
            pe.wait_ge(self.free, self.put - len(self.banks) + 1)
        self.put += 1
        return self.banks[(self.put - 1) % len(self.banks)]

    def read(self, eng):
        eng.wait_ge(self.full, self.got + 1)
        self.got += 1
        return self.banks[(self.got - 1) % len(self.banks)]


class Chain:

    def __init__(self, sem, eng=None):
        self.sem, self.n, self.eng = sem, 0, eng

    def __call__(self, ins):
        self.n += 1
        ins.then_inc(self.sem, 1)
        self.eng.wait_ge(self.sem, self.n)


class Build:

    def __init__(self, nc, a, out, ctx):
        self.nc, self.a, self.out, self.ctx = nc, a, out, ctx
        self.sems = []
        self.all_psum = ctx.enter_context(nc.psum_tensor("psum", [P, 8 * 512], F32))
        self.psum = [self.all_psum[:, i * 512:(i + 1) * 512] for i in range(8)]

    def sem(self, name):
        s = self.ctx.enter_context(self.nc.semaphore(name))
        self.sems.append(s)
        return s

    def of_layer(self, ap):
        return ap[bass.ds(self.layer, 1)]


def sbuf(ctx, nc, name, shape):
    return ctx.enter_context(nc.sbuf_tensor(name, shape, F32))


def weight_chunk(k, n):
    def cols(w, c0, width=WCH, at=0):
        v = k.of_layer(w)[:, :, c0:c0 + width].rearrange("a (k p) n -> p (a k) n", p=P)
        return (slice(at, at + width), v)

    a = k.a
    if n < 6:
        return [cols(a["ada_w"], n * WCH)]
    n -= 6
    if n < 2:
        return [cols(a["w_in"], HY0 + n * WCH)]
    n -= 2
    if n < 4:
        half, first = n // 2, (0, 2 * NA_W)[n % 2]
        return [cols(a["w_in"], first + half * 256, 256), cols(a["w_in"], first + NA_W + half * 256, 256, 256)]
    n -= 4
    if n < 2:
        return [cols(a["w_in"], RE0 + n * WCH)]
    return [cols(a["w_out"], (n - 2) * WCH)]


def load_weights(k, eng, n):
    for where, view in weight_chunk(k, n):
        eng.dma_start(k.wbuf[n % 2][:, :, where], view).then_inc(k.w_here[n % 2], 16)


def wait_weights(k, eng, n):
    parts = sum(2 if 8 <= m < 12 else 1 for m in range(n % 2, n + 1, 2))
    eng.wait_ge(k.w_here[n % 2], 16 * parts)
    return k.wbuf[n % 2]


def weights_stage(k):
    nc, a = k.nc, k.a
    with ExitStack() as mem:
        sb = lambda name, shape: sbuf(mem, nc, name, shape)
        time = sb("s1_time", [P, 2, P])
        fine = sb("s1_fine", [P, 2, GROUPS, 64])
        special = sb("s1_special", [P, 2, 64])
        cdft = sb("s1_cdft", [P, 2, 2, LC])
        cspecial = sb("s1_cspecial", [P, 2, 2, P])
        emb = sb("s1_emb", [EMB, TOK])
        decay = sb("s1_decay", [P, TILES, HW])
        w1, w2 = sb("s1_w1", [EMB, FFN]), sb("s1_w2", [FFN, FFN])
        w3 = sb("s1_w3", [FFN, 4 * HW])
        vec = sb("s1_vec", [FFN, 4])
        arg, turns, hid = sb("s1_arg", [FFN, TOK]), sb("s1_turns", [FFN, TOK]), sb("s1_hid", [FFN, TOK])
        taps = sb("s1_taps", [P, TILES, 2, HW])
        even, odd = sb("s1_even", [P, TILES, HW]), sb("s1_odd", [P, TILES, HW])
        mag = taps[:, :, 0, :]
        ones = sb("s1_ones", [P, P])
        part1, part2 = sb("s1_part1", [P, T2, HW]), sb("s1_part2", [P, GROUPS, HW])
        spec = sb("s1_spec", [P, 22, HW])
        cond = sb("s1_cond", [P, KC, 2])
        condb = sb("s1_condb", [P, 2, KC, P])
        gate_b = sb("s1_gate_b", [P, D])
        ada_b = sb("s1_ada_b", [P, 2 * KC])
        normw = sb("s1_normw", [P, KC])

        s_tab, s_mod, s_w = k.sem("s1_tables_here"), k.sem("s1_mod_inputs_here"), k.sem("s1_mlp_weights_here")
        ra, rv = Ring("s1_act", k.psum[0:4], k.sem), Ring("s1_dve", k.psum[4:8], k.sem)
        s_arg, s_sin = k.sem("s1_arg"), k.sem("s1_sin")
        s_step, s_taps = k.sem("s1_dve_step"), k.sem("s1_taps_ready")
        s_shuf, s_spill = k.sem("s1_shuffled"), k.sem("s1_spilled")
        s_silu, s_condb = k.sem("s1_silu"), k.sem("s1_cond_spread")
        base = [0, 19, 36, 55, 72]
        used = [4, 8, 21, 22, 36, 38]

        with nc.Block() as block:
            @block.tensor
            def _(pe):
                def mlp(w, x):
                    for c0 in range(0, TOK, 512):
                        n = min(512, TOK - c0)
                        bank = rv.fill(pe)
                        pe.matmul(bank[0:FFN, 0:n], w[:, :], x[:, c0:c0 + n], start=True, stop=True).then_inc(rv.full, 1)

                def modulation(n):
                    w = wait_weights(k, pe, n)
                    if n < 4:
                        bank = rv.fill(pe)
                        for m in range(4):
                            for kc in range(KC):
                                mm = pe.matmul(bank[:, 2 * m:2 * m + 2], w[:, kc, m * P:(m + 1) * P], cond[:, kc, :],
                                               start=(kc == 0), stop=(kc == KC - 1))
                        mm.then_inc(rv.full, 1)
                    else:
                        pe.wait_ge(s_condb, 2)
                        for c in range(2):
                            bank = rv.fill(pe)
                            for kc in range(KC):
                                mm = pe.matmul(bank[:, :], condb[:, c, kc, :], w[:, kc, :], start=(kc == 0), stop=(kc == KC - 1))
                            mm.then_inc(rv.full, 1)
                    assert rv.put == used[n]

                pe.wait_ge(s_w, 7 * 16)
                mlp(w1, emb)
                pe.wait_ge(s_silu, 1)
                modulation(0)
                pe.wait_ge(s_sin, 1)
                mlp(w2, hid)
                modulation(1)
                pe.wait_ge(s_sin, 2)
                pe.wait_ge(s_tab, 6 * 16)
                for o in range(2):
                    for i in range(TILES):
                        bank = rv.fill(pe)
                        pe.matmul(bank[:, :], hid[:, i * P:(i + 1) * P], w3[:, o * 512:(o + 1) * 512],
                                  start=True, stop=True).then_inc(rv.full, 1)
                    for part, x in enumerate((even, odd)):
                        n = 2 * o + part
                        pe.wait_ge(s_taps, o + 1)
                        if part == 0:
                            for tiles in (range(0, 8), range(8, 10)):
                                bank = rv.fill(pe)
                                for i in tiles:
                                    mm = pe.matmul(bank[:, 0:HW], ones[:, :], mag[:, i, :], start=(i == tiles[0]), stop=(i == tiles[-1]))
                                mm.then_inc(rv.full, 1)
                        assert ra.put == base[n]
                        for b in range(2):
                            for q in range(4):
                                bank = ra.fill(pe)
                                pe.matmul(bank[:, :], time[:, b, :], x[:, 2 * q:2 * q + 2, :],
                                          start=True, stop=True).then_inc(ra.full, 1)
                        bank = ra.fill(pe)
                        for T in range(2):
                            for kk in range(2):
                                table = cspecial[:, 1, kk, :] if part and T == 0 else cdft[:, part, kk, T * P:(T + 1) * P]
                                mm = pe.matmul(bank[:, T * HW:(T + 1) * HW], table, x[:, 8 + kk, :], start=(kk == 0), stop=(kk == 1))
                        mm.then_inc(ra.full, 1)
                        if part == 0:
                            bank = ra.fill(pe)
                            for kk in range(2):
                                mm = pe.matmul(bank[:, 0:HW], cspecial[:, 0, kk, :], x[:, 8 + kk, :], start=(kk == 0), stop=(kk == 1))
                            mm.then_inc(ra.full, 1)
                        modulation(n + 2)
                        pe.wait_ge(s_shuf, 16 * GROUPS * (n + 1))
                        for T in range(HT):
                            bank = ra.fill(pe)
                            for h in range(2):
                                g = 2 * T + h
                                lhs = special[:, 1, :] if part and g == 0 else fine[:, part, g, :]
                                mm = pe.matmul(bank[64 * h:64 * h + 64, 0:HW], lhs, part2[:, g, :], start=True, stop=True)
                            mm.then_inc(ra.full, 1)
                        if part == 0:
                            bank = ra.fill(pe)
                            pe.matmul(bank[0:64, 0:HW], special[:, 0, :], part2[:, 0, :], start=True, stop=True)
                            pe.matmul(bank[64:128, 0:HW], fine[:, 0, 1, :], part2[:, 1, :], start=True, stop=True).then_inc(ra.full, 1)

            @block.sync
            def _(sp):
                this = k.of_layer
                load_weights(k, sp, 0)
                sp.dma_start(w1[:, :], this(a["hy_w1"]).rearrange("a k n -> (a k) n")).then_inc(s_w, 16)
                sp.dma_start(emb[:, :], a["emb"]).then_inc(s_w, 16)
                sp.dma_start(w2[:, :], this(a["hy_w2"]).rearrange("a k n -> (a k) n")).then_inc(s_w, 16)
                sp.dma_start(vec[:, 0:1], this(a["hy_b1"]).rearrange("a n -> n a")).then_inc(s_w, 16)
                sp.dma_start(vec[:, 1:2], this(a["hy_b2"]).rearrange("a n -> n a")).then_inc(s_w, 16)
                sp.dma_start(vec[:, 2:4], this(a["hy_sin_freq"]).rearrange("a f n -> n (a f)")).then_inc(s_w, 16)
                sp.dma_start(w3[:, :], this(a["hy_w3"]).rearrange("a k n -> (a k) n")).then_inc(s_w, 16)
                sp.dma_start(cond[:, :, 0], a["c_ctx"].rearrange("(k p) -> p k", p=P)).then_inc(s_mod, 16)
                sp.dma_start(cond[:, :, 1], a["c"].rearrange("a (k p) -> p (a k)", p=P)).then_inc(s_mod, 16)
                sp.dma_start(ada_b[:, :], this(a["ada_b"])[:, 0:2 * D].rearrange("a (k p) -> p (a k)", p=P)).then_inc(s_mod, 16)
                sp.dma_start(normw[:, :], this(a["norm_w"]).rearrange("a (k p) -> p (a k)", p=P)).then_inc(s_mod, 16)
                sp.dma_start(gate_b[:, :], this(a["ada_b"])[:, 2 * D:3 * D].to_broadcast((P, D))).then_inc(s_mod, 16)
                sp.dma_start(decay[:, :, :], a["decay"]).then_inc(s_tab, 16)
                sp.dma_start(time[:, :, :], a["dft_time"]).then_inc(s_tab, 16)
                sp.dma_start(fine[:, :, :, :], a["dft_fine"]).then_inc(s_tab, 16)
                sp.dma_start(special[:, :, :], a["fine_special"]).then_inc(s_tab, 16)
                sp.dma_start(cdft[:, :, :, :], a["cdft"]).then_inc(s_tab, 16)
                sp.dma_start(cspecial[:, :, :, :], a["cdft_special"]).then_inc(s_tab, 16)
                load_weights(k, sp, 1)
                for m in (2, 3):
                    sp.wait_ge(rv.full, used[m - 2])
                    load_weights(k, sp, m)
                for n in range(4):
                    sp.wait_ge(ra.free, base[n] + 8)
                    if n >= 1:
                        sp.wait_ge(ra.full, base[n])
                    for g in range(GROUPS):
                        sp.dma_start(part2[:, g, :], part1[8 * g:8 * g + 8, :, :]).then_inc(s_shuf, 16)
                    sp.wait_ge(rv.full, used[n + 2])
                    load_weights(k, sp, n + 4)
                    if n % 2 == 1:
                        sp.wait_ge(ra.free, base[n + 1])
                        sp.dma_start(k.spectra[n // 2], spec[:, :, :]).then_inc(s_spill, 16)
                sp.wait_ge(s_spill, 32)

            @block.scalar
            def _(act):
                act.wait_ge(s_mod, 5 * 16)
                act.activation(cond[:, :, :], cond[:, :, :], ACT.Silu).then_inc(s_silu, 1)
                for n in range(2):
                    act.wait_ge(s_arg, n + 1)
                    if n == 1:
                        act.wait_ge(rv.full, 7)
                    act.activation(hid[:, :], arg[:, :], ACT.Sin).then_inc(s_sin, 1)
                for n in range(4):
                    part = n % 2
                    if n >= 1:
                        act.wait_ge(s_shuf, 16 * GROUPS * n)
                    for b in range(2):
                        for q in range(4):
                            bank = ra.read(act)
                            dst = part1[:, 8 * b + 2 * q:8 * b + 2 * q + 2, :]
                            act.activation(dst, bank[:, :].rearrange("p (a c) -> p a c", a=2), ACT.Copy).then_inc(ra.free, 1)
                    if n == 2:
                        act.wait_ge(s_spill, 16)
                    first = (17, 19)[part]
                    act.activation(spec[:, first:first + 2, :], ra.read(act)[:, :].rearrange("p (a c) -> p a c", a=2), ACT.Copy).then_inc(ra.free, 1)
                    if part == 0:
                        act.activation(spec[:, 21, :], ra.read(act)[:, 0:HW], ACT.Copy).then_inc(ra.free, 1)
                    for T in range(HT):
                        act.activation(spec[:, 8 * part + T, :], ra.read(act)[:, 0:HW], ACT.Copy).then_inc(ra.free, 1)
                    if part == 0:
                        act.activation(spec[:, 16, :], ra.read(act)[:, 0:HW], ACT.Copy).then_inc(ra.free, 1)

            @block.vector
            def _(dve):
                step = Chain(s_step, dve)

                def sin_argument(n):
                    for c0 in range(0, TOK, 512):
                        w = min(512, TOK - c0)
                        bank = rv.read(dve)
                        dve.tensor_scalar(arg[:, c0:c0 + w], bank[0:FFN, 0:w], vec[:, n:n + 1], vec[:, 2 + n:3 + n],
                                          ALU.add, ALU.mult).then_inc(rv.free, 1)
                    dve.wait_ge(rv.free, rv.got)
                    step(dve.tensor_scalar(turns[:, :], arg[:, :], 1.0 / (2 * math.pi), MAGIC, ALU.mult, ALU.add))
                    step(dve.tensor_scalar(turns[:, :], turns[:, :], MAGIC, None, ALU.subtract))
                    step(dve.scalar_tensor_tensor(out=arg[:, :], in0=turns[:, :], scalar=-TWO_PI_HI, in1=arg[:, :], op0=ALU.mult, op1=ALU.add))
                    step(dve.scalar_tensor_tensor(out=arg[:, :], in0=turns[:, :], scalar=-TWO_PI_LO, in1=arg[:, :], op0=ALU.mult, op1=ALU.add))
                    dve.tensor_scalar(arg[:, :], arg[:, :], PI_F, -PI_F, ALU.min, ALU.max).then_inc(s_arg, 1)

                def modulation(n):
                    if n < 4:
                        dst = (k.shift if n < 2 else k.scale)[:, 4 * (n % 2):4 * (n % 2) + 4, :]
                        both = lambda x, c0: x[:, c0:c0 + 4].unsqueeze(2).to_broadcast((P, 4, 2))
                        bank = rv.read(dve)
                        dve.tensor_tensor(dst, bank[:, 0:8].rearrange("p (m c) -> p m c", c=2), both(ada_b, 4 * n), ALU.add).then_inc(rv.free, 1)
                        if n >= 2:
                            dve.wait_ge(rv.free, rv.got)
                            step(dve.scalar_tensor_tensor(out=dst, in0=dst, scalar=1.0, in1=both(normw, 4 * (n - 2)), op0=ALU.add, op1=ALU.mult))
                    else:
                        c0 = (n - 4) * 512
                        for c in range(2):
                            bank = rv.read(dve)
                            dve.tensor_tensor(k.gate[:, c, c0:c0 + 512], bank[:, :], gate_b[:, c0:c0 + 512], ALU.add).then_inc(rv.free, 1)

                dve.memset(ones[:, :], 1.0).then_inc(s_step, 1)
                step.n += 1
                dve.wait_ge(s_w, 7 * 16)
                dve.wait_ge(s_mod, 5 * 16)
                sin_argument(0)
                dve.wait_ge(s_silu, 1)
                for c in range(2):
                    dve.tensor_copy(condb[:, c, :, :], cond[:, :, c].unsqueeze(2).to_broadcast((P, KC, P))).then_inc(s_condb, 1)
                modulation(0)
                dve.wait_ge(s_sin, 1)
                sin_argument(1)
                modulation(1)
                dve.wait_ge(s_tab, 6 * 16)
                for o in range(2):
                    for i in range(TILES):
                        bank = rv.read(dve)
                        dve.tensor_tensor(taps[:, i, :, :], bank[:, :].rearrange("p (w c) -> p w c", w=2),
                                          decay[:, i, :].unsqueeze(1).to_broadcast((P, 2, HW)), ALU.mult).then_inc(rv.free, 1)
                    dve.wait_ge(rv.free, rv.got)
                    step(dve.memset(taps[0:1, 0, 1, :], 0.0))
                    step(dve.memset(taps[0:1, 8, 1, :], 0.0))
                    if o == 1:
                        dve.wait_ge(ra.full, base[2])
                    fwd, bwd = taps[:, :, 0, :], taps[:, :, 1, :]
                    step(dve.tensor_tensor(even[:, :, :], fwd, bwd, ALU.add))
                    step(dve.tensor_tensor(odd[:, :, :], fwd, bwd, ALU.subtract))
                    for x in (fwd, bwd):
                        step(dve.scalar_tensor_tensor(out=x, in0=x, scalar=-1.0, in1=x, op0=ALU.mult, op1=ALU.max))
                    dve.tensor_tensor(mag, fwd, bwd, ALU.add).then_inc(s_taps, 1)
                    for which in range(2):
                        bank = rv.read(dve)
                        dve.reciprocal(k.inv_sum[:, o, which, :], bank[:, 0:HW]).then_inc(rv.free, 1)
                    modulation(2 + 2 * o)
                    modulation(3 + 2 * o)


def stream_tile(k, i):
    return k.context[i * P:(i + 1) * P, :] if i < TC else k.out[0, (i - TC) * P:(i - TC + 1) * P, :]


def norm_stage(k):
    nc = k.nc
    BUFS = 3
    with ExitStack() as mem:
        x = sbuf(mem, nc, "s2_x", [P, BUFS, D])
        square = sbuf(mem, nc, "s2_square", [P, D])
        rms = sbuf(mem, nc, "s2_rms", [P, 2, TILES])
        inv = sbuf(mem, nc, "s2_inv", [P, TILES])
        eps = sbuf(mem, nc, "s2_eps", [P, 1])
        tmp = sbuf(mem, nc, "s2_scaled", [P, 2, 512])
        s_x = [k.sem(f"s2_x{b}_here") for b in range(BUFS)]
        s_sum, s_rms, s_inv, s_scaled = k.sem("s2_squares"), k.sem("s2_rms"), k.sem("s2_inverse"), k.sem("s2_x_scaled")
        s_eps, s_step = k.sem("s2_eps"), k.sem("s2_dve_step")
        ra, rv = Ring("s2_act", k.psum[0:4], k.sem), Ring("s2_dve", k.psum[4:8], k.sem)
        with nc.Block() as block:
            @block.sync
            def _(sp):
                for i in range(TILES):
                    if i >= BUFS:
                        sp.wait_ge(ra.full, i - BUFS + 1)
                    sp.dma_start(x[:, i % BUFS, :], stream_tile(k, i)).then_inc(s_x[i % BUFS], 16)

            @block.scalar
            def _(act):
                def transposed(i):
                    bank = ra.read(act)
                    c = int(i >= TC)
                    for m in range(4):
                        ins = act.activation(k.hxT[:, 4 + m, i * P:(i + 1) * P], bank[:, m * P:(m + 1) * P], ACT.Identity,
                                             bias=k.shift[:, 4 + m, c:c + 1], scale=k.scale[:, 4 + m, c:c + 1])
                    ins.then_inc(ra.free, 1)

                act.wait_ge(s_eps, 1)
                for i in range(TILES):
                    act.wait_ge(s_x[i % BUFS], 16 * (i // BUFS + 1))
                    if i >= 1:
                        act.wait_ge(s_sum, i)
                    act.activation(square[:, :], x[:, i % BUFS, :], ACT.Square, accum_out=rms[:, 0, i:i + 1]).then_inc(s_sum, 1)
                    act.wait_ge(s_sum, i + 1)
                    act.activation(rms[:, 1, i:i + 1], rms[:, 0, i:i + 1], ACT.Sqrt, bias=eps[:, 0:1], scale=1.0 / D).then_inc(s_rms, 1)
                    if i >= 1:
                        transposed(i - 1)
                transposed(TILES - 1)

            @block.vector
            def _(dve):
                dve.memset(eps[:, :], EPS).then_inc(s_eps, 1)
                step = Chain(s_step, dve)

                def transposed(i):
                    bank = rv.read(dve)
                    c = int(i >= TC)
                    per = lambda v: v[:, 0:4, c].unsqueeze(2).to_broadcast((P, 4, P))
                    four = lambda v: v.rearrange("p (m t) -> p m t", m=4)
                    dve.tensor_tensor(four(tmp[:, i % 2, :]), four(bank[:, :]), per(k.scale), ALU.mult).then_inc(rv.free, 1)
                    dve.wait_ge(rv.free, rv.got)
                    dve.tensor_tensor(k.hxT[:, 0:4, i * P:(i + 1) * P], four(tmp[:, i % 2, :]), per(k.shift), ALU.add).then_inc(s_step, 1)

                for i in range(TILES):
                    dve.wait_ge(s_rms, i + 1)
                    dve.reciprocal(inv[:, i:i + 1], rms[:, 1, i:i + 1]).then_inc(s_inv, 1)
                    dve.wait_ge(s_inv, i + 1)
                    dve.tensor_scalar(x[:, i % BUFS, :], x[:, i % BUFS, :], inv[:, i:i + 1], None, ALU.mult).then_inc(s_scaled, 1)
                    if i >= 1:
                        transposed(i - 1)
                transposed(TILES - 1)

            @block.tensor
            def _(pe):
                for i in range(TILES):
                    pe.wait_ge(s_scaled, i + 1)
                    for half, ring in enumerate((rv, ra)):
                        bank = ring.fill(pe)
                        for m in range(4):
                            c0 = (4 * half + m) * P
                            ins = pe.transpose(bank[:, m * P:(m + 1) * P], x[:, i % BUFS, c0:c0 + P], k.ident[:, :])
                        ins.then_inc(ring.full, 1)


def hyena_stage(k):
    nc, a_in = k.nc, k.a
    with ExitStack() as mem:
        sb = lambda name, shape: sbuf(mem, nc, name, shape)
        time, itime = sb("s3_time", [P, 2, P]), sb("s3_itime", [P, 2, P])
        fine, ifine = sb("s3_fine", [P, 2, GROUPS, 64]), sb("s3_ifine", [P, HT, 2, P])
        aux = sb("s3_aux", [P, 17, HW])
        tmp = sb("s3_tmp", [P, 4, HW])
        v = sb("s3_v", [P, NR, 3 * HW])
        gh = sb("s3_gate", [P, NR, HW])
        parts = sb("s3_parts", [P, 2, T2, HW])
        part1, part2 = parts[:, 0], parts[:, 1]
        raw = parts[:, :, :, :].rearrange("p n t c -> p (n t c)")[:, 0:(NR + 2) * 3 * HW].rearrange("p (r c) -> p r c", r=NR + 2)
        convw = aux[:, 0:9, :].rearrange("p (j g) c -> p j (g c)", j=3)
        convb = tmp[:, 0:3, :].rearrange("p g c -> p (g c)")

        ra, rv = Ring("s3_act", k.psum[0:4], k.sem), Ring("s3_dve", k.psum[4:8], k.sem)
        s_tab, s_conv, s_zero, s_shift = k.sem("s3_tables_here"), k.sem("s3_conv_weights_here"), k.sem("s3_zeroed"), k.sem("s3_shifted")
        s_scaled, s_step, s_ready = k.sem("s3_neighbours_scaled"), k.sem("s3_dve_step"), k.sem("s3_conv_done")
        s_shuf, s_spec, s_prod = k.sem("s3_shuffled"), k.sem("s3_spectrum_here"), k.sem("s3_products")
        s_skip, s_y = k.sem("s3_skip_applied"), k.sem("s3_y_ready")
        A = [20, 36]
        with nc.Block() as block:
            @block.tensor
            def _(pe):
                for n in (6, 7):
                    w = wait_weights(k, pe, n)
                    for i in range(NR + TC):
                        bank = ra.fill(pe)
                        for kc in range(KC):
                            lhs = k.hxT[:, kc, LC + i:TOK:NR] if i < NR else k.hxT[:, kc, (i - NR) * P:(i - NR + 1) * P]
                            mm = pe.matmul(bank[:, :], lhs, w[:, kc, :], start=(kc == 0), stop=(kc == KC - 1))
                        mm.then_inc(ra.full, 1)
                pe.wait_ge(s_tab, 4 * 16)
                for o in range(2):
                    pe.wait_ge(s_ready if o == 0 else s_y, 1)
                    for b in range(2):
                        for q in range(4):
                            bank = ra.fill(pe)
                            pe.matmul(bank[:, :], time[:, b, :], v[:, 2 * q:2 * q + 2, 0:HW],
                                      start=True, stop=True).then_inc(ra.full, 1)
                    pe.wait_ge(s_shuf, 16 * GROUPS * (2 * o + 1))
                    for T in range(HT):
                        bank = rv.fill(pe)
                        for h in range(2):
                            for ri in range(2):
                                mm = pe.matmul(bank[64 * h:64 * h + 64, ri * HW:(ri + 1) * HW], fine[:, ri, 2 * T + h, :],
                                               part2[:, 2 * T + h, :], start=True, stop=True)
                        mm.then_inc(rv.full, 1)
                    for T in range(0, HT, 2):
                        pe.wait_ge(s_prod, HT * o + T + 2)
                        banks = [ra.fill(pe), ra.fill(pe)]
                        for t in range(2):
                            for ri in range(2):
                                for h in range(2):
                                    y = part1[64 * h:64 * h + 64, 2 * (T + t) + ri, :]
                                    mm = pe.matmul(banks[h][:, t * HW:(t + 1) * HW], ifine[64 * h:64 * h + 64, T + t, ri, :], y,
                                                   start=(ri == 0), stop=(ri == 1))
                                    if t == 1 and ri == 1:
                                        mm.then_inc(ra.full, 1)
                    pe.wait_ge(s_shuf, 16 * GROUPS * (2 * o + 2))
                    for q in range(4):
                        bank = rv.fill(pe)
                        for b in range(2):
                            y = part1[:, 8 * b + 2 * q:8 * b + 2 * q + 2, :]
                            mm = pe.matmul(bank[:, :], itime[:, b, :], y, start=(b == 0), stop=(b == 1))
                        mm.then_inc(rv.full, 1)
                pe.wait_ge(s_y, 2)
                for half in range(2):
                    for q in range(2):
                        bank = ra.fill(pe)
                        for m in range(4):
                            mm = pe.transpose(bank[:, m * P:(m + 1) * P], v[:, 4 * q + m, half * P:(half + 1) * P], k.ident[:, :])
                        mm.then_inc(ra.full, 1)

            @block.sync
            def _(sp):
                this = k.of_layer
                sp.dma_start(convw, this(a_in["hy_conv_w"]).rearrange("a j c -> a (j c)").to_broadcast((P, 9 * HW))).then_inc(s_conv, 16)
                sp.dma_start(convb, this(a_in["hy_conv_b"]).to_broadcast((P, 3 * HW))).then_inc(s_conv, 16)
                sp.dma_start(k.skip[:, :, :], this(a_in["hy_skip"]).rearrange("a o c -> a (o c)").to_broadcast((P, 2 * HW))).then_inc(s_conv, 16)
                sp.dma_start(time[:, :, :], a_in["dft_time"]).then_inc(s_tab, 16)
                sp.dma_start(itime[:, :, :], a_in["idft_time"]).then_inc(s_tab, 16)
                sp.dma_start(fine[:, :, :, :], a_in["dft_fine"]).then_inc(s_tab, 16)
                sp.dma_start(ifine[:, :, :, :], a_in["idft_fine"]).then_inc(s_tab, 16)
                sp.wait_ge(ra.full, 10)
                load_weights(k, sp, 8)
                sp.wait_ge(ra.free, 10 + NR)
                sp.wait_ge(s_zero, 1)
                sp.dma_start(raw[1:P, 0, :], raw[0:P - 1, NR, :]).then_inc(s_shift, 16)
                sp.dma_start(raw[0:P - 1, NR + 1, :], raw[1:P, 1, :]).then_inc(s_shift, 16)
                sp.wait_ge(ra.full, 20)
                load_weights(k, sp, 9)
                sp.wait_ge(s_ready, 1)
                for o in range(2):
                    if o == 1:
                        sp.wait_ge(s_prod, HT)
                    sp.dma_start(aux[:, :, :], k.spectra[o, :, 0:17, :]).then_inc(s_spec, 16)
                    sp.wait_ge(ra.free, A[o] + 8)
                    if o == 1:
                        sp.wait_ge(ra.full, A[1] + 8)
                    for g in range(GROUPS):
                        sp.dma_start(part2[:, g, :], part1[8 * g:8 * g + 8, :, :]).then_inc(s_shuf, 16)
                    sp.wait_ge(ra.free, A[o] + 16)
                    for g in range(GROUPS):
                        sp.dma_start(part1[8 * g:8 * g + 8, :, :], part2[:, g, :]).then_inc(s_shuf, 16)
                sp.wait_ge(s_shuf, 64 * GROUPS)

            @block.scalar
            def _(act):
                for n in range(2):
                    for i in range(NR + TC):
                        bank = ra.read(act)
                        dst = raw[:, i + 1, :] if i < NR else k.uc[:, i - NR, :]
                        if n == 0:
                            act.activation(dst[:, 0:2 * HW], bank[:, :], ACT.Copy).then_inc(ra.free, 1)
                        else:
                            gate = gh[:, i, :] if i < NR else dst[:, 3 * HW:4 * HW]
                            act.activation(gate, bank[:, HW:2 * HW], ACT.Silu)
                            act.activation(dst[:, 2 * HW:3 * HW], bank[:, 0:HW], ACT.Copy).then_inc(ra.free, 1)
                for o in range(2):
                    if o == 0:
                        act.wait_ge(s_ready, 1)
                    else:
                        act.wait_ge(rv.full, 12)
                    for b in range(2):
                        for q in range(4):
                            bank = ra.read(act)
                            dst = part1[:, 8 * b + 2 * q:8 * b + 2 * q + 2, :]
                            act.activation(dst, bank[:, :].rearrange("p (a c) -> p a c", a=2), ACT.Copy).then_inc(ra.free, 1)
                    for n in range(HT):
                        bank = ra.read(act)
                        g = 4 * (n // 2) + n % 2
                        act.activation(part2[:, g:g + 3:2, :], bank[:, :].rearrange("p (a c) -> p a c", a=2), ACT.Copy).then_inc(ra.free, 1)
                for half in range(2):
                    for q in range(2):
                        bank = ra.read(act)
                        dst = k.z_hy[:, half, LC:].rearrange("p (m r) -> p r m", r=NR)[:, 4 * q:4 * q + 4, :]
                        act.activation(dst, bank[:, :].rearrange("p (r m) -> p r m", r=4), ACT.Copy).then_inc(ra.free, 1)

            @block.gpsimd
            def _(pool):
                pool.memset(raw[0:1, 0, :], 0.0)
                pool.memset(raw[96:P, NR + 1, :], 0.0).then_inc(s_zero, 1)
                for o in range(2):
                    pool.wait_ge(ra.full, A[o] + 8)
                    pool.tensor_tensor(v[:, :, 0:HW], v[:, :, 0:HW], k.skip[:, o, :].unsqueeze(1).to_broadcast((P, NR, HW)),
                                       ALU.mult).then_inc(s_skip, 1)

            @block.vector
            def _(dve):
                step = Chain(s_step, dve)
                row = lambda r: r.unsqueeze(1).to_broadcast((P, NR, HW))
                dve.wait_ge(s_conv, 3 * 16)
                dve.wait_ge(s_shift, 32)
                prod = aux[:, 9:17, :]
                for g in range(3):
                    c = slice(g * HW, (g + 1) * HW)
                    x = v[:, :, c]
                    step(dve.tensor_tensor(x, raw[:, 1:NR + 1, c], row(convw[:, 1, c]), ALU.mult))
                    step(dve.tensor_tensor(x, x, row(convb[:, c]), ALU.add))
                    for j, r0 in ((0, 0), (2, 2)):
                        step(dve.tensor_tensor(prod, raw[:, r0:r0 + NR, c], row(convw[:, j, c]), ALU.mult))
                        step(dve.tensor_tensor(x, x, prod, ALU.add))
                dve.memset(tmp[:, 0, 0:1], 0.0).then_inc(s_ready, 1)
                dve.wait_ge(s_ready, 1)
                for o in range(2):
                    dve.wait_ge(s_spec, 16 * (o + 1))
                    dve.wait_ge(s_shuf, 16 * GROUPS * (2 * o + 1))
                    for T in range(HT):
                        bank = rv.read(dve)
                        x = bank[:, :].rearrange("p (r c) -> p r c", r=2)
                        y = part1[:, 2 * T:2 * T + 2, :]
                        t = tmp[:, 2 * (T % 2):2 * (T % 2) + 2, :]
                        f = aux[:, T, :].unsqueeze(1).to_broadcast((P, 2, HW)) if T else aux[:, 0:17:16, :]
                        dve.tensor_tensor(y, x, f, ALU.mult).then_inc(s_step, 1)
                        step.n += 1
                        dve.tensor_tensor(t, x, aux[:, 8 + T, :].unsqueeze(1).to_broadcast((P, 2, HW)), ALU.mult).then_inc(rv.free, 1)
                        dve.wait_ge(rv.free, rv.got)
                        dve.tensor_tensor(y[:, 0, :], y[:, 0, :], t[:, 1, :], ALU.subtract)
                        dve.tensor_tensor(y[:, 1, :], y[:, 1, :], t[:, 0, :], ALU.add).then_inc(s_prod, 1)
                    dve.wait_ge(s_prod, HT * (o + 1))
                    dve.wait_ge(s_skip, o + 1)
                    for q in range(4):
                        bank = rv.read(dve)
                        t = tmp[:, 2 * (q % 2):2 * (q % 2) + 2, :]
                        x = v[:, 2 * q:2 * q + 2, 0:HW]
                        dve.tensor_tensor(t, bank[:, :].rearrange("p (a c) -> p a c", a=2),
                                          k.inv_sum[:, o, 0, :].unsqueeze(1).to_broadcast((P, 2, HW)), ALU.mult).then_inc(rv.free, 1)
                        dve.wait_ge(rv.free, rv.got)
                        step(dve.tensor_tensor(x, x, t, ALU.add))
                        ins = dve.tensor_tensor(x, x, v[:, 2 * q:2 * q + 2, (1 + o) * HW:(2 + o) * HW], ALU.mult)
                        if o == 1:
                            step(ins)
                            ins = dve.tensor_tensor(x, x, gh[:, 2 * q:2 * q + 2, :], ALU.mult)
                        if q < 3:
                            step(ins)
                    ins.then_inc(s_y, 1)


def context_hyena_stage(k):
    nc, a_in, u = k.nc, k.a, k.uc
    with ExitStack() as mem:
        sb = lambda name, shape: sbuf(mem, nc, name, shape)
        cdft, cidft = sb("s4_cdft", [P, 2, 2, LC]), sb("s4_cidft", [P, 2, 2, LC])
        spec = sb("s4_spectra", [P, 2, 5, HW])
        convw, convb = sb("s4_conv_w", [P, 3, 3 * HW]), sb("s4_conv_b", [P, 3 * HW])
        before, after = sb("s4_before", [P, TC, 3 * HW]), sb("s4_after", [P, TC, 3 * HW])
        y, tmp = sb("s4_y", [P, 2 * TC, HW]), sb("s4_tmp", [P, 2, HW])

        ring = Ring("s4_dve", k.psum[4:8], k.sem)
        s_tab, s_zero, s_shift = k.sem("s4_tables_here"), k.sem("s4_zeroed"), k.sem("s4_shifted")
        s_step, s_v, s_prod = k.sem("s4_dve_step"), k.sem("s4_v_ready"), k.sem("s4_products")

        with nc.Block() as block:
            @block.sync
            def _(sp):
                this = k.of_layer
                sp.wait_ge(s_zero, 1)
                sp.dma_start(before[1:P, :, :], u[0:P - 1, :, 0:3 * HW]).then_inc(s_shift, 16)
                sp.dma_start(before[0:1, 1, :], u[P - 1:P, 0, 0:3 * HW]).then_inc(s_shift, 16)
                sp.dma_start(after[0:P - 1, :, :], u[1:P, :, 0:3 * HW]).then_inc(s_shift, 16)
                sp.dma_start(after[P - 1:P, 0, :], u[0:1, 1, 0:3 * HW]).then_inc(s_shift, 16)
                sp.dma_start(convw[:, :, :], this(a_in["hy_conv_w"]).rearrange("a j c -> a (j c)").to_broadcast((P, 9 * HW))).then_inc(s_tab, 16)
                sp.dma_start(convb[:, :], this(a_in["hy_conv_b"]).to_broadcast((P, 3 * HW))).then_inc(s_tab, 16)
                sp.dma_start(cdft[:, :, :, :], a_in["cdft"]).then_inc(s_tab, 16)
                sp.dma_start(cidft[:, :, :, :], a_in["cidft"]).then_inc(s_tab, 16)
                for o in range(2):
                    sp.dma_start(spec[:, o], k.spectra[o, :, 17:22, :]).then_inc(s_tab, 16)

            @block.gpsimd
            def _(pool):
                pool.memset(before[0:1, 0, :], 0.0)
                pool.memset(after[96:P, :, :], 0.0).then_inc(s_zero, 1)

            @block.tensor
            def _(pe):
                for o in range(2):
                    pe.wait_ge(s_tab, 6 * 16)
                    pe.wait_ge(s_v, o + 1)
                    for T in range(2):
                        bank = ring.fill(pe)
                        for ri in range(2):
                            for kk in range(TC):
                                mm = pe.matmul(bank[:, ri * HW:(ri + 1) * HW], cdft[:, ri, kk, T * P:(T + 1) * P], u[:, kk, 0:HW],
                                               start=(kk == 0), stop=(kk == TC - 1))
                        mm.then_inc(ring.full, 1)
                    pe.wait_ge(s_prod, o + 1)
                    bank = ring.fill(pe)
                    for kk in range(TC):
                        for n in range(4):
                            T, ri = n // 2, n % 2
                            mm = pe.matmul(bank[:, kk * HW:(kk + 1) * HW], cidft[:, ri, T, kk * P:(kk + 1) * P], y[:, n, :],
                                           start=(n == 0), stop=(n == 3))
                    mm.then_inc(ring.full, 1)
                pe.wait_ge(s_v, 3)
                bank = ring.fill(pe)
                for half in range(2):
                    for kk in range(TC):
                        c0 = (2 * half + kk) * P
                        mm = pe.transpose(bank[:, c0:c0 + P], u[:, kk, half * P:(half + 1) * P], k.ident[:, :])
                mm.then_inc(ring.full, 1)

            @block.vector
            def _(dve):
                step = Chain(s_step, dve)
                wide = lambda r: r.unsqueeze(1).to_broadcast((P, TC, r.shape[-1]))
                x = u[:, :, 0:3 * HW]
                dve.wait_ge(s_tab, 6 * 16)
                dve.wait_ge(s_shift, 4 * 16)
                step(dve.tensor_tensor(x, x, wide(convw[:, 1, :]), ALU.mult))
                step(dve.tensor_tensor(x, x, wide(convb[:, :]), ALU.add))
                for buf, j in ((before, 0), (after, 2)):
                    step(dve.tensor_tensor(buf[:, :, :], buf[:, :, :], wide(convw[:, j, :]), ALU.mult))
                    ins = dve.tensor_tensor(x, x, buf[:, :, :], ALU.add)
                    if j == 0:
                        step(ins)
                ins.then_inc(s_v, 1)
                for o in range(2):
                    for T in range(2):
                        bank = ring.read(dve)
                        xf = bank[:, :].rearrange("p (r c) -> p r c", r=2)
                        f = wide(spec[:, o, 1, :]) if T else spec[:, o, 0:5:4, :]
                        yy = y[:, 2 * T:2 * T + 2, :]
                        step(dve.tensor_tensor(yy, xf, f, ALU.mult))
                        dve.tensor_tensor(tmp[:, :, :], xf, wide(spec[:, o, 2 + T, :]), ALU.mult).then_inc(ring.free, 1)
                        dve.wait_ge(ring.free, ring.got)
                        step(dve.tensor_tensor(yy[:, 0, :], yy[:, 0, :], tmp[:, 1, :], ALU.subtract))
                        ins = dve.tensor_tensor(yy[:, 1, :], yy[:, 1, :], tmp[:, 0, :], ALU.add)
                        if T == 0:
                            step(ins)
                    ins.then_inc(s_prod, 1)
                    bank = ring.read(dve)
                    v = u[:, :, 0:HW]
                    dve.tensor_tensor(tmp[:, :, :], bank[:, :].rearrange("p (a c) -> p a c", a=2), wide(k.inv_sum[:, o, 1, :]), ALU.mult).then_inc(ring.free, 1)
                    dve.wait_ge(ring.free, ring.got)
                    step(dve.tensor_tensor(v, v, wide(k.skip[:, o, :]), ALU.mult))
                    step(dve.tensor_tensor(v, v, tmp[:, :, :], ALU.add))
                    ins = dve.tensor_tensor(v, v, u[:, :, (1 + o) * HW:(2 + o) * HW], ALU.mult)
                    if o == 1:
                        step(ins)
                        ins = dve.tensor_tensor(v, v, u[:, :, 3 * HW:4 * HW], ALU.mult)
                    ins.then_inc(s_v, 1)
                bank = ring.read(dve)
                dve.tensor_copy(k.z_hy[:, :, 0:LC], bank[:, :].rearrange("p (h t) -> p h t", h=2)).then_inc(ring.free, 1)


ROWS = L // GRID


def window(i):
    if i < TC:
        return None
    r = 2 * (i - TC)
    s = min(max(r - KH // 2, 0), ROWS - KH)
    inner = r - KH // 2 == s and r + 1 - KH // 2 <= ROWS - KH and r - KH // 2 >= 0
    return s, KH + (1 if inner and r + 1 - KH // 2 == s + 1 else 0), s - r + KH - 1


def attention_stage(k):
    nc, a_in = k.nc, k.a
    HEADS = 4
    UNITS = HEADS * TILES
    NW = (KH + 1) * GRID
    BLOCKS = TC + (NW + P - 1) // P
    with ExitStack() as mem:
        sb = lambda name, shape: sbuf(mem, nc, name, shape)
        qT, kT = sb("s5_qT", [P, 2, TOK]), sb("s5_kT", [P, 2, TOK])
        v, g = sb("s5_v", [P, TILES, 256]), sb("s5_g", [P, TILES, 256])
        qk, square = sb("s5_qk", [P, 2, 512]), sb("s5_square", [P, 512])
        norm = sb("s5_norm", [P, 2, 3, 8])
        gains = sb("s5_gains", [P, 2])
        eps = sb("s5_eps", [P, 1])
        mask = sb("s5_mask", [P, GRID])
        table = sb("s5_bias", [P, 2, 2 * KH, GRID])
        raw = sb("s5_raw_bias", [P, 2 * KH, GRID])
        inner = sb("s5_inner_bias", [P, 2, KH + 1, GRID])
        s_sb, p_sb = sb("s5_scores", [P, 2, NW]), sb("s5_probs", [P, 2, LC + NW])
        pT = sb("s5_probsT", [P, 2, BLOCKS * P])
        top, total = sb("s5_max", [P, 4, 3]), sb("s5_sum", [P, 4, 4])

        ra, rv = Ring("s5_act", k.psum[0:4], k.sem), Ring("s5_dve", k.psum[4:8], k.sem)
        s_in, s_bias, s_zero = k.sem("s5_gains_here"), k.sem("s5_bias_ready"), k.sem("s5_eps")
        s_raw = k.sem("s5_raw_bias_here")
        s_sq, s_ss, s_rt = (k.sem("s5_" + n) for n in ("squares", "square_sums", "roots"))
        s_scores, s_max, s_exp = k.sem("s5_scores"), k.sem("s5_max_ready"), k.sem("s5_exp_done")
        s_t0, s_t1, s_c0, s_c1 = (k.sem("s5_" + n) for n in ("probsT_low", "probsT_high", "probsT_low_copied", "probsT_high_copied"))
        s_o, s_z, s_step, s_pool = k.sem("s5_o"), k.sem("s5_z"), k.sem("s5_dve_step"), k.sem("s5_pool_step")
        RA, RV = TILES + TILES // 2, 2 * TILES

        def unit(n):
            return n // UNITS, n % UNITS // TILES, n % TILES

        def scores_of(n):
            return k.all_psum[:, (n % 2) * 1024:(n % 2) * 1024 + 1024]

        def blocks(i):
            out = [(0, P), (1, P)]
            if window(i):
                s, rows, _ = window(i)
                keys = rows * GRID
                out += [(TC + s // 2 + b, min(P, keys - b * P)) for b in range((keys + P - 1) // P)]
            return out

        def qk_unit(half, i):
            return RV * half + max(2 * i, 1)

        def turn_unit(half, i):
            return RV * half + min(2 * i + 3, RV)

        def place(i, b):
            return 4 if i < TC and b == 1 else b

        with nc.Block() as block:
            @block.sync
            def _(sp):
                this = k.of_layer
                for c, name in enumerate(("na_q_gain", "na_k_gain")):
                    for h in range(2):
                        sp.dma_start(gains[64 * h:64 * h + 64, c:c + 1], this(a_in[name]).rearrange("a n -> n a")).then_inc(s_in, 16)
                sp.dma_start(mask[:, :], a_in["colmask"]).then_inc(s_in, 16)
                for h in range(2 * HEADS):
                    if h >= 1:
                        sp.wait_ge(s_bias, h)
                    rpb = this(a_in["na_rpb"])[:, h]
                    for part in range(2):
                        src = bass.AP(rpb.tensor, rpb.offset + (1 - part) * P, [[1, GRID], [P, 2 * KH], [1, GRID]])
                        sp.dma_start(raw[64 * part:64 * part + 64], src).then_inc(s_raw, 16)
                    if h == 2:
                        sp.wait_ge(ra.free, TILES)
                        load_weights(k, sp, 10)
                        load_weights(k, sp, 11)
                sp.wait_ge(ra.free, RA + TILES)
                load_weights(k, sp, 12)
                load_weights(k, sp, 13)

            @block.gpsimd
            def _(pool):
                pool.wait_ge(s_in, 5 * 16)
                for h in range(2 * HEADS):
                    pool.wait_ge(s_raw, 32 * (h + 1))
                    t = table[:, h % 2]
                    if h >= 1:
                        pool.wait_ge(s_bias, h)
                    if h >= 2:
                        pool.wait_ge(s_max, TILES * (h - 1))
                    pool.tensor_tensor(t, raw[:, :, ::-1], mask[:, :].unsqueeze(1).to_broadcast((P, 2 * KH, GRID)), ALU.add).then_inc(s_pool, 1)
                    pool.wait_ge(s_pool, 3 * h + 1)
                    pool.tensor_copy(inner[:, h % 2], t[:, 3:4 + KH, :]).then_inc(s_pool, 1)
                    pool.wait_ge(s_pool, 3 * h + 2)
                    pool.memset(inner[0:64, h % 2, KH, :], NEG).then_inc(s_pool, 1)
                    pool.wait_ge(s_pool, 3 * h + 3)
                    pool.memset(inner[64:128, h % 2, 0, :], NEG).then_inc(s_bias, 1)

            @block.tensor
            def _(pe):
                def projections(half):
                    w = wait_weights(k, pe, 8 + 2 * half)

                    def turn(i):
                        pe.wait_ge(rv.free, qk_unit(half, i))
                        bank = rv.fill(pe)
                        for m in range(4):
                            mm = pe.transpose(bank[:, m * P:(m + 1) * P], qk[:, i % 2, m * P:(m + 1) * P], k.ident[:, :])
                        mm.then_inc(rv.full, 1)

                    def project(ring, w, i):
                        bank = ring.fill(pe)
                        for kc in range(KC):
                            mm = pe.matmul(bank[:, :], k.hxT[:, kc, i * P:(i + 1) * P], w[:, kc, :], start=(kc == 0), stop=(kc == KC - 1))
                        mm.then_inc(ring.full, 1)

                    for i in range(TILES):
                        project(rv, w, i)
                        if i >= 1:
                            turn(i - 1)
                    w = wait_weights(k, pe, 9 + 2 * half)
                    project(ra, w, 0)
                    turn(TILES - 1)
                    for i in range(1, TILES):
                        project(ra, w, i)

                def scores(n):
                    half, h, i = unit(n)
                    if n >= 2:
                        pe.wait_ge(s_exp, n - 1)
                    rows, pair = slice(64 * (h % 2), 64 * (h % 2) + 64), h // 2
                    q = qT[rows, pair, i * P:(i + 1) * P]
                    bank = scores_of(n)
                    mm = pe.matmul(bank[:, 0:LC], q, kT[rows, pair, 0:LC], start=True, stop=True)
                    if window(i):
                        s, n_rows, _ = window(i)
                        k0 = LC + s * GRID
                        pe.matmul(bank[:, LC:512], q, kT[rows, pair, k0:k0 + 256], start=True, stop=True)
                        mm = pe.matmul(bank[:, 512:LC + n_rows * GRID], q, kT[rows, pair, k0 + 256:k0 + n_rows * GRID], start=True, stop=True)
                    mm.then_inc(s_scores, 1)

                def turn_probs(n):
                    _, _, i = unit(n)
                    pe.wait_ge(s_exp, n + 1)
                    if n >= 1:
                        pe.wait_ge(s_c0, n)
                    for b, (_, keys) in enumerate(blocks(i)):
                        at = place(i, b)
                        if at == 4 and n >= 1:
                            pe.wait_ge(s_c1, n)
                        mm = pe.transpose(k.all_psum[0:keys, 2048 + at * P:2048 + (at + 1) * P], p_sb[:, n % 2, b * P:b * P + keys], k.ident[:, :])
                        if place(i, b + 1) == 4:
                            mm.then_inc(s_t0, 1)
                    mm.then_inc(s_t1, 1)

                def outputs(n):
                    _, h, i = unit(n)
                    pe.wait_ge(s_c0, n + 1)
                    pe.wait_ge(s_c1, n + 1)
                    if n >= 2:
                        pe.wait_ge(s_z, n - 1)
                    bank = k.psum[6 + n % 2]
                    last = len(blocks(i)) - 1
                    for b, (tile, keys) in enumerate(blocks(i)):
                        mm = pe.matmul(bank[:, 0:HD], pT[0:keys, n % 2, place(i, b) * P:(place(i, b) + 1) * P], v[0:keys, tile, h * HD:(h + 1) * HD],
                                       start=(b == 0), stop=(b == last))
                    mm.then_inc(s_o, 1)

                for half in range(2):
                    n0, n1 = half * UNITS, (half + 1) * UNITS
                    projections(half)
                    pe.wait_ge(rv.free, RV * (half + 1))
                    pe.wait_ge(ra.free, RA * half + TILES)
                    for n in range(n0, n1 + 2):
                        if n < n1:
                            scores(n)
                        if n0 <= n - 1 < n1:
                            turn_probs(n - 1)
                        if n0 <= n - 2 < n1:
                            outputs(n - 2)
                    pe.wait_ge(s_z, n1)
                    for t in range(TILES // 2):
                        bank = ra.fill(pe)
                        for m in range(4):
                            mm = pe.transpose(bank[:, m * P:(m + 1) * P], g[:, 2 * t + m % 2, (m // 2) * P:(m // 2 + 1) * P], k.ident[:, :])
                        mm.then_inc(ra.full, 1)

            @block.scalar
            def _(act):
                act.wait_ge(s_zero, 1)
                for half in range(2):
                    for i in range(TILES):
                        n = TILES * half + i
                        act.wait_ge(rv.full, qk_unit(half, i))
                        if n >= 1:
                            act.wait_ge(s_ss, n)
                        act.activation(square[:, :], rv.banks[(qk_unit(half, i) - 1) % 4][:, :], ACT.Square).then_inc(s_sq, 1)
                        act.wait_ge(s_ss, n + 1)
                        act.activation(norm[:, i % 2, 1, :], norm[:, i % 2, 0, :], ACT.Sqrt, bias=eps[:, 0:1], scale=1.0 / HD).then_inc(s_rt, 1)
                    for i in range(TILES):
                        bank = ra.read(act)
                        act.activation(g[:, i, :], bank[:, 256:512], ACT.Silu)
                        act.activation(v[:, i, :], bank[:, 0:256], ACT.Copy).then_inc(ra.free, 1)
                    n0, n1 = half * UNITS, (half + 1) * UNITS
                    for n in range(n0, n1 + 1):
                        if n < n1:
                            i = unit(n)[2]
                            act.wait_ge(s_max, n + 1)
                            if n >= 2:
                                act.wait_ge(s_t1, n - 1)
                            bias = top[:, n % 4, 2:3]
                            if window(i):
                                keys = window(i)[1] * GRID
                                act.activation(p_sb[:, n % 2, LC:LC + keys], s_sb[:, n % 2, 0:keys], ACT.Exp, bias=bias,
                                               accum_out=total[:, n % 4, 1:2])
                            act.activation(p_sb[:, n % 2, 0:LC], scores_of(n)[:, 0:LC], ACT.Exp, bias=bias,
                                           accum_out=total[:, n % 4, 0:1]).then_inc(s_exp, 1)
                        if n - 1 >= n0:
                            m = n - 1
                            cols = (4 if window(unit(m)[2]) else 1) * P
                            act.wait_ge(s_t0, m + 1)
                            if m >= 2:
                                act.wait_ge(s_o, m - 1)
                            act.activation(pT[:, m % 2, 0:cols], k.all_psum[:, 2048:2048 + cols], ACT.Copy).then_inc(s_c0, 1)
                    for t in range(TILES // 2):
                        bank = ra.read(act)
                        act.activation(k.z_na[:, 2 * half:2 * half + 2, 2 * t * P:(2 * t + 2) * P],
                                       bank[:, :].rearrange("p (c t) -> p c t", c=2), ACT.Copy).then_inc(ra.free, 1)

            @block.vector
            def _(dve):
                step = Chain(s_step, dve)
                dve.memset(eps[:, :], EPS).then_inc(s_zero, 1)
                dve.wait_ge(s_in, 5 * 16)
                step(dve.tensor_scalar(gains[:, 0:1], gains[:, 0:1], HD ** -0.5, None, ALU.mult))

                def turned(half, i):
                    bank = rv.read(dve)
                    for c, dst in enumerate((qT, kT)):
                        ins = dve.tensor_scalar(dst[:, :, i * P:(i + 1) * P], bank[:, c * 256:(c + 1) * 256].rearrange("p (m t) -> p m t", m=2),
                                                gains[:, c:c + 1], None, ALU.mult)
                    ins.then_inc(rv.free, 1)

                def maximum(n):
                    half, h, i = unit(n)
                    dve.wait_ge(s_scores, n + 1)
                    slot = top[:, n % 4]
                    bank = scores_of(n)
                    best = slot[:, 0:1]
                    dve.tensor_reduce(best, bank[:, 0:LC], AX.X, ALU.max).then_inc(s_step, 1)
                    step.n += 1
                    if window(i):
                        s, rows, first = window(i)
                        head = HEADS * half + h
                        if i == TC:
                            dve.wait_ge(s_bias, head + 1)
                        bias = inner[:, head % 2] if rows > KH else table[:, head % 2, first:first + KH, :]
                        keys = rows * GRID
                        step(dve.tensor_tensor_reduce(s_sb[:, n % 2, 0:keys], bank[:, LC:LC + keys], bias.rearrange("p j c -> p (j c)"),
                                                      1.0, -3e38, ALU.add, ALU.max, slot[:, 1:2]))
                        dve.tensor_scalar(slot[:, 2:3], best, slot[:, 1:2], -1.0, ALU.max, ALU.mult).then_inc(s_max, 1)
                    else:
                        dve.wait_ge(s_step, step.n)
                        dve.tensor_scalar(slot[:, 2:3], best, -1.0, None, ALU.mult).then_inc(s_max, 1)

                def copy_high(n):
                    i = unit(n)[2]
                    dve.wait_ge(s_t1, n + 1)
                    if n >= 2:
                        dve.wait_ge(s_o, n - 1)
                    parts = [(place(i, b), keys) for b, (_, keys) in enumerate(blocks(i)) if place(i, b) >= 4]
                    full = sum(keys == P for _, keys in parts)
                    at = 4 * P
                    cols = full * P
                    ins = dve.tensor_copy(pT[:, n % 2, at:at + cols], k.all_psum[:, 2048 + at:2048 + at + cols])
                    if full < len(parts):
                        at += cols
                        ins = dve.tensor_copy(pT[0:64, n % 2, at:at + P], k.all_psum[0:64, 2048 + at:2048 + at + P])
                    ins.then_inc(s_c1, 1)

                def gated(n):
                    half, h, i = unit(n)
                    slot = total[:, n % 4]
                    if i < TC:
                        step(dve.reciprocal(slot[:, 3:4], slot[:, 0:1]))
                    else:
                        step(dve.tensor_tensor(slot[:, 2:3], slot[:, 0:1], slot[:, 1:2], ALU.add))
                        step(dve.reciprocal(slot[:, 3:4], slot[:, 2:3]))
                    dve.wait_ge(s_o, n + 1)
                    z = g[:, i, h * HD:(h + 1) * HD]
                    dve.scalar_tensor_tensor(out=z, in0=k.psum[6 + n % 2][:, 0:HD], scalar=slot[:, 3:4], in1=z, op0=ALU.mult, op1=ALU.mult).then_inc(s_z, 1)

                for half in range(2):
                    for i in range(TILES):
                        n = TILES * half + i
                        dve.wait_ge(s_sq, n + 1)
                        dve.tensor_reduce(norm[:, i % 2, 0, :], square[:, :].rearrange("p (h d) -> p h d", d=HD), AX.X, ALU.add).then_inc(s_ss, 1)
                        dve.wait_ge(s_rt, n + 1)
                        step(dve.reciprocal(norm[:, i % 2, 2, :], norm[:, i % 2, 1, :]))
                        if n >= 2:
                            dve.wait_ge(rv.full, turn_unit((n - 2) // TILES, (n - 2) % TILES))
                        bank = rv.read(dve)
                        dve.tensor_tensor(qk[:, i % 2, :].rearrange("p (h d) -> p h d", d=HD), bank[:, :].rearrange("p (h d) -> p h d", d=HD),
                                          norm[:, i % 2, 2, :].unsqueeze(2).to_broadcast((P, 8, HD)), ALU.mult).then_inc(rv.free, 1)
                        if i >= 1:
                            turned(half, i - 1)
                    turned(half, TILES - 1)
                    n0, n1 = half * UNITS, (half + 1) * UNITS
                    for n in range(n0, n1 + 2):
                        if n < n1:
                            maximum(n)
                        if n0 <= n - 1 < n1:
                            copy_high(n - 1)
                        if n0 <= n - 2 < n1:
                            gated(n - 2)


CHAINS = (list(range(TILES)), [1, 0] + list(range(TILES - 1, TC - 1, -1)))


def retention_stage(k):
    nc, a_in = k.nc, k.a
    with ExitStack() as mem:
        sb = lambda name, shape: sbuf(mem, nc, name, shape)
        qk, vg = sb("s6_qk", [P, TILES, 512]), sb("s6_vg", [P, TILES, 512])
        rope, tmp = sb("s6_rope", [P, TILES, 64]), sb("s6_tmp", [P, 512])
        dist, age, rest = sb("s6_dist", [P, 4, P]), sb("s6_age", [P, 2, P]), sb("s6_rest", [P, 8])
        rate, zeta = sb("s6_log_gamma", [P, 8]), sb("s6_zeta", [P, 8])
        rate_p, power = sb("s6_log_gamma_turned", [P, 4]), sb("s6_chunk_decay", [P, 4])
        decay = sb("s6_decay", [P, 2, 2, P])
        fade = sb("s6_fade", [P, 2, 2, P])
        state = sb("s6_state", [P, TILES, 2, P])
        kz = sb("s6_k_weighted", [P, 2, 2, RW])
        qkT, qx = sb("s6_qkT", [P, 2, 512]), sb("s6_q_faded", [P, 2, 2, RW])
        sT, r = sb("s6_scoresT", [P, 2, 2, RW]), sb("s6_r", [P, 2, RW])
        stat, eps = sb("s6_stat", [P, 2, 3, RH]), sb("s6_eps", [P, 1])

        ra, rv = Ring("s6_act", k.psum[0:4], k.sem), Ring("s6_dve", k.psum[4:8], k.sem)
        names = ("tables_here", "rates", "tables", "dve_step", "act_step", "roped", "k_weighted", "weighted_free", "states",
                 "q_faded", "scores", "scores_weighted", "o", "o_copied", "square_sums", "roots", "z", "eps", "pool_step")
        (s_tab, s_rate, s_table, s_step, s_act, s_rope, s_kz, s_kzfree, s_state, s_qx, s_sc, s_sw, s_o, s_oc, s_ss, s_rt, s_z,
         s_eps, s_pool) = (k.sem("s6_" + n) for n in names)

        with nc.Block() as block:
            @block.sync
            def _(sp):
                rates = k.of_layer(a_in["ret_log_rate"])
                sp.dma_start(rate[:, :], rates.rearrange("a d h -> a (d h)").to_broadcast((P, 8))).then_inc(s_tab, 16)
                for h2 in range(2):
                    src = rates.rearrange("a d (p h) -> a (d p) h", h=2)[:, :, h2]
                    sp.dma_start(rate_p[64 * h2:64 * h2 + 64, :], src.to_broadcast((64, 4))).then_inc(s_tab, 16)
                sp.dma_start(rest[:, :], a_in["rest"].rearrange("p d h -> p (d h)")).then_inc(s_tab, 16)
                sp.dma_start(dist[:, :, :], a_in["dist"]).then_inc(s_tab, 16)
                sp.dma_start(age[:, :, :], a_in["age"]).then_inc(s_tab, 16)
                sp.dma_start(rope[:, :, :], a_in["rope"]).then_inc(s_tab, 16)
                sp.wait_ge(rv.full, TILES)
                load_weights(k, sp, 14)
                sp.wait_ge(ra.full, TILES)
                load_weights(k, sp, 15)

            @block.tensor
            def _(pe):
                for ring, n in ((rv, 12), (ra, 13)):
                    w = wait_weights(k, pe, n)
                    for i in range(TILES):
                        bank = ring.fill(pe)
                        for kc in range(KC):
                            mm = pe.matmul(bank[:, :], k.hxT[:, kc, i * P:(i + 1) * P], w[:, kc, :], start=(kc == 0), stop=(kc == KC - 1))
                        mm.then_inc(ring.full, 1)
                pe.wait_ge(ra.free, TILES)
                for j in range(TILES - 1):
                    pe.wait_ge(s_kz, 2 * j + 2)
                    bank = rv.fill(pe)
                    for d in range(2):
                        t = CHAINS[d][j]
                        for h in range(RH):
                            mm = pe.matmul(bank[64 * (h % 2):64 * (h % 2) + 64, d * P + (h // 2) * HD:d * P + (h // 2 + 1) * HD],
                                           kz[:, j % 2, d, h * HD:(h + 1) * HD], vg[:, t, h * HD:(h + 1) * HD], start=True, stop=True)
                    mm.then_inc(rv.full, 1)

                def turn(i):
                    bank = ra.fill(pe)
                    for m in range(4):
                        mm = pe.transpose(bank[:, m * P:(m + 1) * P], qk[:, i, m * P:(m + 1) * P], k.ident[:, :])
                    mm.then_inc(ra.full, 1)

                pe.wait_ge(rv.free, 2 * TILES - 1)
                turn(0)
                for i in range(TILES):
                    if i + 1 < TILES:
                        turn(i + 1)
                    pe.wait_ge(ra.free, TILES + i + 1)
                    if i >= 1:
                        pe.wait_ge(s_sw, i)
                    for h in (0, 2, 1, 3):
                        rows = slice(64 * (h % 2), 64 * (h % 2) + 64)
                        pair = h // 2
                        mm = pe.matmul(k.psum[4 + h % 2][:, pair * P:(pair + 1) * P], qkT[rows, i % 2, (2 + pair) * P:(3 + pair) * P],
                                       qkT[rows, i % 2, pair * P:(pair + 1) * P], start=True, stop=True)
                    mm.then_inc(s_sc, 1)
                    pe.wait_ge(s_sw, i + 1)
                    pe.wait_ge(s_qx, i + 1)
                    if i >= 1:
                        pe.wait_ge(s_oc, i)
                    for h in (0, 2, 1, 3):
                        rows = slice(64 * (h % 2), 64 * (h % 2) + 64)
                        pair = h // 2
                        out = k.psum[6 + h % 2][:, pair * HD:(pair + 1) * HD]
                        pe.matmul(out, sT[:, i % 2, h % 2, pair * P:(pair + 1) * P], vg[:, i, h * HD:(h + 1) * HD], start=True, stop=False)
                        for d in range(2):
                            mm = pe.matmul(out, qx[rows, i % 2, d, pair * P:(pair + 1) * P], state[rows, i, d, pair * HD:(pair + 1) * HD],
                                           start=False, stop=(d == 1))
                    mm.then_inc(s_o, 1)
                pe.wait_ge(s_z, TILES)
                for t in range(TILES // 2):
                    bank = ra.fill(pe)
                    for m in range(4):
                        mm = pe.transpose(bank[:, m * P:(m + 1) * P], qk[:, 2 * t + m % 2, (m // 2) * P:(m // 2 + 1) * P], k.ident[:, :])
                    mm.then_inc(ra.full, 1)

            @block.scalar
            def _(act):
                act.wait_ge(s_tab, 7 * 16)
                act.activation(rate[:, :], rate[:, :], ACT.Exp)
                act.activation(rate_p[:, :], rate_p[:, :], ACT.Exp).then_inc(s_rate, 1)
                act.wait_ge(s_table, 1)
                act.activation(zeta[:, :], zeta[:, :], ACT.Exp).then_inc(s_act, 1)
                act.activation(power[:, :], rate_p[:, :], ACT.Exp, scale=float(P)).then_inc(s_act, 1)
                for d in range(2):
                    for pair in range(2):
                        act.activation(fade[:, d, pair, :], age[:, d, :], ACT.Exp, scale=rate_p[:, 2 * d + pair:2 * d + pair + 1]).then_inc(s_act, 1)
                for h in range(RH):
                    if h >= 1:
                        act.wait_ge(s_table, 1 + h)
                    for d in range(2):
                        act.activation(tmp[:, d * P:(d + 1) * P], dist[:, d, :], ACT.Exp, scale=rate[:, RH * d + h:RH * d + h + 1]).then_inc(s_act, 1)
                for i in range(TILES):
                    bank = ra.read(act)
                    act.activation(vg[:, i, RW:2 * RW], bank[:, RW:2 * RW], ACT.Silu)
                    act.activation(vg[:, i, 0:RW], bank[:, 0:RW], ACT.Copy).then_inc(ra.free, 1)
                act.wait_ge(s_eps, 1)

                def root(i):
                    act.wait_ge(s_ss, i + 1)
                    act.activation(stat[:, i % 2, 1, :], stat[:, i % 2, 0, :], ACT.Sqrt, bias=eps[:, 0:1], scale=1.0 / HD).then_inc(s_rt, 1)

                for i in range(TILES):
                    if i >= 2:
                        root(i - 2)
                        act.wait_ge(s_qx, i - 1)
                        act.wait_ge(s_sc, i - 1)
                    bank = ra.read(act)
                    act.activation(qkT[:, i % 2, :], bank[:, :], ACT.Copy).then_inc(ra.free, 1)
                root(TILES - 2)
                root(TILES - 1)
                for t in range(TILES // 2):
                    bank = ra.read(act)
                    act.activation(k.z_re[:, :, 2 * t * P:(2 * t + 2) * P], bank[:, :].rearrange("p (c t) -> p c t", c=2), ACT.Copy).then_inc(ra.free, 1)

            @block.gpsimd
            def _(pool):
                pool.memset(state[:, 0, 0, :], 0.0).then_inc(s_pool, 1)
                pool.memset(state[:, 1, 1, :], 0.0).then_inc(s_pool, 1)
                pool.wait_ge(s_pool, 2)
                pool.wait_ge(s_table, 6)
                pool.wait_ge(s_rope, TILES)
                for j in range(TILES - 1):
                    if j >= 2:
                        pool.wait_ge(rv.full, TILES + j - 1)
                    for d in range(2):
                        t = CHAINS[d][j]
                        if j or d:
                            pool.wait_ge(s_kz, 2 * j + d)
                        pool.tensor_tensor(kz[:, j % 2, d, :].rearrange("p (h e) -> p h e", h=RH),
                                           qk[:, t, RW:2 * RW].rearrange("p (h e) -> p h e", h=RH),
                                           zeta[:, RH * d:RH * d + RH].unsqueeze(2).to_broadcast((P, RH, HD)), ALU.mult).then_inc(s_kz, 1)

            @block.vector
            def _(dve):
                step = Chain(s_step, dve)
                dve.memset(eps[:, :], EPS).then_inc(s_eps, 1)
                dve.wait_ge(s_rate, 1)
                step(dve.tensor_scalar(rate[:, :], rate[:, :], -1.0, None, ALU.mult))
                dve.tensor_scalar(rate_p[:, :], rate_p[:, :], -1.0, None, ALU.mult).then_inc(s_step, 1)
                step.n += 1
                dve.tensor_tensor(zeta[:, :], rest[:, :], rate[:, :], ALU.mult).then_inc(s_table, 1)
                for h in range(RH):
                    dve.wait_ge(s_act, 6 + 2 * h + 2)
                    dst = decay[:, h % 2, h // 2, :]
                    step(dve.tensor_tensor(dst, tmp[:, 0:P], dist[:, 2, :], ALU.mult))
                    step(dve.tensor_tensor(tmp[:, P:2 * P], tmp[:, P:2 * P], dist[:, 3, :], ALU.mult))
                    dve.tensor_tensor(dst, dst, tmp[:, P:2 * P], ALU.add).then_inc(s_table, 1)
                dve.wait_ge(s_table, 1 + RH)
                dve.tensor_scalar(zeta[:, :], zeta[:, :], HD ** -0.5, None, ALU.mult).then_inc(s_table, 1)

                for i in range(TILES):
                    bank = rv.read(dve)
                    halves = lambda x, n: x.rearrange("p (g n c) -> p g n c", n=2, c=16)[:, :, n, :].rearrange("p (h a) c -> p h a c", a=2)
                    x1, x2 = halves(bank[:, :], 0), halves(bank[:, :], 1)
                    o1, o2 = halves(qk[:, i, :], 0), halves(qk[:, i, :], 1)
                    cos, sin = (rope[:, i, 32 * n:32 * n + 32].rearrange("p (a c) -> p a c", a=2).unsqueeze(1).to_broadcast((P, 8, 2, 16)) for n in range(2))
                    t1 = tmp[:, 0:256].rearrange("p (h a c) -> p h a c", a=2, c=16)
                    t2 = tmp[:, 256:512].rearrange("p (h a c) -> p h a c", a=2, c=16)
                    dve.tensor_tensor(o1, x1, cos, ALU.mult)
                    step(dve.tensor_tensor(t1, x2, sin, ALU.mult))
                    step(dve.tensor_tensor(o1, o1, t1, ALU.subtract))
                    dve.tensor_tensor(o2, x1, sin, ALU.mult)
                    dve.tensor_tensor(t2, x2, cos, ALU.mult).then_inc(rv.free, 1)
                    dve.wait_ge(rv.free, rv.got)
                    dve.tensor_tensor(o2, o2, t2, ALU.add).then_inc(s_rope, 1)
                dve.wait_ge(s_rope, TILES)
                dve.wait_ge(s_pool, 2)
                for j in range(TILES - 1):
                    bank = rv.read(dve)
                    for d in range(2):
                        a, b = CHAINS[d][j], CHAINS[d][j + 1]
                        for pair in range(2):
                            c = slice(pair * HD, (pair + 1) * HD)
                            ins = dve.scalar_tensor_tensor(out=state[:, b, d, c], in0=state[:, a, d, c], scalar=power[:, 2 * d + pair:2 * d + pair + 1],
                                                           in1=bank[:, d * P + pair * HD:d * P + (pair + 1) * HD], op0=ALU.mult, op1=ALU.add)
                    ins.then_inc(rv.free, 1)
                    dve.wait_ge(rv.free, rv.got)

                def normed(i):
                    dve.wait_ge(s_rt, i + 1)
                    st = stat[:, i % 2]
                    step(dve.reciprocal(st[:, 2, :], st[:, 1, :]))
                    rr = r[:, i % 2, :]
                    heads = lambda x: x.rearrange("p (h e) -> p h e", h=RH)
                    step(dve.tensor_tensor(heads(rr), heads(rr), st[:, 2, :].unsqueeze(2).to_broadcast((P, RH, HD)), ALU.mult))
                    dve.tensor_tensor(qk[:, i, 0:RW], rr, vg[:, i, RW:2 * RW], ALU.mult).then_inc(s_z, 1)

                for i in range(TILES):
                    dve.wait_ge(ra.free, TILES + i + 1)
                    if i >= 2:
                        dve.wait_ge(s_o, i - 1)
                    for d in range(2):
                        ins = dve.tensor_tensor(qx[:, i % 2, d, :], qkT[:, i % 2, 0:RW], fade[:, d, :, :].rearrange("p a j -> p (a j)"), ALU.mult)
                    ins.then_inc(s_qx, 1)
                    dve.wait_ge(s_sc, i + 1)
                    for h2 in range(2):
                        ins = dve.tensor_tensor(sT[:, i % 2, h2, :], k.psum[4 + h2][:, 0:RW], decay[:, h2, :, :].rearrange("p a j -> p (a j)"), ALU.mult)
                    ins.then_inc(s_sw, 1)
                    if i >= 1:
                        normed(i - 1)
                    dve.wait_ge(s_o, i + 1)
                    for h2 in range(2):
                        ins = dve.tensor_copy(r[:, i % 2, :].rearrange("p (a h e) -> p h a e", h=2, e=HD)[:, h2], k.psum[6 + h2][:, 0:P].rearrange("p (a e) -> p a e", a=2))
                    ins.then_inc(s_oc, 1)
                    dve.wait_ge(s_oc, i + 1)
                    step(dve.tensor_tensor(tmp[:, 0:RW], r[:, i % 2, :], r[:, i % 2, :], ALU.mult))
                    dve.tensor_reduce(stat[:, i % 2, 0, :], tmp[:, 0:RW].rearrange("p (h e) -> p h e", h=RH), AX.X, ALU.add).then_inc(s_ss, 1)
                normed(TILES - 1)


def output_stage(k):
    nc = k.nc
    BUFS = 3
    with ExitStack() as mem:
        x = sbuf(mem, nc, "s7_x", [P, BUFS, D])
        y = sbuf(mem, nc, "s7_y", [P, 2, WCH])
        s_x = [k.sem(f"s7_x{b}_here") for b in range(BUFS)]
        s_new, s_step = k.sem("s7_x_new"), k.sem("s7_dve_step")
        s_out = [k.sem(f"s7_x{b}_stored") for b in range(BUFS)]
        ring = Ring("s7_dve", k.psum, k.sem)
        z = [k.z_na[:, c, :] for c in range(4)] + [k.z_hy[:, c, :] for c in range(2)] + [k.z_re[:, c, :] for c in range(2)]
        with nc.Block() as block:
            @block.sync
            def _(sp):
                def load(i):
                    sp.dma_start(x[:, i % BUFS, :], stream_tile(k, i)).then_inc(s_x[i % BUFS], 16)

                for i in range(BUFS):
                    load(i)
                for i in range(TILES):
                    sp.wait_ge(s_new, i + 1)
                    sp.dma_start(stream_tile(k, i), x[:, i % BUFS, :]).then_inc(s_out[i % BUFS], 16)
                    if i + BUFS < TILES:
                        sp.wait_ge(s_out[i % BUFS], 16 * (i // BUFS + 1))
                        load(i + BUFS)
                for b in range(BUFS):
                    sp.wait_ge(s_out[b], 16 * ((TILES - 1 - b) // BUFS + 1))

            @block.tensor
            def _(pe):
                w = [wait_weights(k, pe, 14 + h) for h in range(2)]
                for i in range(TILES):
                    for h in range(2):
                        bank = ring.fill(pe)
                        for c in range(KC):
                            mm = pe.matmul(bank[:, :], z[c][:, i * P:(i + 1) * P], w[h][:, c, :], start=(c == 0), stop=(c == KC - 1))
                        mm.then_inc(ring.full, 1)

            @block.vector
            def _(dve):
                for i in range(TILES):
                    dve.wait_ge(s_x[i % BUFS], 16 * (i // BUFS + 1))
                    for h in range(2):
                        c = slice(h * WCH, (h + 1) * WCH)
                        bank = ring.read(dve)
                        dve.tensor_tensor(y[:, h, :], bank[:, :], k.gate[:, int(i >= TC), c], ALU.mult).then_inc(ring.free, 1)
                        dve.wait_ge(ring.free, ring.got)
                        ins = dve.tensor_tensor(x[:, i % BUFS, c], x[:, i % BUFS, c], y[:, h, :], ALU.add)
                    ins.then_inc(s_new, 1)


CONST_SHAPES = {n: v.shape for n, v in constants().items()}
INPUTS = ("x", "c", "ctx", "c_ctx", "norm_w", "ada_w", "ada_b", "w_in", "w_out", "na_q_gain", "na_k_gain", "na_rpb",
          "hy_conv_w", "hy_conv_b", "hy_w1", "hy_b1", "hy_w2", "hy_b2", "hy_w3", "hy_sin_freq", "hy_skip", "ret_log_rate")


def program(nc, a, out, scratch, depth=DEPTH):
    with ExitStack() as ctx:
        k = Build(nc, a, out, ctx)
        ctx.enter_context(nc.allow_non_contiguous_dma(reason="vectors of a layer go down the partitions"))
        k.spectra, k.context = scratch
        sb = lambda name, shape: sbuf(ctx, nc, name, shape)
        k.ident = sb("ident", [P, P])
        k.wbuf = [sb(f"weights{i}", [P, KC, WCH]) for i in range(2)]
        k.shift, k.scale = sb("mod_shift", [P, KC, 2]), sb("mod_scale", [P, KC, 2])
        k.gate = sb("mod_gate", [P, 2, D])
        k.inv_sum = sb("inv_sum", [P, 2, 2, HW])
        k.skip = sb("hy_skip_rows", [P, 2, HW])
        s_start = ctx.enter_context(nc.semaphore("start_copied"))
        k.w_here = [k.sem(f"weights{i}_here") for i in range(2)]

        with nc.Block() as block:
            @block.sync
            def _(sp):
                sp.dma_start(k.ident[:, :], a["ident"]).then_inc(s_start, 16)
                sp.dma_start(out[0], a["x"][0]).then_inc(s_start, 16)
                sp.dma_start(k.context, a["ctx"][0]).then_inc(s_start, 16)
                sp.wait_ge(s_start, 48)

        with nc.Fori(0, depth) as layer:
            k.layer = layer
            with ExitStack() as held:
                sb = lambda name, shape: sbuf(held, nc, name, shape)
                weights_stage(k)
                k.hxT = sb("hxT", [P, KC, TOK])
                norm_stage(k)
                k.z_hy = sb("z_hyena", [P, 2, TOK])
                with nc.sbuf_tensor("context_hyena_columns", [P, TC, 4 * HW], F32) as k.uc:
                    hyena_stage(k)
                    context_hyena_stage(k)
                k.z_na = sb("z_attention", [P, 4, TOK])
                k.z_re = sb("z_retention", [P, 2, TOK])
                attention_stage(k)
                retention_stage(k)
                output_stage(k)
            with nc.Block() as block:
                @block.vector
                def _(dve):
                    for s in k.sems:
                        dve.sem_clear(s)


def build(nc, arrays):
    a = {n: nc.dram_tensor("in_" + n, v.shape, F32, kind="ExternalInput").ap() for n, v in arrays.items()}
    out = nc.dram_tensor("out", (1, L, D), F32, kind="ExternalOutput").ap()
    spectra = nc.dram_tensor("filter_spectra", (2, P, 22, HW), F32, kind="Internal").ap()
    context = nc.dram_tensor("context_stream", (LC, D), F32, kind="Internal").ap()
    return a, out, (spectra, context)


def laid_out(inputs):
    arrays = {n: np.ascontiguousarray(inputs[n]) for n in INPUTS}
    arrays["na_rpb"] = np.ascontiguousarray(np.pad(arrays["na_rpb"], ((0, 0), (0, 0), (1, 1), (GRID + 1 - KW, GRID - KW)))[..., ::-1])
    arrays.update(constants())
    return arrays


def kernel(**inputs):
    import concourse.bacc as bacc
    from concourse.bass_utils import run_bass_kernel_spmd

    arrays = laid_out(inputs)
    nc = bacc.Bacc("TRN2", target_bir_lowering=False, num_devices=1)
    a, out, scratch = build(nc, arrays)
    program(nc, a, out, scratch)
    r = run_bass_kernel_spmd(nc, [{"in_" + n: v for n, v in arrays.items()}], core_ids=[0])
    return r.results[0]["out"]
```

```python
from contextlib import ExitStack
import math

import numpy as np

import concourse.bass as bass
from concourse import mybir

F32 = mybir.dt.float32
ALU = mybir.AluOpType
ACT = mybir.ActivationFunctionType
AX = mybir.AxisListType

P = 128
D = 1024
KC = D // P
L = 1024
LC = 256
DEPTH = 2
TC = LC // P
TILES = TC + L // P
TOK = LC + L
GRID = 64
NA_HEADS, HD = 8, 64
NA_W = NA_HEADS * HD
KH, KW = 8, 16
HW = 256
FFN = 64
EMB = 17
RH = 4
RW = RH * HD
IN_W = 4 * (NA_W + HW + RW)
EPS = 1e-6
NEG = -1e30
NF = 2 * L
T2 = 16
T1 = L // T2
NR = L // P
GROUPS = 16
HT = 8
WCH = 512
HY0 = 4 * NA_W
RE0 = HY0 + 4 * HW
MAGIC = 1.5 * 2.0 ** 23
TWO_PI_HI = 6.28125
TWO_PI_LO = 2.0 * math.pi - TWO_PI_HI
PI_F = 3.1415925


def constants():
    c = {}
    c["ident"] = np.eye(P)
    t1 = np.arange(T1)[:, None]
    slot = np.arange(64)
    time = np.zeros((T1, 64, 2))
    ang = 2 * np.pi * t1 * slot / 128
    time[:, :, 0] = np.cos(ang)
    time[:, :, 1] = -np.sin(ang)
    time[:, 0, 0] = 1.0
    time[:, 0, 1] = (-1.0) ** t1[:, 0]
    time = time.reshape(T1, P)
    both = np.zeros((P, 2, P))
    for b in range(2):
        both[b::2, b] = time
    c["dft_time"] = both
    c["idft_time"] = both.transpose(2, 1, 0)
    fine = np.zeros((P, 2, GROUPS, 64))
    inv = np.zeros((P, HT, 2, P))
    t2 = np.arange(T2)
    for g in range(GROUPS):
        for s in range(4):
            sl = 4 * g + s
            for f2 in range(16):
                col = s * 16 + f2
                irow = 64 * (g % 2) + col
                w = 2.0 / NF
                if sl > 0:
                    th = 2 * np.pi * t2 * (sl + 128 * f2) / NF
                    r0, r1 = s * 32 + t2, s * 32 + 16 + t2
                    fine[r0, 0, g, col], fine[r1, 0, g, col] = np.cos(th), np.sin(th)
                    fine[r0, 1, g, col], fine[r1, 1, g, col] = -np.sin(th), np.cos(th)
                    inv[irow, g // 2, 0, r0], inv[irow, g // 2, 0, r1] = w * np.cos(th), w * np.sin(th)
                    inv[irow, g // 2, 1, r0], inv[irow, g // 2, 1, r1] = -w * np.sin(th), w * np.cos(th)
                else:
                    f = 128 * f2 if f2 < 8 else 64 + 128 * (f2 - 8)
                    r = t2 if f2 < 8 else 16 + t2
                    th = 2 * np.pi * t2 * f / NF
                    if f2 == 0:
                        fine[r, 0, g, col], fine[r, 1, g, col] = 1.0, np.cos(np.pi * t2)
                        inv[irow, 0, 0, r], inv[irow, 0, 1, r] = 1.0 / NF, np.cos(np.pi * t2) / NF
                    else:
                        fine[r, 0, g, col], fine[r, 1, g, col] = np.cos(th), -np.sin(th)
                        inv[irow, 0, 0, r], inv[irow, 0, 1, r] = w * np.cos(th), -w * np.sin(th)
    c["dft_fine"] = fine
    c["idft_fine"] = inv
    special = np.zeros((P, 2, 64))
    special[:, 0] = fine[:, 0, 0]
    special[:, 0, 0] = fine[:, 1, 0, 0]
    special[:, 1] = fine[:, 1, 0]
    special[:, 1, 0] = 0.0
    c["fine_special"] = special
    t = np.arange(LC)
    f = np.arange(LC)
    th = 2 * np.pi * np.outer(t, f) / (2 * LC)
    re, im = np.cos(th), -np.sin(th)
    im[:, 0] = np.cos(np.pi * t)
    h, g = re.copy(), im.copy()
    h[:, 0] = im[:, 0]
    g[:, 0] = 0.0
    rows = lambda m: m.reshape(2, P, -1).transpose(1, 0, 2)
    c["cdft"] = np.stack([rows(re), rows(im)], 1)
    c["cdft_special"] = np.stack([rows(h)[:, :, :P], rows(g)[:, :, :P]], 1)
    w = np.full(LC, 2.0 / (2 * LC))
    w[0] = 1.0 / (2 * LC)
    c["cidft"] = np.stack([rows(re.T * w[:, None]), rows(im.T * w[:, None])], 1)
    px = (NR * np.arange(P)[None] + np.arange(NR)[:, None]).ravel()
    emb, dec = [], []
    for n, pos in ((L, px), (LC, np.arange(LC))):
        tn = np.linspace(0.0, 1.0, n).astype(np.float32).astype(np.float64)[pos][:, None]
        om = 2 * np.pi * pos[:, None] / n
        bands = np.linspace(1e-4, 7.0, 8).astype(np.float32).astype(np.float64)[None]
        emb.append(np.concatenate([tn, np.cos(bands * om), -np.sin(bands * om)], 1))
        deltas = np.abs(np.linspace(math.log(1e-2) / 1.5, math.log(1e-2) / 0.3, HW))
        dec.append(np.exp(-tn * deltas))
    c["emb"] = np.concatenate(emb, 0).T
    c["decay"] = np.concatenate(dec, 0).reshape(TILES, P, HW).transpose(1, 0, 2)
    tok = np.arange(L)
    fr = 10000.0 ** (-np.arange(16) / 16.0)
    ang = np.stack([tok // GRID, tok % GRID], 1)[:, :, None] * fr
    rope = np.zeros((TOK, 2, 2, 16))
    rope[:LC, 0] = 1.0
    rope[LC:, 0] = np.cos(ang)
    rope[LC:, 1] = np.sin(ang)
    c["rope"] = rope.reshape(TILES, P, 64).transpose(1, 0, 2)
    l, j = np.arange(P)[:, None], np.arange(P)[None]
    c["dist"] = np.stack([np.maximum(j - l, 0), np.maximum(l - j, 0), (j >= l) * 0.125, (l >= j) * 0.125], 1)
    c["age"] = np.broadcast_to(np.stack([np.arange(P) + 1, P - np.arange(P)])[None], (P, 2, P))
    c["rest"] = np.stack([P - 1 - np.arange(P), np.arange(P)], 1)[:, :, None].repeat(RH, 2)
    cq, ck = np.arange(GRID)[:, None], np.arange(GRID)[None]
    cs = np.clip(cq - KW // 2, 0, GRID - KW)
    ok = (ck >= cs) & (ck < cs + KW)
    c["colmask"] = np.concatenate([np.where(ok, 0.0, NEG)] * 2, 0)
    return {k: np.ascontiguousarray(v, np.float32) for k, v in c.items()}


class Ring:

    def __init__(self, name, banks, sem):
        self.banks, self.full, self.free = banks, sem(name + "_full"), sem(name + "_free")
        self.put, self.got = 0, 0

    def fill(self, pe):
        if self.put >= len(self.banks):
            pe.wait_ge(self.free, self.put - len(self.banks) + 1)
        self.put += 1
        return self.banks[(self.put - 1) % len(self.banks)]

    def read(self, eng):
        eng.wait_ge(self.full, self.got + 1)
        self.got += 1
        return self.banks[(self.got - 1) % len(self.banks)]


class Chain:

    def __init__(self, sem, eng=None):
        self.sem, self.n, self.eng = sem, 0, eng

    def __call__(self, ins):
        self.n += 1
        ins.then_inc(self.sem, 1)
        self.eng.wait_ge(self.sem, self.n)


class Build:

    def __init__(self, nc, a, out, ctx):
        self.nc, self.a, self.out, self.ctx = nc, a, out, ctx
        self.sems = []
        self.all_psum = ctx.enter_context(nc.psum_tensor("psum", [P, 8 * 512], F32))
        self.psum = [self.all_psum[:, i * 512:(i + 1) * 512] for i in range(8)]

    def sem(self, name):
        s = self.ctx.enter_context(self.nc.semaphore(name))
        self.sems.append(s)
        return s

    def of_layer(self, ap):
        return ap[bass.ds(self.layer, 1)]


def R32(ap):
    return ap.bitcast(mybir.dt.float32r)


def sbuf(ctx, nc, name, shape):
    return ctx.enter_context(nc.sbuf_tensor(name, shape, F32))


def weight_chunk(k, n):
    def cols(w, c0, width=WCH, at=0):
        v = k.of_layer(w)[:, :, c0:c0 + width].rearrange("a (k p) n -> p (a k) n", p=P)
        return (slice(at, at + width), v)

    a = k.a
    if n < 6:
        return [cols(a["ada_w"], n * WCH)]
    n -= 6
    if n < 2:
        return [cols(a["w_in"], HY0 + n * WCH)]
    n -= 2
    if n < 4:
        return [cols(a["w_in"], m * NA_W + n * P, P, m * P) for m in range(4)]
    n -= 4
    if n < 2:
        return [cols(a["w_in"], RE0 + n * WCH)]
    return [cols(a["w_out"], (n - 2) * WCH)]


def load_weights(k, eng, n):
    for where, view in weight_chunk(k, n):
        eng.dma_start(k.wbuf[n % 2][:, :, where], view).then_inc(k.w_here[n % 2], 16)


def wait_weights(k, eng, n):
    parts = sum(4 if 8 <= m < 12 else 1 for m in range(n % 2, n + 1, 2))
    eng.wait_ge(k.w_here[n % 2], 16 * parts)
    return k.wbuf[n % 2]


def weights_stage(k):
    nc, a = k.nc, k.a
    with ExitStack() as mem:
        sb = lambda name, shape: sbuf(mem, nc, name, shape)
        time = sb("s1_time", [P, 2, P])
        fine = sb("s1_fine", [P, 2, GROUPS, 64])
        special = sb("s1_special", [P, 2, 64])
        cdft = sb("s1_cdft", [P, 2, 2, LC])
        cspecial = sb("s1_cspecial", [P, 2, 2, P])
        emb = sb("s1_emb", [EMB, TOK])
        decay = sb("s1_decay", [P, TILES, HW])
        w1, w2 = sb("s1_w1", [EMB, FFN]), sb("s1_w2", [FFN, FFN])
        w3 = sb("s1_w3", [FFN, 4 * HW])
        vec = sb("s1_vec", [FFN, 4])
        arg, turns, hid = sb("s1_arg", [FFN, TOK]), sb("s1_turns", [FFN, TOK]), sb("s1_hid", [FFN, TOK])
        taps = sb("s1_taps", [P, TILES, 2, HW])
        even, odd = sb("s1_even", [P, TILES, HW]), sb("s1_odd", [P, TILES, HW])
        mag = taps[:, :, 0, :]
        ones = sb("s1_ones", [P, P])
        part1, part2 = sb("s1_part1", [P, T2, HW]), sb("s1_part2", [P, GROUPS, HW])
        spec = sb("s1_spec", [P, 22, HW])
        cond = sb("s1_cond", [P, KC, 2])
        condb = sb("s1_condb", [P, 2, KC, P])
        gate_b = sb("s1_gate_b", [P, D])
        ada_b = sb("s1_ada_b", [P, 2 * KC])
        normw = sb("s1_normw", [P, KC])

        s_tab, s_mod, s_w = k.sem("s1_tables_here"), k.sem("s1_mod_inputs_here"), k.sem("s1_mlp_weights_here")
        ra, rv = Ring("s1_act", k.psum[0:4], k.sem), Ring("s1_dve", k.psum[4:8], k.sem)
        s_arg, s_sin = k.sem("s1_arg"), k.sem("s1_sin")
        s_step, s_taps = k.sem("s1_dve_step"), k.sem("s1_taps_ready")
        s_shuf, s_spill = k.sem("s1_shuffled"), k.sem("s1_spilled")
        s_silu, s_condb = k.sem("s1_silu"), k.sem("s1_cond_spread")
        base = [0, 19, 36, 55, 72]
        used = [4, 8, 21, 22, 36, 38]

        with nc.Block() as block:
            @block.tensor
            def _(pe):
                def mlp(w, x):
                    for c0 in range(0, TOK, 512):
                        n = min(512, TOK - c0)
                        bank = rv.fill(pe)
                        pe.matmul(bank[0:FFN, 0:n], w[:, :], x[:, c0:c0 + n], start=True, stop=True).then_inc(rv.full, 1)

                def modulation(n):
                    w = wait_weights(k, pe, n)
                    if n < 4:
                        bank = rv.fill(pe)
                        for m in range(4):
                            for kc in range(KC):
                                mm = pe.matmul(bank[:, 2 * m:2 * m + 2], w[:, kc, m * P:(m + 1) * P], cond[:, kc, :],
                                               start=(kc == 0), stop=(kc == KC - 1))
                        mm.then_inc(rv.full, 1)
                    else:
                        pe.wait_ge(s_condb, 2)
                        for c in range(2):
                            bank = rv.fill(pe)
                            for kc in range(KC):
                                mm = pe.matmul(bank[:, :], condb[:, c, kc, :], w[:, kc, :], start=(kc == 0), stop=(kc == KC - 1))
                            mm.then_inc(rv.full, 1)
                    assert rv.put == used[n]

                pe.wait_ge(s_w, 7 * 16)
                mlp(w1, emb)
                pe.wait_ge(s_silu, 1)
                modulation(0)
                pe.wait_ge(s_sin, 1)
                mlp(w2, hid)
                modulation(1)
                pe.wait_ge(s_sin, 2)
                pe.wait_ge(s_tab, 6 * 16)
                for o in range(2):
                    for i in range(TILES):
                        bank = rv.fill(pe)
                        pe.matmul(bank[:, :], hid[:, i * P:(i + 1) * P], w3[:, o * 512:(o + 1) * 512],
                                  start=True, stop=True).then_inc(rv.full, 1)
                    for part, x in enumerate((even, odd)):
                        n = 2 * o + part
                        pe.wait_ge(s_taps, o + 1)
                        if part == 0:
                            for tiles in (range(0, 8), range(8, 10)):
                                bank = rv.fill(pe)
                                for i in tiles:
                                    mm = pe.matmul(bank[:, 0:HW], ones[:, :], mag[:, i, :], start=(i == tiles[0]), stop=(i == tiles[-1]))
                                mm.then_inc(rv.full, 1)
                        assert ra.put == base[n]
                        for b in range(2):
                            for q in range(4):
                                bank = ra.fill(pe)
                                pe.matmul(bank[:, :], time[:, b, :], x[:, 2 * q:2 * q + 2, :],
                                          start=True, stop=True).then_inc(ra.full, 1)
                        bank = ra.fill(pe)
                        for T in range(2):
                            for kk in range(2):
                                table = cspecial[:, 1, kk, :] if part and T == 0 else cdft[:, part, kk, T * P:(T + 1) * P]
                                mm = pe.matmul(bank[:, T * HW:(T + 1) * HW], table, x[:, 8 + kk, :], start=(kk == 0), stop=(kk == 1))
                        mm.then_inc(ra.full, 1)
                        if part == 0:
                            bank = ra.fill(pe)
                            for kk in range(2):
                                mm = pe.matmul(bank[:, 0:HW], cspecial[:, 0, kk, :], x[:, 8 + kk, :], start=(kk == 0), stop=(kk == 1))
                            mm.then_inc(ra.full, 1)
                        modulation(n + 2)
                        pe.wait_ge(s_shuf, 16 * GROUPS * (n + 1))
                        for T in range(HT):
                            bank = ra.fill(pe)
                            for h in range(2):
                                g = 2 * T + h
                                lhs = special[:, 1, :] if part and g == 0 else fine[:, part, g, :]
                                mm = pe.matmul(bank[64 * h:64 * h + 64, 0:HW], lhs, part2[:, g, :], start=True, stop=True)
                            mm.then_inc(ra.full, 1)
                        if part == 0:
                            bank = ra.fill(pe)
                            pe.matmul(bank[0:64, 0:HW], special[:, 0, :], part2[:, 0, :], start=True, stop=True)
                            pe.matmul(bank[64:128, 0:HW], fine[:, 0, 1, :], part2[:, 1, :], start=True, stop=True).then_inc(ra.full, 1)

            @block.sync
            def _(sp):
                this = k.of_layer
                load_weights(k, sp, 0)
                sp.dma_start(w1[:, :], this(a["hy_w1"]).rearrange("a k n -> (a k) n")).then_inc(s_w, 16)
                sp.dma_start(emb[:, :], a["emb"]).then_inc(s_w, 16)
                sp.dma_start(w2[:, :], this(a["hy_w2"]).rearrange("a k n -> (a k) n")).then_inc(s_w, 16)
                sp.dma_start(vec[:, 0:1], this(a["hy_b1"]).rearrange("a n -> n a")).then_inc(s_w, 16)
                sp.dma_start(vec[:, 1:2], this(a["hy_b2"]).rearrange("a n -> n a")).then_inc(s_w, 16)
                sp.dma_start(vec[:, 2:4], this(a["hy_sin_freq"]).rearrange("a f n -> n (a f)")).then_inc(s_w, 16)
                sp.dma_start(w3[:, :], this(a["hy_w3"]).rearrange("a k n -> (a k) n")).then_inc(s_w, 16)
                sp.dma_start(cond[:, :, 0], a["c_ctx"].rearrange("(k p) -> p k", p=P)).then_inc(s_mod, 16)
                sp.dma_start(cond[:, :, 1], a["c"].rearrange("a (k p) -> p (a k)", p=P)).then_inc(s_mod, 16)
                sp.dma_start(ada_b[:, :], this(a["ada_b"])[:, 0:2 * D].rearrange("a (k p) -> p (a k)", p=P)).then_inc(s_mod, 16)
                sp.dma_start(normw[:, :], this(a["norm_w"]).rearrange("a (k p) -> p (a k)", p=P)).then_inc(s_mod, 16)
                sp.dma_start(gate_b[:, :], this(a["ada_b"])[:, 2 * D:3 * D].to_broadcast((P, D))).then_inc(s_mod, 16)
                sp.dma_start(decay[:, :, :], a["decay"]).then_inc(s_tab, 16)
                sp.dma_start(time[:, :, :], a["dft_time"]).then_inc(s_tab, 16)
                sp.dma_start(fine[:, :, :, :], a["dft_fine"]).then_inc(s_tab, 16)
                sp.dma_start(special[:, :, :], a["fine_special"]).then_inc(s_tab, 16)
                sp.dma_start(cdft[:, :, :, :], a["cdft"]).then_inc(s_tab, 16)
                sp.dma_start(cspecial[:, :, :, :], a["cdft_special"]).then_inc(s_tab, 16)
                load_weights(k, sp, 1)
                for m in (2, 3):
                    sp.wait_ge(rv.full, used[m - 2])
                    load_weights(k, sp, m)
                for n in range(4):
                    sp.wait_ge(ra.free, base[n] + 8)
                    if n >= 1:
                        sp.wait_ge(ra.full, base[n])
                    for g in range(GROUPS):
                        sp.dma_start(part2[:, g, :], part1[8 * g:8 * g + 8, :, :]).then_inc(s_shuf, 16)
                    sp.wait_ge(rv.full, used[n + 2])
                    load_weights(k, sp, n + 4)
                    if n % 2 == 1:
                        sp.wait_ge(ra.free, base[n + 1])
                        sp.dma_start(k.spectra[n // 2], spec[:, :, :]).then_inc(s_spill, 16)
                sp.wait_ge(s_spill, 32)

            @block.scalar
            def _(act):
                act.wait_ge(s_mod, 5 * 16)
                act.activation(cond[:, :, :], cond[:, :, :], ACT.Silu).then_inc(s_silu, 1)
                for n in range(2):
                    act.wait_ge(s_arg, n + 1)
                    if n == 1:
                        act.wait_ge(rv.full, 7)
                    act.activation(hid[:, :], arg[:, :], ACT.Sin).then_inc(s_sin, 1)
                for n in range(4):
                    part = n % 2
                    if n >= 1:
                        act.wait_ge(s_shuf, 16 * GROUPS * n)
                    for b in range(2):
                        for q in range(4):
                            bank = ra.read(act)
                            dst = part1[:, 8 * b + 2 * q:8 * b + 2 * q + 2, :]
                            act.activation(dst, bank[:, :].rearrange("p (a c) -> p a c", a=2), ACT.Copy).then_inc(ra.free, 1)
                    if n == 2:
                        act.wait_ge(s_spill, 16)
                    first = (17, 19)[part]
                    act.activation(spec[:, first:first + 2, :], ra.read(act)[:, :].rearrange("p (a c) -> p a c", a=2), ACT.Copy).then_inc(ra.free, 1)
                    if part == 0:
                        act.activation(spec[:, 21, :], ra.read(act)[:, 0:HW], ACT.Copy).then_inc(ra.free, 1)
                    for T in range(HT):
                        act.activation(spec[:, 8 * part + T, :], ra.read(act)[:, 0:HW], ACT.Copy).then_inc(ra.free, 1)
                    if part == 0:
                        act.activation(spec[:, 16, :], ra.read(act)[:, 0:HW], ACT.Copy).then_inc(ra.free, 1)

            @block.vector
            def _(dve):
                step = Chain(s_step, dve)

                def sin_argument(n):
                    for c0 in range(0, TOK, 512):
                        w = min(512, TOK - c0)
                        bank = rv.read(dve)
                        dve.tensor_scalar(arg[:, c0:c0 + w], bank[0:FFN, 0:w], vec[:, n:n + 1], vec[:, 2 + n:3 + n],
                                          ALU.add, ALU.mult).then_inc(rv.free, 1)
                    dve.wait_ge(rv.free, rv.got)
                    step(dve.tensor_scalar(turns[:, :], arg[:, :], 1.0 / (2 * math.pi), MAGIC, ALU.mult, ALU.add))
                    step(dve.tensor_scalar(turns[:, :], turns[:, :], MAGIC, None, ALU.subtract))
                    step(dve.scalar_tensor_tensor(out=arg[:, :], in0=turns[:, :], scalar=-TWO_PI_HI, in1=arg[:, :], op0=ALU.mult, op1=ALU.add))
                    step(dve.scalar_tensor_tensor(out=arg[:, :], in0=turns[:, :], scalar=-TWO_PI_LO, in1=arg[:, :], op0=ALU.mult, op1=ALU.add))
                    dve.tensor_scalar(arg[:, :], arg[:, :], PI_F, -PI_F, ALU.min, ALU.max).then_inc(s_arg, 1)

                def modulation(n):
                    if n < 4:
                        dst = (k.shift if n < 2 else k.scale)[:, 4 * (n % 2):4 * (n % 2) + 4, :]
                        both = lambda x, c0: x[:, c0:c0 + 4].unsqueeze(2).to_broadcast((P, 4, 2))
                        bank = rv.read(dve)
                        dve.tensor_tensor(dst, bank[:, 0:8].rearrange("p (m c) -> p m c", c=2), both(ada_b, 4 * n), ALU.add).then_inc(rv.free, 1)
                        if n >= 2:
                            dve.wait_ge(rv.free, rv.got)
                            step(dve.scalar_tensor_tensor(out=dst, in0=dst, scalar=1.0, in1=both(normw, 4 * (n - 2)), op0=ALU.add, op1=ALU.mult))
                    else:
                        c0 = (n - 4) * 512
                        for c in range(2):
                            bank = rv.read(dve)
                            dve.tensor_tensor(k.gate[:, c, c0:c0 + 512], bank[:, :], gate_b[:, c0:c0 + 512], ALU.add).then_inc(rv.free, 1)

                dve.memset(ones[:, :], 1.0).then_inc(s_step, 1)
                step.n += 1
                dve.wait_ge(s_w, 7 * 16)
                dve.wait_ge(s_mod, 5 * 16)
                sin_argument(0)
                dve.wait_ge(s_silu, 1)
                for c in range(2):
                    dve.tensor_copy(condb[:, c, :, :], cond[:, :, c].unsqueeze(2).to_broadcast((P, KC, P))).then_inc(s_condb, 1)
                modulation(0)
                dve.wait_ge(s_sin, 1)
                sin_argument(1)
                modulation(1)
                dve.wait_ge(s_tab, 6 * 16)
                for o in range(2):
                    for i in range(TILES):
                        bank = rv.read(dve)
                        dve.tensor_tensor(taps[:, i, :, :], bank[:, :].rearrange("p (w c) -> p w c", w=2),
                                          decay[:, i, :].unsqueeze(1).to_broadcast((P, 2, HW)), ALU.mult).then_inc(rv.free, 1)
                    dve.wait_ge(rv.free, rv.got)
                    step(dve.memset(taps[0:1, 0, 1, :], 0.0))
                    step(dve.memset(taps[0:1, 8, 1, :], 0.0))
                    if o == 1:
                        dve.wait_ge(ra.full, base[2])
                    fwd, bwd = taps[:, :, 0, :], taps[:, :, 1, :]
                    step(dve.tensor_tensor(even[:, :, :], fwd, bwd, ALU.add))
                    step(dve.tensor_tensor(odd[:, :, :], fwd, bwd, ALU.subtract))
                    for x in (fwd, bwd):
                        step(dve.scalar_tensor_tensor(out=x, in0=x, scalar=-1.0, in1=x, op0=ALU.mult, op1=ALU.max))
                    dve.tensor_tensor(mag, fwd, bwd, ALU.add).then_inc(s_taps, 1)
                    for which in range(2):
                        bank = rv.read(dve)
                        dve.reciprocal(k.inv_sum[:, o, which, :], bank[:, 0:HW]).then_inc(rv.free, 1)
                    modulation(2 + 2 * o)
                    modulation(3 + 2 * o)


def stream_tile(k, i):
    return k.context[i * P:(i + 1) * P, :] if i < TC else k.out[0, (i - TC) * P:(i - TC + 1) * P, :]


def norm_stage(k):
    nc = k.nc
    BUFS = 3
    with ExitStack() as mem:
        x = sbuf(mem, nc, "s2_x", [P, BUFS, D])
        square = sbuf(mem, nc, "s2_square", [P, D])
        rms = sbuf(mem, nc, "s2_rms", [P, 2, TILES])
        inv = sbuf(mem, nc, "s2_inv", [P, TILES])
        eps = sbuf(mem, nc, "s2_eps", [P, 1])
        tmp = sbuf(mem, nc, "s2_scaled", [P, 2, 512])
        s_x = [k.sem(f"s2_x{b}_here") for b in range(BUFS)]
        s_sum, s_rms, s_inv, s_scaled = k.sem("s2_squares"), k.sem("s2_rms"), k.sem("s2_inverse"), k.sem("s2_x_scaled")
        s_eps, s_step = k.sem("s2_eps"), k.sem("s2_dve_step")
        ra, rv = Ring("s2_act", k.psum[0:4], k.sem), Ring("s2_dve", k.psum[4:8], k.sem)
        with nc.Block() as block:
            @block.sync
            def _(sp):
                for i in range(TILES):
                    if i >= BUFS:
                        sp.wait_ge(ra.full, i - BUFS + 1)
                    sp.dma_start(x[:, i % BUFS, :], stream_tile(k, i)).then_inc(s_x[i % BUFS], 16)

            @block.scalar
            def _(act):
                def transposed(i):
                    bank = ra.read(act)
                    c = int(i >= TC)
                    for m in range(4):
                        ins = act.activation(k.hxT[:, 4 + m, i * P:(i + 1) * P], bank[:, m * P:(m + 1) * P], ACT.Identity,
                                             bias=k.shift[:, 4 + m, c:c + 1], scale=k.scale[:, 4 + m, c:c + 1])
                    ins.then_inc(ra.free, 1)

                act.wait_ge(s_eps, 1)
                for i in range(TILES):
                    act.wait_ge(s_x[i % BUFS], 16 * (i // BUFS + 1))
                    if i >= 1:
                        act.wait_ge(s_sum, i)
                    act.activation(square[:, :], x[:, i % BUFS, :], ACT.Square, accum_out=rms[:, 0, i:i + 1]).then_inc(s_sum, 1)
                    act.wait_ge(s_sum, i + 1)
                    act.activation(rms[:, 1, i:i + 1], rms[:, 0, i:i + 1], ACT.Sqrt, bias=eps[:, 0:1], scale=1.0 / D).then_inc(s_rms, 1)
                    if i >= 1:
                        transposed(i - 1)
                transposed(TILES - 1)

            @block.vector
            def _(dve):
                dve.memset(eps[:, :], EPS).then_inc(s_eps, 1)
                step = Chain(s_step, dve)

                def transposed(i):
                    bank = rv.read(dve)
                    c = int(i >= TC)
                    per = lambda v: v[:, 0:4, c].unsqueeze(2).to_broadcast((P, 4, P))
                    four = lambda v: v.rearrange("p (m t) -> p m t", m=4)
                    dve.tensor_tensor(four(tmp[:, i % 2, :]), four(bank[:, :]), per(k.scale), ALU.mult).then_inc(rv.free, 1)
                    dve.wait_ge(rv.free, rv.got)
                    dve.tensor_tensor(k.hxT[:, 0:4, i * P:(i + 1) * P], four(tmp[:, i % 2, :]), per(k.shift), ALU.add).then_inc(s_step, 1)

                for i in range(TILES):
                    dve.wait_ge(s_rms, i + 1)
                    dve.reciprocal(inv[:, i:i + 1], rms[:, 1, i:i + 1]).then_inc(s_inv, 1)
                    dve.wait_ge(s_inv, i + 1)
                    dve.tensor_scalar(x[:, i % BUFS, :], x[:, i % BUFS, :], inv[:, i:i + 1], None, ALU.mult).then_inc(s_scaled, 1)
                    if i >= 1:
                        transposed(i - 1)
                transposed(TILES - 1)

            @block.tensor
            def _(pe):
                for i in range(TILES):
                    pe.wait_ge(s_scaled, i + 1)
                    for half, ring in enumerate((rv, ra)):
                        bank = ring.fill(pe)
                        for m in range(4):
                            c0 = (4 * half + m) * P
                            ins = pe.transpose(bank[:, m * P:(m + 1) * P], x[:, i % BUFS, c0:c0 + P], k.ident[:, :])
                        ins.then_inc(ring.full, 1)


def hyena_stage(k):
    nc, a_in = k.nc, k.a
    with ExitStack() as mem:
        sb = lambda name, shape: sbuf(mem, nc, name, shape)
        time, itime = sb("s3_time", [P, 2, P]), sb("s3_itime", [P, 2, P])
        fine, ifine = sb("s3_fine", [P, 2, GROUPS, 64]), sb("s3_ifine", [P, HT, 2, P])
        aux = sb("s3_aux", [P, 17, HW])
        tmp = sb("s3_tmp", [P, 4, HW])
        v = sb("s3_v", [P, NR, 3 * HW])
        gh = sb("s3_gate", [P, NR, HW])
        uc = sb("s3_context_columns", [P, TC, 4 * HW])
        parts = sb("s3_parts", [P, 2, T2, HW])
        part1, part2 = parts[:, 0], parts[:, 1]
        raw = parts[:, :, :, :].rearrange("p n t c -> p (n t c)")[:, 0:(NR + 2) * 3 * HW].rearrange("p (r c) -> p r c", r=NR + 2)
        convw = aux[:, 0:9, :].rearrange("p (j g) c -> p j (g c)", j=3)
        convb = tmp[:, 0:3, :].rearrange("p g c -> p (g c)")

        ra, rv = Ring("s3_act", k.psum[0:4], k.sem), Ring("s3_dve", k.psum[4:8], k.sem)
        s_tab, s_conv, s_zero, s_shift = k.sem("s3_tables_here"), k.sem("s3_conv_weights_here"), k.sem("s3_zeroed"), [k.sem(f"s3_shifted{n}") for n in range(2)]
        s_scaled, s_step, s_ready = k.sem("s3_neighbours_scaled"), k.sem("s3_dve_step"), k.sem("s3_conv_done")
        s_shuf, s_spec, s_prod = k.sem("s3_shuffled"), k.sem("s3_spectrum_here"), k.sem("s3_products")
        s_spill = k.sem("s3_context_columns_stored")
        s_skip, s_y = k.sem("s3_skip_applied"), k.sem("s3_y_ready")
        PROJECTIONS = [(n, i) for n in (6, 7) for i in range(NR)] + [(n, NR + i) for n in (6, 7) for i in range(TC)]
        A = [20, 36]
        with nc.Block() as block:
            @block.tensor
            def _(pe):
                for n, i in PROJECTIONS:
                    w = wait_weights(k, pe, n)
                    bank = ra.fill(pe)
                    for kc in range(KC):
                        lhs = k.hxT[:, kc, LC + i:TOK:NR] if i < NR else k.hxT[:, kc, (i - NR) * P:(i - NR + 1) * P]
                        mm = pe.matmul(bank[:, :], lhs, w[:, kc, :], start=(kc == 0), stop=(kc == KC - 1))
                    mm.then_inc(ra.full, 1)
                pe.wait_ge(s_tab, 4 * 16)
                for o in range(2):
                    pe.wait_ge(s_ready if o == 0 else s_y, 1)
                    for b in range(2):
                        for q in range(4):
                            bank = ra.fill(pe)
                            pe.matmul(bank[:, :], time[:, b, :], v[:, 2 * q:2 * q + 2, 0:HW],
                                      start=True, stop=True).then_inc(ra.full, 1)
                    pe.wait_ge(s_shuf, 16 * GROUPS * (2 * o + 1))
                    for T in range(HT):
                        bank = rv.fill(pe)
                        for h in range(2):
                            for ri in range(2):
                                mm = pe.matmul(bank[64 * h:64 * h + 64, ri * HW:(ri + 1) * HW], fine[:, ri, 2 * T + h, :],
                                               part2[:, 2 * T + h, :], start=True, stop=True)
                        mm.then_inc(rv.full, 1)
                    for T in range(0, HT, 2):
                        pe.wait_ge(s_prod, HT * o + T + 2)
                        banks = [ra.fill(pe), ra.fill(pe)]
                        for t in range(2):
                            for ri in range(2):
                                for h in range(2):
                                    y = part1[64 * h:64 * h + 64, 2 * (T + t) + ri, :]
                                    mm = pe.matmul(banks[h][:, t * HW:(t + 1) * HW], ifine[64 * h:64 * h + 64, T + t, ri, :], y,
                                                   start=(ri == 0), stop=(ri == 1))
                                    if t == 1 and ri == 1:
                                        mm.then_inc(ra.full, 1)
                    pe.wait_ge(s_shuf, 16 * GROUPS * (2 * o + 2))
                    for q in range(4):
                        bank = rv.fill(pe)
                        for b in range(2):
                            y = part1[:, 8 * b + 2 * q:8 * b + 2 * q + 2, :]
                            mm = pe.matmul(bank[:, :], itime[:, b, :], y, start=(b == 0), stop=(b == 1))
                        mm.then_inc(rv.full, 1)
                pe.wait_ge(s_y, 2)
                for half in range(2):
                    for q in range(2):
                        bank = ra.fill(pe)
                        for m in range(4):
                            mm = pe.transpose(bank[:, m * P:(m + 1) * P], v[:, 4 * q + m, half * P:(half + 1) * P], k.ident[:, :])
                        mm.then_inc(ra.full, 1)

            @block.sync
            def _(sp):
                this = k.of_layer
                sp.dma_start(convw, this(a_in["hy_conv_w"]).rearrange("a j c -> a (j c)").to_broadcast((P, 9 * HW))).then_inc(s_conv, 16)
                sp.dma_start(convb, this(a_in["hy_conv_b"]).to_broadcast((P, 3 * HW))).then_inc(s_conv, 16)
                sp.dma_start(k.skip[:, :, :], this(a_in["hy_skip"]).rearrange("a o c -> a (o c)").to_broadcast((P, 2 * HW))).then_inc(s_conv, 16)
                sp.dma_start(time[:, :, :], a_in["dft_time"]).then_inc(s_tab, 16)
                sp.dma_start(itime[:, :, :], a_in["idft_time"]).then_inc(s_tab, 16)
                sp.dma_start(fine[:, :, :, :], a_in["dft_fine"]).then_inc(s_tab, 16)
                sp.dma_start(ifine[:, :, :, :], a_in["idft_fine"]).then_inc(s_tab, 16)
                for n, c in enumerate((slice(0, 2 * HW), slice(2 * HW, 3 * HW))):
                    sp.wait_ge(ra.free, (n + 1) * NR)
                    sp.wait_ge(s_zero, 1)
                    sp.dma_start(raw[1:P, 0, c], raw[0:P - 1, NR, c]).then_inc(s_shift[n], 16)
                    sp.dma_start(raw[0:P - 1, NR + 1, c], raw[1:P, 1, c]).then_inc(s_shift[n], 16)
                sp.wait_ge(ra.free, 20)
                sp.dma_start(k.context_columns, uc[:, :, :]).then_inc(s_spill, 16)
                sp.wait_ge(s_ready, 1)
                for o in range(2):
                    if o == 1:
                        sp.wait_ge(s_prod, HT)
                    sp.dma_start(aux[:, :, :], k.spectra[o, :, 0:17, :]).then_inc(s_spec, 16)
                    sp.wait_ge(ra.free, A[o] + 8)
                    if o == 1:
                        sp.wait_ge(ra.full, A[1] + 8)
                    for g in range(GROUPS):
                        sp.dma_start(part2[:, g, :], part1[8 * g:8 * g + 8, :, :]).then_inc(s_shuf, 16)
                    load_weights(k, sp, 8 + o)
                    sp.wait_ge(ra.free, A[o] + 16)
                    for g in range(GROUPS):
                        sp.dma_start(part1[8 * g:8 * g + 8, :, :], part2[:, g, :]).then_inc(s_shuf, 16)
                sp.wait_ge(s_shuf, 64 * GROUPS)
                sp.wait_ge(s_spill, 16)

            @block.scalar
            def _(act):
                for n, i in PROJECTIONS:
                    bank = ra.read(act)
                    dst = raw[:, i + 1, :] if i < NR else uc[:, i - NR, :]
                    if n == 6:
                        act.activation(dst[:, 0:2 * HW], bank[:, :], ACT.Copy).then_inc(ra.free, 1)
                    else:
                        gate = gh[:, i, :] if i < NR else dst[:, 3 * HW:4 * HW]
                        act.activation(gate, bank[:, HW:2 * HW], ACT.Silu)
                        act.activation(dst[:, 2 * HW:3 * HW], bank[:, 0:HW], ACT.Copy).then_inc(ra.free, 1)
                for o in range(2):
                    if o == 0:
                        act.wait_ge(s_ready, 1)
                    else:
                        act.wait_ge(rv.full, 12)
                    for b in range(2):
                        for q in range(4):
                            bank = ra.read(act)
                            dst = part1[:, 8 * b + 2 * q:8 * b + 2 * q + 2, :]
                            act.activation(dst, bank[:, :].rearrange("p (a c) -> p a c", a=2), ACT.Copy).then_inc(ra.free, 1)
                    for n in range(HT):
                        bank = ra.read(act)
                        g = 4 * (n // 2) + n % 2
                        act.activation(part2[:, g:g + 3:2, :], bank[:, :].rearrange("p (a c) -> p a c", a=2), ACT.Copy).then_inc(ra.free, 1)
                for half in range(2):
                    for q in range(2):
                        bank = ra.read(act)
                        dst = k.z_hy[:, half, LC:].rearrange("p (m r) -> p r m", r=NR)[:, 4 * q:4 * q + 4, :]
                        act.activation(dst, bank[:, :].rearrange("p (r m) -> p r m", r=4), ACT.Copy).then_inc(ra.free, 1)

            @block.gpsimd
            def _(pool):
                pool.memset(raw[0:1, 0, :], 0.0)
                pool.memset(raw[96:P, NR + 1, :], 0.0).then_inc(s_zero, 1)
                for o in range(2):
                    pool.wait_ge(ra.full, A[o] + 8)
                    pool.tensor_tensor(v[:, :, 0:HW], v[:, :, 0:HW], k.skip[:, o, :].unsqueeze(1).to_broadcast((P, NR, HW)),
                                       ALU.mult).then_inc(s_skip, 1)

            @block.vector
            def _(dve):
                step = Chain(s_step, dve)
                row = lambda r: r.unsqueeze(1).to_broadcast((P, NR, HW))
                dve.wait_ge(s_conv, 3 * 16)
                prod = aux[:, 9:17, :]
                for g in range(3):
                    dve.wait_ge(s_shift[g // 2], 32)
                    c = slice(g * HW, (g + 1) * HW)
                    x = v[:, :, c]
                    step(dve.tensor_tensor(x, raw[:, 1:NR + 1, c], row(convw[:, 1, c]), ALU.mult))
                    step(dve.tensor_tensor(x, x, row(convb[:, c]), ALU.add))
                    for j, r0 in ((0, 0), (2, 2)):
                        step(dve.tensor_tensor(prod, raw[:, r0:r0 + NR, c], row(convw[:, j, c]), ALU.mult))
                        step(dve.tensor_tensor(x, x, prod, ALU.add))
                dve.memset(tmp[:, 0, 0:1], 0.0).then_inc(s_ready, 1)
                dve.wait_ge(s_ready, 1)
                for o in range(2):
                    dve.wait_ge(s_spec, 16 * (o + 1))
                    dve.wait_ge(s_shuf, 16 * GROUPS * (2 * o + 1))
                    for T in range(HT):
                        bank = rv.read(dve)
                        x = bank[:, :].rearrange("p (r c) -> p r c", r=2)
                        y = part1[:, 2 * T:2 * T + 2, :]
                        t = tmp[:, 2 * (T % 2):2 * (T % 2) + 2, :]
                        f = aux[:, T, :].unsqueeze(1).to_broadcast((P, 2, HW)) if T else aux[:, 0:17:16, :]
                        dve.tensor_tensor(y, x, f, ALU.mult).then_inc(s_step, 1)
                        step.n += 1
                        dve.tensor_tensor(t, x, aux[:, 8 + T, :].unsqueeze(1).to_broadcast((P, 2, HW)), ALU.mult).then_inc(rv.free, 1)
                        dve.wait_ge(rv.free, rv.got)
                        dve.tensor_tensor(y[:, 0, :], y[:, 0, :], t[:, 1, :], ALU.subtract)
                        dve.tensor_tensor(y[:, 1, :], y[:, 1, :], t[:, 0, :], ALU.add).then_inc(s_prod, 1)
                    dve.wait_ge(s_prod, HT * (o + 1))
                    dve.wait_ge(s_skip, o + 1)
                    for q in range(4):
                        bank = rv.read(dve)
                        t = tmp[:, 2 * (q % 2):2 * (q % 2) + 2, :]
                        x = v[:, 2 * q:2 * q + 2, 0:HW]
                        dve.tensor_tensor(t, bank[:, :].rearrange("p (a c) -> p a c", a=2),
                                          k.inv_sum[:, o, 0, :].unsqueeze(1).to_broadcast((P, 2, HW)), ALU.mult).then_inc(rv.free, 1)
                        dve.wait_ge(rv.free, rv.got)
                        step(dve.tensor_tensor(x, x, t, ALU.add))
                        ins = dve.tensor_tensor(x, x, v[:, 2 * q:2 * q + 2, (1 + o) * HW:(2 + o) * HW], ALU.mult)
                        if o == 1:
                            step(ins)
                            ins = dve.tensor_tensor(x, x, gh[:, 2 * q:2 * q + 2, :], ALU.mult)
                        if q < 3:
                            step(ins)
                    ins.then_inc(s_y, 1)


ROWS = L // GRID


def window(i):
    if i < TC:
        return None
    r = 2 * (i - TC)
    s = min(max(r - KH // 2, 0), ROWS - KH)
    inner = r - KH // 2 == s and r + 1 - KH // 2 <= ROWS - KH and r - KH // 2 >= 0
    return s, KH + (1 if inner and r + 1 - KH // 2 == s + 1 else 0), s - r + KH - 1


def attention_stage(k):
    nc, a_in = k.nc, k.a
    PAIRS = NA_HEADS // 2
    UNITS = 2 * TILES
    NW = (KH + 1) * GRID
    BLOCKS = TC + (NW + P - 1) // P
    with ExitStack() as mem:
        sb = lambda name, shape: sbuf(mem, nc, name, shape)
        q, k_hi, k_lo = sb("s4_q", [P, 2, TOK]), sb("s4_k_high", [P, 2, TOK]), sb("s4_k_low", [P, 2, TOK])
        v, g = sb("s4_v", [P, TILES, 2 * HD]), sb("s4_g", [P, TILES, 2 * HD])
        qk, square = sb("s4_qk", [P, 2, 512]), sb("s4_square", [P, 4 * HD])
        norm = sb("s4_norm", [P, 2, 3, 4])
        gains = sb("s4_gains", [P, 2])
        eps = sb("s4_eps", [P, 1])
        mask = sb("s4_mask", [P, GRID])
        table = sb("s4_bias", [P, 2, 2 * KH, GRID])
        raw = sb("s4_raw_bias", [P, 2 * KH, GRID])
        inner = sb("s4_inner_bias", [P, 2, KH + 1, GRID])
        p_sb = sb("s4_probs", [P, 4, LC + NW])
        pT = sb("s4_probsT", [P, 2, BLOCKS * P])
        top, total = sb("s4_max", [P, 4, 3]), sb("s4_sum", [P, 8, 4])

        ring, rz = Ring("s4_qkv", k.psum[4:8], k.sem), Ring("s4_zT", k.psum[0:4], k.sem)
        s_in, s_bias, s_zero = k.sem("s4_gains_here"), k.sem("s4_bias_ready"), k.sem("s4_eps")
        s_raw = k.sem("s4_raw_bias_here")
        s_sq, s_ss, s_rt, s_vg, s_hi = (k.sem("s4_" + n) for n in ("squares", "square_sums", "roots", "v_and_gate", "high_parts"))
        s_scores, s_max, s_exp = k.sem("s4_scores"), k.sem("s4_max_ready"), k.sem("s4_exp_done")
        s_t0, s_t1, s_c0, s_c1 = (k.sem("s4_" + n) for n in ("probsT_low", "probsT_high", "probsT_low_copied", "probsT_high_copied"))
        s_o, s_z, s_step, s_pool = k.sem("s4_o"), k.sem("s4_z"), k.sem("s4_dve_step"), k.sem("s4_pool_step")
        RU = 2 * TILES
        ZU = (TILES + 3) // 4

        def unit(n):
            return n // UNITS, n % 2, n % UNITS // 2

        def scores_of(n):
            return k.all_psum[:, (n % 2) * 1024:(n % 2) * 1024 + 1024]

        def blocks(i):
            out = [(0, P), (1, P)]
            if window(i):
                s, rows, _ = window(i)
                keys = rows * GRID
                out += [(TC + s // 2 + b, min(P, keys - b * P)) for b in range((keys + P - 1) // P)]
            return out

        def projected(pair, i):
            return RU * pair + max(2 * i, 1)

        def turned_at(pair, i):
            return RU * pair + min(2 * i + 3, RU)

        def bank_at(count):
            return ring.banks[(count - 1) % len(ring.banks)]

        def place(i, b):
            return 4 if i < TC and b == 1 else b

        with nc.Block() as block:
            @block.sync
            def _(sp):
                this = k.of_layer
                for c, name in enumerate(("na_q_gain", "na_k_gain")):
                    for h in range(2):
                        sp.dma_start(gains[64 * h:64 * h + 64, c:c + 1], this(a_in[name]).rearrange("a n -> n a")).then_inc(s_in, 16)
                sp.dma_start(mask[:, :], a_in["colmask"]).then_inc(s_in, 16)
                for h in range(NA_HEADS):
                    if h >= 1:
                        sp.wait_ge(s_bias, h)
                    rpb = this(a_in["na_rpb"])[:, h]
                    for part in range(2):
                        src = bass.AP(rpb.tensor, rpb.offset + (1 - part) * P, [[1, GRID], [P, 2 * KH], [1, GRID]])
                        sp.dma_start(raw[64 * part:64 * part + 64], src).then_inc(s_raw, 16)
                    if h % 2 == 0 and h >= 2:
                        pair = h // 2 - 1
                        sp.wait_ge(ring.full, projected(pair, TILES - 1))
                        load_weights(k, sp, 10 + pair)
                sp.wait_ge(ring.full, projected(PAIRS - 1, TILES - 1))
                load_weights(k, sp, 10 + PAIRS - 1)

            @block.gpsimd
            def _(pool):
                pool.wait_ge(s_in, 5 * 16)
                for h in range(NA_HEADS):
                    pool.wait_ge(s_raw, 32 * (h + 1))
                    t = table[:, h % 2]
                    if h >= 1:
                        pool.wait_ge(s_bias, h)
                    if h >= 2:
                        pool.wait_ge(s_max, UNITS * (h // 2) - 1 + h % 2)
                    pool.tensor_tensor(t, raw[:, :, ::-1], mask[:, :].unsqueeze(1).to_broadcast((P, 2 * KH, GRID)), ALU.add).then_inc(s_pool, 1)
                    pool.wait_ge(s_pool, 3 * h + 1)
                    pool.tensor_copy(inner[:, h % 2], t[:, 3:4 + KH, :]).then_inc(s_pool, 1)
                    pool.wait_ge(s_pool, 3 * h + 2)
                    pool.memset(inner[0:64, h % 2, KH, :], NEG).then_inc(s_pool, 1)
                    pool.wait_ge(s_pool, 3 * h + 3)
                    pool.memset(inner[64:128, h % 2, 0, :], NEG).then_inc(s_bias, 1)

            @block.tensor
            def _(pe):
                def projections(pair):
                    w = wait_weights(k, pe, 8 + pair)

                    def turn(i):
                        pe.wait_ge(ring.free, projected(pair, i))
                        bank = ring.fill(pe)
                        for m in range(4):
                            mm = pe.transpose(bank[:, m * P:(m + 1) * P], qk[:, i % 2, m * P:(m + 1) * P], k.ident[:, :])
                        mm.then_inc(ring.full, 1)

                    for i in range(TILES):
                        bank = ring.fill(pe)
                        for kc in range(KC):
                            mm = pe.matmul(bank[:, :], k.hxT[:, kc, i * P:(i + 1) * P], w[:, kc, :], start=(kc == 0), stop=(kc == KC - 1))
                        mm.then_inc(ring.full, 1)
                        if i >= 1:
                            turn(i - 1)
                    turn(TILES - 1)

                def scores(n):
                    _, _, i = unit(n)
                    if n >= 2:
                        pe.wait_ge(s_exp, n)
                    parts = [(0, 0, LC)]
                    if window(i):
                        s, n_rows, _ = window(i)
                        k0 = LC + s * GRID
                        parts += [(LC, k0, 256), (512, k0 + 256, n_rows * GRID - 256)]
                    for h in range(2):
                        for c0, key, keys in parts:
                            for kk in (k_hi, k_lo):
                                mm = pe.matmul(scores_of(h)[:, c0:c0 + keys], R32(q[:, h, i * P:(i + 1) * P]), R32(kk[:, h, key:key + keys]),
                                               start=(kk is k_hi), stop=(kk is k_lo))
                        mm.then_inc(s_scores, 1)

                def turn_probs(n):
                    _, _, i = unit(n)
                    pe.wait_ge(s_exp, n + 1)
                    if n >= 1:
                        pe.wait_ge(s_c0, n)
                    for b, (_, keys) in enumerate(blocks(i)):
                        at = place(i, b)
                        if at == 4 and n >= 1:
                            pe.wait_ge(s_c1, n)
                        mm = pe.transpose(k.all_psum[0:keys, 2048 + at * P:2048 + (at + 1) * P], p_sb[:, n % 4, b * P:b * P + keys], k.ident[:, :])
                        if place(i, b + 1) == 4:
                            mm.then_inc(s_t0, 1)
                    mm.then_inc(s_t1, 1)

                def outputs(n):
                    _, h, i = unit(n)
                    pe.wait_ge(s_c0, n + 1)
                    pe.wait_ge(s_c1, n + 1)
                    if n >= 2:
                        pe.wait_ge(s_z, n - 1)
                    bank = k.psum[6 + n % 2]
                    last = len(blocks(i)) - 1
                    for b, (tile, keys) in enumerate(blocks(i)):
                        mm = pe.matmul(bank[:, 0:HD], pT[0:keys, n % 2, place(i, b) * P:(place(i, b) + 1) * P], v[0:keys, tile, h * HD:(h + 1) * HD],
                                       start=(b == 0), stop=(b == last))
                    mm.then_inc(s_o, 1)

                for pair in range(PAIRS):
                    n0, n1 = pair * UNITS, (pair + 1) * UNITS
                    projections(pair)
                    pe.wait_ge(ring.free, RU * (pair + 1))
                    if pair >= 1:
                        pe.wait_ge(rz.free, ZU * pair)
                    for n in range(n0, n1 + 4, 2):
                        if n < n1:
                            scores(n)
                        for h in range(2):
                            if n0 <= n - 4:
                                outputs(n - 4 + h)
                            if n0 <= n - 2 < n1:
                                turn_probs(n - 2 + h)
                    pe.wait_ge(s_z, n1)
                    for t in range(0, TILES, 4):
                        bank = rz.fill(pe)
                        for i in range(t, min(t + 4, TILES)):
                            mm = pe.transpose(bank[:, (i - t) * P:(i - t + 1) * P], g[:, i, :], k.ident[:, :])
                        mm.then_inc(rz.full, 1)

            @block.scalar
            def _(act):
                def high_parts(pair, i):
                    bank = bank_at(turned_at(pair, i))
                    act.wait_ge(ring.full, turned_at(pair, i))
                    for c, dst in enumerate((q, k_hi)):
                        ins = act.activation(R32(dst[:, :, i * P:(i + 1) * P]), bank[:, c * 256:(c + 1) * 256].rearrange("p (m t) -> p m t", m=2),
                                             ACT.Copy, scale=gains[:, c:c + 1])
                    ins.then_inc(s_hi, 1)

                def probs(n):
                    i = unit(n)[2]
                    act.wait_ge(s_max, n + 1)
                    bias = top[:, n % 4, 2:3]
                    if window(i):
                        p = p_sb[:, n % 4, LC:LC + window(i)[1] * GRID]
                        act.activation(p, p, ACT.Exp, bias=bias, accum_out=total[:, n % 8, 1:2])
                    act.activation(p_sb[:, n % 4, 0:LC], scores_of(n)[:, 0:LC], ACT.Exp, bias=bias,
                                   accum_out=total[:, n % 8, 0:1]).then_inc(s_exp, 1)

                def copy_low(n):
                    cols = (4 if window(unit(n)[2]) else 1) * P
                    act.wait_ge(s_t0, n + 1)
                    if n >= 2:
                        act.wait_ge(s_o, n - 1)
                    act.activation(pT[:, n % 2, 0:cols], k.all_psum[:, 2048:2048 + cols], ACT.Copy).then_inc(s_c0, 1)

                act.wait_ge(s_zero, 1)
                for pair in range(PAIRS):
                    if pair >= 1:
                        act.wait_ge(rz.full, ZU * pair)
                        act.wait_ge(s_o, UNITS * pair)
                    for i in range(TILES):
                        n = TILES * pair + i
                        bank = bank_at(projected(pair, i))
                        act.wait_ge(ring.full, projected(pair, i))
                        if n >= 1:
                            act.wait_ge(s_ss, n)
                        act.activation(square[:, :], bank[:, 0:256], ACT.Square).then_inc(s_sq, 1)
                        act.activation(g[:, i, :], bank[:, 384:512], ACT.Silu)
                        act.activation(v[:, i, :], bank[:, 256:384], ACT.Copy).then_inc(s_vg, 1)
                        act.wait_ge(s_ss, n + 1)
                        act.activation(norm[:, i % 2, 1, :], norm[:, i % 2, 0, :], ACT.Sqrt, bias=eps[:, 0:1], scale=1.0 / HD).then_inc(s_rt, 1)
                        if i >= 1:
                            high_parts(pair, i - 1)
                    high_parts(pair, TILES - 1)
                    n0, n1 = pair * UNITS, (pair + 1) * UNITS
                    for n in range(n0, n1 + 2, 2):
                        for h in range(2):
                            if n < n1:
                                probs(n + h)
                            if n > n0:
                                copy_low(n - 2 + h)
                    for t in range(0, TILES, 4):
                        tiles = min(4, TILES - t)
                        bank = rz.read(act)
                        act.activation(k.z_na[:, pair, t * P:(t + tiles) * P], bank[:, 0:tiles * P], ACT.Copy).then_inc(rz.free, 1)

            @block.vector
            def _(dve):
                step = Chain(s_step, dve)
                dve.memset(eps[:, :], EPS).then_inc(s_zero, 1)
                dve.wait_ge(s_in, 5 * 16)
                step(dve.tensor_scalar(gains[:, 0:1], gains[:, 0:1], HD ** -0.5, None, ALU.mult))

                def low_parts(pair, i):
                    bank = ring.read(dve)
                    dve.wait_ge(s_hi, TILES * pair + i + 1)
                    cols = slice(i * P, (i + 1) * P)
                    two = lambda x: x.rearrange("p (m t) -> p m t", m=2)
                    dve.scalar_tensor_tensor(out=R32(k_lo[:, :, cols]), in0=two(bank[:, 256:512]), scalar=gains[:, 1:2], in1=k_hi[:, :, cols],
                                             op0=ALU.mult, op1=ALU.subtract)
                    dve.scalar_tensor_tensor(out=R32(q[64:128, :, cols]), in0=two(bank[64:128, 0:256]), scalar=gains[64:128, 0:1],
                                             in1=q[64:128, :, cols], op0=ALU.mult, op1=ALU.subtract).then_inc(ring.free, 1)

                def maximum(n):
                    pair, h, i = unit(n)
                    dve.wait_ge(s_scores, n + 1)
                    if n >= 4:
                        dve.wait_ge(s_t1, n - 3)
                    slot = top[:, n % 4]
                    bank = scores_of(n)
                    best = slot[:, 0:1]
                    dve.tensor_reduce(best, bank[:, 0:LC], AX.X, ALU.max).then_inc(s_step, 1)
                    step.n += 1
                    if window(i):
                        s, rows, first = window(i)
                        if i == TC:
                            dve.wait_ge(s_bias, 2 * pair + h + 1)
                        bias = inner[:, h] if rows > KH else table[:, h, first:first + KH, :]
                        keys = rows * GRID
                        step(dve.tensor_tensor_reduce(p_sb[:, n % 4, LC:LC + keys], bank[:, LC:LC + keys], bias.rearrange("p j c -> p (j c)"),
                                                      1.0, -3e38, ALU.add, ALU.max, slot[:, 1:2]))
                        dve.tensor_scalar(slot[:, 2:3], best, slot[:, 1:2], -1.0, ALU.max, ALU.mult).then_inc(s_max, 1)
                    else:
                        dve.wait_ge(s_step, step.n)
                        dve.tensor_scalar(slot[:, 2:3], best, -1.0, None, ALU.mult).then_inc(s_max, 1)

                def copy_high(n):
                    i = unit(n)[2]
                    dve.wait_ge(s_t1, n + 1)
                    if n >= 2:
                        dve.wait_ge(s_o, n - 1)
                    parts = [(place(i, b), keys) for b, (_, keys) in enumerate(blocks(i)) if place(i, b) >= 4]
                    full = sum(keys == P for _, keys in parts)
                    at = 4 * P
                    cols = full * P
                    ins = dve.tensor_copy(pT[:, n % 2, at:at + cols], k.all_psum[:, 2048 + at:2048 + at + cols])
                    if full < len(parts):
                        at += cols
                        ins = dve.tensor_copy(pT[0:64, n % 2, at:at + P], k.all_psum[0:64, 2048 + at:2048 + at + P])
                    ins.then_inc(s_c1, 1)

                def gated(n):
                    _, h, i = unit(n)
                    slot = total[:, n % 8]
                    if i < TC:
                        step(dve.reciprocal(slot[:, 3:4], slot[:, 0:1]))
                    else:
                        step(dve.tensor_tensor(slot[:, 2:3], slot[:, 0:1], slot[:, 1:2], ALU.add))
                        step(dve.reciprocal(slot[:, 3:4], slot[:, 2:3]))
                    dve.wait_ge(s_o, n + 1)
                    z = g[:, i, h * HD:(h + 1) * HD]
                    dve.scalar_tensor_tensor(out=z, in0=k.psum[6 + n % 2][:, 0:HD], scalar=slot[:, 3:4], in1=z, op0=ALU.mult, op1=ALU.mult).then_inc(s_z, 1)

                for pair in range(PAIRS):
                    for i in range(TILES):
                        n = TILES * pair + i
                        dve.wait_ge(s_sq, n + 1)
                        dve.tensor_reduce(norm[:, i % 2, 0, :], square[:, :].rearrange("p (h d) -> p h d", d=HD), AX.X, ALU.add).then_inc(s_ss, 1)
                        dve.wait_ge(s_rt, n + 1)
                        step(dve.reciprocal(norm[:, i % 2, 2, :], norm[:, i % 2, 1, :]))
                        if n >= 2:
                            dve.wait_ge(ring.full, turned_at((n - 2) // TILES, (n - 2) % TILES))
                        bank = ring.read(dve)
                        dve.wait_ge(s_vg, n + 1)
                        twice = lambda x: x.unsqueeze(2).to_broadcast((P, 4, 2, HD))
                        dve.tensor_tensor(qk[:, i % 2, :].rearrange("p (h w d) -> p h w d", w=2, d=HD), twice(bank[:, 0:256].rearrange("p (h d) -> p h d", d=HD)),
                                          twice(norm[:, i % 2, 2, :].unsqueeze(2).to_broadcast((P, 4, HD))), ALU.mult).then_inc(ring.free, 1)
                        if i >= 1:
                            low_parts(pair, i - 1)
                    low_parts(pair, TILES - 1)
                    n0, n1 = pair * UNITS, (pair + 1) * UNITS
                    for n in range(n0, n1 + 4, 2):
                        if n < n1:
                            maximum(n)
                            maximum(n + 1)
                        for h in range(2):
                            if n0 <= n - 4:
                                gated(n - 4 + h)
                            if n0 <= n - 2 < n1:
                                copy_high(n - 2 + h)


CHAINS = (list(range(TILES)), [1, 0] + list(range(TILES - 1, TC - 1, -1)))


def retention_stage(k):
    nc, a_in = k.nc, k.a
    with ExitStack() as mem:
        sb = lambda name, shape: sbuf(mem, nc, name, shape)
        qk, vg = sb("s5_qk", [P, TILES, 512]), sb("s5_vg", [P, TILES, 512])
        rope, tmp = sb("s5_rope", [P, TILES, 64]), sb("s5_tmp", [P, 512])
        dist, age, rest = sb("s5_dist", [P, 4, P]), sb("s5_age", [P, 2, P]), sb("s5_rest", [P, 8])
        rate, zeta = sb("s5_log_gamma", [P, 8]), sb("s5_zeta", [P, 8])
        rate_p, power = sb("s5_log_gamma_turned", [P, 4]), sb("s5_chunk_decay", [P, 4])
        decay = sb("s5_decay", [P, 2, 2, P])
        fade = sb("s5_fade", [P, 2, 2, P])
        state = sb("s5_state", [P, TILES, 2, P])
        kz = sb("s5_k_weighted", [P, 2, 2, RW])
        qkT, qx = sb("s5_qkT", [P, 2, 512]), sb("s5_q_faded", [P, 2, 2, RW])
        sT, r = sb("s5_scoresT", [P, 2, 2, RW]), sb("s5_r", [P, 2, RW])
        stat, eps = sb("s5_stat", [P, 2, 3, RH]), sb("s5_eps", [P, 1])

        ra, rv = Ring("s5_act", k.psum[0:4], k.sem), Ring("s5_dve", k.psum[4:8], k.sem)
        names = ("tables_here", "rates", "tables", "dve_step", "act_step", "roped", "k_weighted", "weighted_free", "states",
                 "q_faded", "scores", "scores_weighted", "o", "o_copied", "square_sums", "roots", "z", "eps", "pool_step")
        (s_tab, s_rate, s_table, s_step, s_act, s_rope, s_kz, s_kzfree, s_state, s_qx, s_sc, s_sw, s_o, s_oc, s_ss, s_rt, s_z,
         s_eps, s_pool) = (k.sem("s5_" + n) for n in names)

        with nc.Block() as block:
            @block.sync
            def _(sp):
                rates = k.of_layer(a_in["ret_log_rate"])
                sp.dma_start(rate[:, :], rates.rearrange("a d h -> a (d h)").to_broadcast((P, 8))).then_inc(s_tab, 16)
                for h2 in range(2):
                    src = rates.rearrange("a d (p h) -> a (d p) h", h=2)[:, :, h2]
                    sp.dma_start(rate_p[64 * h2:64 * h2 + 64, :], src.to_broadcast((64, 4))).then_inc(s_tab, 16)
                sp.dma_start(rest[:, :], a_in["rest"].rearrange("p d h -> p (d h)")).then_inc(s_tab, 16)
                sp.dma_start(dist[:, :, :], a_in["dist"]).then_inc(s_tab, 16)
                sp.dma_start(age[:, :, :], a_in["age"]).then_inc(s_tab, 16)
                sp.dma_start(rope[:, :, :], a_in["rope"]).then_inc(s_tab, 16)
                sp.wait_ge(rv.full, TILES)
                load_weights(k, sp, 14)
                sp.wait_ge(ra.full, TILES)
                load_weights(k, sp, 15)

            @block.tensor
            def _(pe):
                for ring, n in ((rv, 12), (ra, 13)):
                    w = wait_weights(k, pe, n)
                    for i in range(TILES):
                        bank = ring.fill(pe)
                        for kc in range(KC):
                            mm = pe.matmul(bank[:, :], k.hxT[:, kc, i * P:(i + 1) * P], w[:, kc, :], start=(kc == 0), stop=(kc == KC - 1))
                        mm.then_inc(ring.full, 1)
                pe.wait_ge(ra.free, TILES)
                for j in range(TILES - 1):
                    pe.wait_ge(s_kz, 2 * j + 2)
                    bank = rv.fill(pe)
                    for d in range(2):
                        t = CHAINS[d][j]
                        for h in range(RH):
                            mm = pe.matmul(bank[64 * (h % 2):64 * (h % 2) + 64, d * P + (h // 2) * HD:d * P + (h // 2 + 1) * HD],
                                           kz[:, j % 2, d, h * HD:(h + 1) * HD], vg[:, t, h * HD:(h + 1) * HD], start=True, stop=True)
                    mm.then_inc(rv.full, 1)

                def turn(i):
                    bank = ra.fill(pe)
                    for m in range(4):
                        mm = pe.transpose(bank[:, m * P:(m + 1) * P], qk[:, i, m * P:(m + 1) * P], k.ident[:, :])
                    mm.then_inc(ra.full, 1)

                pe.wait_ge(rv.free, 2 * TILES - 1)
                turn(0)
                for i in range(TILES):
                    if i + 1 < TILES:
                        turn(i + 1)
                    pe.wait_ge(ra.free, TILES + i + 1)
                    if i >= 1:
                        pe.wait_ge(s_sw, i)
                    for h in (0, 2, 1, 3):
                        rows = slice(64 * (h % 2), 64 * (h % 2) + 64)
                        pair = h // 2
                        mm = pe.matmul(k.psum[4 + h % 2][:, pair * P:(pair + 1) * P], qkT[rows, i % 2, (2 + pair) * P:(3 + pair) * P],
                                       qkT[rows, i % 2, pair * P:(pair + 1) * P], start=True, stop=True)
                    mm.then_inc(s_sc, 1)
                    pe.wait_ge(s_sw, i + 1)
                    pe.wait_ge(s_qx, i + 1)
                    if i >= 1:
                        pe.wait_ge(s_oc, i)
                    for h in (0, 2, 1, 3):
                        rows = slice(64 * (h % 2), 64 * (h % 2) + 64)
                        pair = h // 2
                        out = k.psum[6 + h % 2][:, pair * HD:(pair + 1) * HD]
                        pe.matmul(out, sT[:, i % 2, h % 2, pair * P:(pair + 1) * P], vg[:, i, h * HD:(h + 1) * HD], start=True, stop=False)
                        for d in range(2):
                            mm = pe.matmul(out, qx[rows, i % 2, d, pair * P:(pair + 1) * P], state[rows, i, d, pair * HD:(pair + 1) * HD],
                                           start=False, stop=(d == 1))
                    mm.then_inc(s_o, 1)
                pe.wait_ge(s_z, TILES)
                for t in range(TILES // 2):
                    bank = ra.fill(pe)
                    for m in range(4):
                        mm = pe.transpose(bank[:, m * P:(m + 1) * P], qk[:, 2 * t + m % 2, (m // 2) * P:(m // 2 + 1) * P], k.ident[:, :])
                    mm.then_inc(ra.full, 1)

            @block.scalar
            def _(act):
                act.wait_ge(s_tab, 7 * 16)
                act.activation(rate[:, :], rate[:, :], ACT.Exp)
                act.activation(rate_p[:, :], rate_p[:, :], ACT.Exp).then_inc(s_rate, 1)
                act.wait_ge(s_table, 1)
                act.activation(zeta[:, :], zeta[:, :], ACT.Exp).then_inc(s_act, 1)
                act.activation(power[:, :], rate_p[:, :], ACT.Exp, scale=float(P)).then_inc(s_act, 1)
                for d in range(2):
                    for pair in range(2):
                        act.activation(fade[:, d, pair, :], age[:, d, :], ACT.Exp, scale=rate_p[:, 2 * d + pair:2 * d + pair + 1]).then_inc(s_act, 1)
                for h in range(RH):
                    if h >= 1:
                        act.wait_ge(s_table, 1 + h)
                    for d in range(2):
                        act.activation(tmp[:, d * P:(d + 1) * P], dist[:, d, :], ACT.Exp, scale=rate[:, RH * d + h:RH * d + h + 1]).then_inc(s_act, 1)
                for i in range(TILES):
                    bank = ra.read(act)
                    act.activation(vg[:, i, RW:2 * RW], bank[:, RW:2 * RW], ACT.Silu)
                    act.activation(vg[:, i, 0:RW], bank[:, 0:RW], ACT.Copy).then_inc(ra.free, 1)
                act.wait_ge(s_eps, 1)

                def root(i):
                    act.wait_ge(s_ss, i + 1)
                    act.activation(stat[:, i % 2, 1, :], stat[:, i % 2, 0, :], ACT.Sqrt, bias=eps[:, 0:1], scale=1.0 / HD).then_inc(s_rt, 1)

                for i in range(TILES):
                    if i >= 2:
                        root(i - 2)
                        act.wait_ge(s_qx, i - 1)
                        act.wait_ge(s_sc, i - 1)
                    bank = ra.read(act)
                    act.activation(qkT[:, i % 2, :], bank[:, :], ACT.Copy).then_inc(ra.free, 1)
                root(TILES - 2)
                root(TILES - 1)
                for t in range(TILES // 2):
                    bank = ra.read(act)
                    act.activation(k.z_re[:, :, 2 * t * P:(2 * t + 2) * P], bank[:, :].rearrange("p (c t) -> p c t", c=2), ACT.Copy).then_inc(ra.free, 1)

            @block.gpsimd
            def _(pool):
                pool.memset(state[:, 0, 0, :], 0.0).then_inc(s_pool, 1)
                pool.memset(state[:, 1, 1, :], 0.0).then_inc(s_pool, 1)
                pool.wait_ge(s_pool, 2)
                pool.wait_ge(s_table, 6)
                pool.wait_ge(s_rope, TILES)
                for j in range(TILES - 1):
                    if j >= 2:
                        pool.wait_ge(rv.full, TILES + j - 1)
                    for d in range(2):
                        t = CHAINS[d][j]
                        if j or d:
                            pool.wait_ge(s_kz, 2 * j + d)
                        pool.tensor_tensor(kz[:, j % 2, d, :].rearrange("p (h e) -> p h e", h=RH),
                                           qk[:, t, RW:2 * RW].rearrange("p (h e) -> p h e", h=RH),
                                           zeta[:, RH * d:RH * d + RH].unsqueeze(2).to_broadcast((P, RH, HD)), ALU.mult).then_inc(s_kz, 1)

            @block.vector
            def _(dve):
                step = Chain(s_step, dve)
                dve.memset(eps[:, :], EPS).then_inc(s_eps, 1)
                dve.wait_ge(s_rate, 1)
                step(dve.tensor_scalar(rate[:, :], rate[:, :], -1.0, None, ALU.mult))
                dve.tensor_scalar(rate_p[:, :], rate_p[:, :], -1.0, None, ALU.mult).then_inc(s_step, 1)
                step.n += 1
                dve.tensor_tensor(zeta[:, :], rest[:, :], rate[:, :], ALU.mult).then_inc(s_table, 1)
                for h in range(RH):
                    dve.wait_ge(s_act, 6 + 2 * h + 2)
                    dst = decay[:, h % 2, h // 2, :]
                    step(dve.tensor_tensor(dst, tmp[:, 0:P], dist[:, 2, :], ALU.mult))
                    step(dve.tensor_tensor(tmp[:, P:2 * P], tmp[:, P:2 * P], dist[:, 3, :], ALU.mult))
                    dve.tensor_tensor(dst, dst, tmp[:, P:2 * P], ALU.add).then_inc(s_table, 1)
                dve.wait_ge(s_table, 1 + RH)
                dve.tensor_scalar(zeta[:, :], zeta[:, :], HD ** -0.5, None, ALU.mult).then_inc(s_table, 1)

                for i in range(TILES):
                    bank = rv.read(dve)
                    halves = lambda x, n: x.rearrange("p (g n c) -> p g n c", n=2, c=16)[:, :, n, :].rearrange("p (h a) c -> p h a c", a=2)
                    x1, x2 = halves(bank[:, :], 0), halves(bank[:, :], 1)
                    o1, o2 = halves(qk[:, i, :], 0), halves(qk[:, i, :], 1)
                    cos, sin = (rope[:, i, 32 * n:32 * n + 32].rearrange("p (a c) -> p a c", a=2).unsqueeze(1).to_broadcast((P, 8, 2, 16)) for n in range(2))
                    t1 = tmp[:, 0:256].rearrange("p (h a c) -> p h a c", a=2, c=16)
                    t2 = tmp[:, 256:512].rearrange("p (h a c) -> p h a c", a=2, c=16)
                    dve.tensor_tensor(o1, x1, cos, ALU.mult)
                    step(dve.tensor_tensor(t1, x2, sin, ALU.mult))
                    step(dve.tensor_tensor(o1, o1, t1, ALU.subtract))
                    dve.tensor_tensor(o2, x1, sin, ALU.mult)
                    dve.tensor_tensor(t2, x2, cos, ALU.mult).then_inc(rv.free, 1)
                    dve.wait_ge(rv.free, rv.got)
                    dve.tensor_tensor(o2, o2, t2, ALU.add).then_inc(s_rope, 1)
                dve.wait_ge(s_rope, TILES)
                dve.wait_ge(s_pool, 2)
                for j in range(TILES - 1):
                    bank = rv.read(dve)
                    for d in range(2):
                        a, b = CHAINS[d][j], CHAINS[d][j + 1]
                        for pair in range(2):
                            c = slice(pair * HD, (pair + 1) * HD)
                            ins = dve.scalar_tensor_tensor(out=state[:, b, d, c], in0=state[:, a, d, c], scalar=power[:, 2 * d + pair:2 * d + pair + 1],
                                                           in1=bank[:, d * P + pair * HD:d * P + (pair + 1) * HD], op0=ALU.mult, op1=ALU.add)
                    ins.then_inc(rv.free, 1)
                    dve.wait_ge(rv.free, rv.got)

                def normed(i):
                    dve.wait_ge(s_rt, i + 1)
                    st = stat[:, i % 2]
                    step(dve.reciprocal(st[:, 2, :], st[:, 1, :]))
                    rr = r[:, i % 2, :]
                    heads = lambda x: x.rearrange("p (h e) -> p h e", h=RH)
                    step(dve.tensor_tensor(heads(rr), heads(rr), st[:, 2, :].unsqueeze(2).to_broadcast((P, RH, HD)), ALU.mult))
                    dve.tensor_tensor(qk[:, i, 0:RW], rr, vg[:, i, RW:2 * RW], ALU.mult).then_inc(s_z, 1)

                for i in range(TILES):
                    dve.wait_ge(ra.free, TILES + i + 1)
                    if i >= 2:
                        dve.wait_ge(s_o, i - 1)
                    for d in range(2):
                        ins = dve.tensor_tensor(qx[:, i % 2, d, :], qkT[:, i % 2, 0:RW], fade[:, d, :, :].rearrange("p a j -> p (a j)"), ALU.mult)
                    ins.then_inc(s_qx, 1)
                    dve.wait_ge(s_sc, i + 1)
                    for h2 in range(2):
                        ins = dve.tensor_tensor(sT[:, i % 2, h2, :], k.psum[4 + h2][:, 0:RW], decay[:, h2, :, :].rearrange("p a j -> p (a j)"), ALU.mult)
                    ins.then_inc(s_sw, 1)
                    if i >= 1:
                        normed(i - 1)
                    dve.wait_ge(s_o, i + 1)
                    for h2 in range(2):
                        ins = dve.tensor_copy(r[:, i % 2, :].rearrange("p (a h e) -> p h a e", h=2, e=HD)[:, h2], k.psum[6 + h2][:, 0:P].rearrange("p (a e) -> p a e", a=2))
                    ins.then_inc(s_oc, 1)
                    dve.wait_ge(s_oc, i + 1)
                    step(dve.tensor_tensor(tmp[:, 0:RW], r[:, i % 2, :], r[:, i % 2, :], ALU.mult))
                    dve.tensor_reduce(stat[:, i % 2, 0, :], tmp[:, 0:RW].rearrange("p (h e) -> p h e", h=RH), AX.X, ALU.add).then_inc(s_ss, 1)
                normed(TILES - 1)


def output_stage(k):
    nc, a_in = k.nc, k.a
    BUFS = 3
    ORDER = list(range(TC, TILES)) + list(range(TC))
    IMAGE = TILES - TC
    with ExitStack() as mem:
        sb = lambda name, shape: sbuf(mem, nc, name, shape)
        x, y = sb("s6_x", [P, BUFS, D]), sb("s6_y", [P, 2, WCH])
        u = sb("s6_context_columns", [P, TC, 4 * HW])
        cdft, cidft = sb("s6_cdft", [P, 2, 2, LC]), sb("s6_cidft", [P, 2, 2, LC])
        spec = sb("s6_spectra", [P, 2, 5, HW])
        convw, convb = sb("s6_conv_w", [P, 3, 3 * HW]), sb("s6_conv_b", [P, 3 * HW])
        before, after = sb("s6_before", [P, TC, 3 * HW]), sb("s6_after", [P, TC, 3 * HW])
        yf, tmp = sb("s6_product", [P, 2 * TC, HW]), sb("s6_tmp", [P, 2, HW])

        ring, cring = Ring("s6_out", k.psum[0:4], k.sem), Ring("s6_context", k.psum[4:8], k.sem)
        s_x = [k.sem(f"s6_x{b}_here") for b in range(BUFS)]
        s_out = [k.sem(f"s6_x{b}_stored") for b in range(BUFS)]
        s_new = k.sem("s6_x_new")
        s_tab, s_zero = k.sem("s6_tables_here"), k.sem("s6_zeroed")
        s_step, s_v, s_prod = k.sem("s6_dve_step"), k.sem("s6_v_ready"), k.sem("s6_products")
        z = [k.z_na[:, c, :] for c in range(4)] + [k.z_hy[:, c, :] for c in range(2)] + [k.z_re[:, c, :] for c in range(2)]

        def not_last(eng):
            return eng.If(k.layer < DEPTH - 1)

        with nc.Block() as block:
            @block.sync
            def _(sp):
                this = k.of_layer
                uc = k.context_columns

                def load(n):
                    sp.dma_start(x[:, n % BUFS, :], stream_tile(k, ORDER[n])).then_inc(s_x[n % BUFS], 16)

                def store(n):
                    sp.wait_ge(s_new, n + 1)
                    sp.dma_start(stream_tile(k, ORDER[n]), x[:, n % BUFS, :]).then_inc(s_out[n % BUFS], 16)

                def reload(n):
                    sp.wait_ge(s_out[n % BUFS], 16 * (n // BUFS))
                    load(n)

                for n in range(BUFS):
                    load(n)
                with not_last(sp):
                    sp.dma_start(u[:, :, :], uc).then_inc(s_tab, 16)
                    sp.wait_ge(s_zero, 1)
                    sp.dma_start(before[1:P, :, :], uc[0:P - 1, :, 0:3 * HW]).then_inc(s_tab, 16)
                    sp.dma_start(before[0:1, 1, :], uc[P - 1:P, 0, 0:3 * HW]).then_inc(s_tab, 16)
                    sp.dma_start(after[0:P - 1, :, :], uc[1:P, :, 0:3 * HW]).then_inc(s_tab, 16)
                    sp.dma_start(after[P - 1:P, 0, :], uc[0:1, 1, 0:3 * HW]).then_inc(s_tab, 16)
                    sp.dma_start(convw[:, :, :], this(a_in["hy_conv_w"]).rearrange("a j c -> a (j c)").to_broadcast((P, 9 * HW))).then_inc(s_tab, 16)
                    sp.dma_start(convb[:, :], this(a_in["hy_conv_b"]).to_broadcast((P, 3 * HW))).then_inc(s_tab, 16)
                    sp.dma_start(cdft[:, :, :, :], a_in["cdft"]).then_inc(s_tab, 16)
                    sp.dma_start(cidft[:, :, :, :], a_in["cidft"]).then_inc(s_tab, 16)
                    for o in range(2):
                        sp.dma_start(spec[:, o], k.spectra[o, :, 17:22, :]).then_inc(s_tab, 16)
                for n in range(IMAGE):
                    store(n)
                    if n + BUFS < IMAGE:
                        reload(n + BUFS)
                for n in range(IMAGE - BUFS, IMAGE):
                    sp.wait_ge(s_out[n % BUFS], 16 * (n // BUFS + 1))
                with not_last(sp):
                    for n in range(IMAGE, TILES):
                        reload(n)
                    for n in range(IMAGE, TILES):
                        store(n)
                    for n in range(IMAGE, TILES):
                        sp.wait_ge(s_out[n % BUFS], 16 * (n // BUFS + 1))

            @block.gpsimd
            def _(pool):
                pool.memset(before[0:1, 0, :], 0.0)
                pool.memset(after[96:P, :, :], 0.0).then_inc(s_zero, 1)

            @block.tensor
            def _(pe):
                w = [wait_weights(k, pe, 14 + h) for h in range(2)]

                def tile(i):
                    for h in range(2):
                        bank = ring.fill(pe)
                        for c in range(KC):
                            mm = pe.matmul(bank[:, :], z[c][:, i * P:(i + 1) * P], w[h][:, c, :], start=(c == 0), stop=(c == KC - 1))
                        mm.then_inc(ring.full, 1)

                def forward(o):
                    pe.wait_ge(s_v, o + 1)
                    for T in range(2):
                        bank = cring.fill(pe)
                        for ri in range(2):
                            for kk in range(TC):
                                mm = pe.matmul(bank[:, ri * HW:(ri + 1) * HW], cdft[:, ri, kk, T * P:(T + 1) * P], u[:, kk, 0:HW],
                                               start=(kk == 0), stop=(kk == TC - 1))
                        mm.then_inc(cring.full, 1)

                def back(o):
                    pe.wait_ge(s_prod, o + 1)
                    bank = cring.fill(pe)
                    for kk in range(TC):
                        for n in range(4):
                            T, ri = n // 2, n % 2
                            mm = pe.matmul(bank[:, kk * HW:(kk + 1) * HW], cidft[:, ri, T, kk * P:(kk + 1) * P], yf[:, n, :],
                                           start=(n == 0), stop=(n == 3))
                    mm.then_inc(cring.full, 1)

                def turn():
                    pe.wait_ge(s_v, 3)
                    bank = cring.fill(pe)
                    for half in range(2):
                        for kk in range(TC):
                            c0 = (2 * half + kk) * P
                            mm = pe.transpose(bank[:, c0:c0 + P], u[:, kk, half * P:(half + 1) * P], k.ident[:, :])
                    mm.then_inc(cring.full, 1)

                steps = {2: lambda: forward(0), 3: lambda: back(0), 4: lambda: forward(1), 5: lambda: back(1), 6: turn}
                for n in range(IMAGE):
                    tile(ORDER[n])
                    if n in steps:
                        with not_last(pe):
                            steps[n]()
                with not_last(pe):
                    pe.wait_ge(cring.free, cring.put)
                    for n in range(IMAGE, TILES):
                        tile(ORDER[n])

            @block.vector
            def _(dve):
                step = Chain(s_step, dve)
                wide = lambda r: r.unsqueeze(1).to_broadcast((P, TC, r.shape[-1]))
                v = u[:, :, 0:HW]

                def tile(n):
                    i = ORDER[n]
                    dve.wait_ge(s_x[n % BUFS], 16 * (n // BUFS + 1))
                    for h in range(2):
                        c = slice(h * WCH, (h + 1) * WCH)
                        bank = ring.read(dve)
                        dve.tensor_tensor(y[:, h, :], bank[:, :], k.gate[:, int(i >= TC), c], ALU.mult).then_inc(ring.free, 1)
                        dve.wait_ge(ring.free, ring.got)
                        ins = dve.tensor_tensor(x[:, n % BUFS, c], x[:, n % BUFS, c], y[:, h, :], ALU.add)
                    ins.then_inc(s_new, 1)

                def short_convolution():
                    xs = u[:, :, 0:3 * HW]
                    dve.wait_ge(s_zero, 1)
                    dve.wait_ge(s_tab, 11 * 16)
                    step(dve.tensor_tensor(xs, xs, wide(convw[:, 1, :]), ALU.mult))
                    step(dve.tensor_tensor(xs, xs, wide(convb[:, :]), ALU.add))
                    for buf, j in ((before, 0), (after, 2)):
                        step(dve.tensor_tensor(buf[:, :, :], buf[:, :, :], wide(convw[:, j, :]), ALU.mult))
                        ins = dve.tensor_tensor(xs, xs, buf[:, :, :], ALU.add)
                        if j == 0:
                            step(ins)
                    ins.then_inc(s_v, 1)

                def products(o):
                    for T in range(2):
                        bank = cring.read(dve)
                        xf = bank[:, :].rearrange("p (r c) -> p r c", r=2)
                        f = wide(spec[:, o, 1, :]) if T else spec[:, o, 0:5:4, :]
                        yy = yf[:, 2 * T:2 * T + 2, :]
                        step(dve.tensor_tensor(yy, xf, f, ALU.mult))
                        dve.tensor_tensor(tmp[:, :, :], xf, wide(spec[:, o, 2 + T, :]), ALU.mult).then_inc(cring.free, 1)
                        dve.wait_ge(cring.free, cring.got)
                        step(dve.tensor_tensor(yy[:, 0, :], yy[:, 0, :], tmp[:, 1, :], ALU.subtract))
                        ins = dve.tensor_tensor(yy[:, 1, :], yy[:, 1, :], tmp[:, 0, :], ALU.add)
                        if T == 0:
                            step(ins)
                    ins.then_inc(s_prod, 1)

                def gated(o):
                    bank = cring.read(dve)
                    dve.tensor_tensor(tmp[:, :, :], bank[:, :].rearrange("p (a c) -> p a c", a=2), wide(k.inv_sum[:, o, 1, :]), ALU.mult).then_inc(cring.free, 1)
                    dve.wait_ge(cring.free, cring.got)
                    step(dve.tensor_tensor(v, v, wide(k.skip[:, o, :]), ALU.mult))
                    step(dve.tensor_tensor(v, v, tmp[:, :, :], ALU.add))
                    ins = dve.tensor_tensor(v, v, u[:, :, (1 + o) * HW:(2 + o) * HW], ALU.mult)
                    if o == 1:
                        step(ins)
                        ins = dve.tensor_tensor(v, v, u[:, :, 3 * HW:4 * HW], ALU.mult)
                    ins.then_inc(s_v, 1)

                def turned():
                    bank = cring.read(dve)
                    dve.tensor_copy(k.z_hy[:, :, 0:LC], bank[:, :].rearrange("p (h t) -> p h t", h=2)).then_inc(cring.free, 1)

                steps = {1: short_convolution, 3: lambda: products(0), 4: lambda: gated(0), 5: lambda: products(1),
                         6: lambda: gated(1), 7: turned}
                for n in range(IMAGE):
                    if n in steps:
                        with not_last(dve):
                            steps[n]()
                    tile(n)
                with not_last(dve):
                    for n in range(IMAGE, TILES):
                        tile(n)


CONST_SHAPES = {n: v.shape for n, v in constants().items()}
INPUTS = ("x", "c", "ctx", "c_ctx", "norm_w", "ada_w", "ada_b", "w_in", "w_out", "na_q_gain", "na_k_gain", "na_rpb",
          "hy_conv_w", "hy_conv_b", "hy_w1", "hy_b1", "hy_w2", "hy_b2", "hy_w3", "hy_sin_freq", "hy_skip", "ret_log_rate")


def program(nc, a, out, scratch, depth=DEPTH):
    with ExitStack() as ctx:
        k = Build(nc, a, out, ctx)
        ctx.enter_context(nc.allow_non_contiguous_dma(reason="vectors of a layer go down the partitions"))
        k.spectra, k.context, k.context_columns = scratch
        sb = lambda name, shape: sbuf(ctx, nc, name, shape)
        k.ident = sb("ident", [P, P])
        k.wbuf = [sb(f"weights{i}", [P, KC, WCH]) for i in range(2)]
        k.shift, k.scale = sb("mod_shift", [P, KC, 2]), sb("mod_scale", [P, KC, 2])
        k.gate = sb("mod_gate", [P, 2, D])
        k.inv_sum = sb("inv_sum", [P, 2, 2, HW])
        k.skip = sb("hy_skip_rows", [P, 2, HW])
        s_start = ctx.enter_context(nc.semaphore("start_copied"))
        k.w_here = [k.sem(f"weights{i}_here") for i in range(2)]

        with nc.Block() as block:
            @block.sync
            def _(sp):
                sp.dma_start(k.ident[:, :], a["ident"]).then_inc(s_start, 16)
                sp.dma_start(out[0], a["x"][0]).then_inc(s_start, 16)
                sp.dma_start(k.context, a["ctx"][0]).then_inc(s_start, 16)
                sp.wait_ge(s_start, 48)

        with nc.Fori(0, depth) as layer:
            k.layer = layer
            with ExitStack() as held:
                sb = lambda name, shape: sbuf(held, nc, name, shape)
                weights_stage(k)
                k.hxT = sb("hxT", [P, KC, TOK])
                norm_stage(k)
                k.z_hy = sb("z_hyena", [P, 2, TOK])
                hyena_stage(k)
                k.z_na = sb("z_attention", [P, 4, TOK])
                attention_stage(k)
                k.z_re = sb("z_retention", [P, 2, TOK])
                retention_stage(k)
                output_stage(k)
            with nc.Block() as block:
                @block.vector
                def _(dve):
                    for s in k.sems:
                        dve.sem_clear(s)


def build(nc, arrays):
    a = {n: nc.dram_tensor("in_" + n, v.shape, F32, kind="ExternalInput").ap() for n, v in arrays.items()}
    out = nc.dram_tensor("out", (1, L, D), F32, kind="ExternalOutput").ap()
    spectra = nc.dram_tensor("filter_spectra", (2, P, 22, HW), F32, kind="Internal").ap()
    context = nc.dram_tensor("context_stream", (LC, D), F32, kind="Internal").ap()
    columns = nc.dram_tensor("context_hyena_columns", (P, TC, 4 * HW), F32, kind="Internal").ap()
    return a, out, (spectra, context, columns)


def laid_out(inputs):
    arrays = {n: np.ascontiguousarray(inputs[n]) for n in INPUTS}
    arrays["na_rpb"] = np.ascontiguousarray(np.pad(arrays["na_rpb"], ((0, 0), (0, 0), (1, 1), (GRID + 1 - KW, GRID - KW)))[..., ::-1])
    arrays.update(constants())
    return arrays


def kernel(**inputs):
    import concourse.bacc as bacc
    from concourse.bass_utils import run_bass_kernel_spmd

    arrays = laid_out(inputs)
    nc = bacc.Bacc("TRN2", target_bir_lowering=False, num_devices=1)
    a, out, scratch = build(nc, arrays)
    program(nc, a, out, scratch)
    r = run_bass_kernel_spmd(nc, [{"in_" + n: v for n, v in arrays.items()}], core_ids=[0])
    return r.results[0]["out"]
```

```python
from contextlib import ExitStack
import math

import numpy as np

import concourse.bass as bass
from concourse import mybir

F32 = mybir.dt.float32
ALU = mybir.AluOpType
ACT = mybir.ActivationFunctionType
AX = mybir.AxisListType

P = 128
D = 1024
KC = D // P
L = 1024
LC = 256
DEPTH = 2
TC = LC // P
TILES = TC + L // P
TOK = LC + L
GRID = 64
NA_HEADS, HD = 8, 64
NA_W = NA_HEADS * HD
KH, KW = 8, 16
HW = 256
FFN = 64
EMB = 17
RH = 4
RW = RH * HD
IN_W = 4 * (NA_W + HW + RW)
EPS = 1e-6
NEG = -1e30
NF = 2 * L
T2 = 16
T1 = L // T2
NR = L // P
GROUPS = 16
HT = 8
WCH = 512
HY0 = 4 * NA_W
RE0 = HY0 + 4 * HW
MAGIC = 1.5 * 2.0 ** 23
TWO_PI_HI = 6.28125
TWO_PI_LO = 2.0 * math.pi - TWO_PI_HI
PI_F = 3.1415925


def constants():
    c = {}
    c["ident"] = np.eye(P)
    t1 = np.arange(T1)[:, None]
    slot = np.arange(64)
    time = np.zeros((T1, 64, 2))
    ang = 2 * np.pi * t1 * slot / 128
    time[:, :, 0] = np.cos(ang)
    time[:, :, 1] = -np.sin(ang)
    time[:, 0, 0] = 1.0
    time[:, 0, 1] = (-1.0) ** t1[:, 0]
    time = time.reshape(T1, P)
    both = np.zeros((P, 2, P))
    for b in range(2):
        both[b::2, b] = time
    c["dft_time"] = both
    c["idft_time"] = both.transpose(2, 1, 0)
    fine = np.zeros((P, 2, GROUPS, 64))
    inv = np.zeros((P, HT, 2, P))
    t2 = np.arange(T2)
    for g in range(GROUPS):
        for s in range(4):
            sl = 4 * g + s
            for f2 in range(16):
                col = s * 16 + f2
                irow = 64 * (g % 2) + col
                w = 2.0 / NF
                if sl > 0:
                    th = 2 * np.pi * t2 * (sl + 128 * f2) / NF
                    r0, r1 = s * 32 + t2, s * 32 + 16 + t2
                    fine[r0, 0, g, col], fine[r1, 0, g, col] = np.cos(th), np.sin(th)
                    fine[r0, 1, g, col], fine[r1, 1, g, col] = -np.sin(th), np.cos(th)
                    inv[irow, g // 2, 0, r0], inv[irow, g // 2, 0, r1] = w * np.cos(th), w * np.sin(th)
                    inv[irow, g // 2, 1, r0], inv[irow, g // 2, 1, r1] = -w * np.sin(th), w * np.cos(th)
                else:
                    f = 128 * f2 if f2 < 8 else 64 + 128 * (f2 - 8)
                    r = t2 if f2 < 8 else 16 + t2
                    th = 2 * np.pi * t2 * f / NF
                    if f2 == 0:
                        fine[r, 0, g, col], fine[r, 1, g, col] = 1.0, np.cos(np.pi * t2)
                        inv[irow, 0, 0, r], inv[irow, 0, 1, r] = 1.0 / NF, np.cos(np.pi * t2) / NF
                    else:
                        fine[r, 0, g, col], fine[r, 1, g, col] = np.cos(th), -np.sin(th)
                        inv[irow, 0, 0, r], inv[irow, 0, 1, r] = w * np.cos(th), -w * np.sin(th)
    c["dft_fine"] = fine
    c["idft_fine"] = inv
    special = np.zeros((P, 2, 64))
    special[:, 0] = fine[:, 0, 0]
    special[:, 0, 0] = fine[:, 1, 0, 0]
    special[:, 1] = fine[:, 1, 0]
    special[:, 1, 0] = 0.0
    c["fine_special"] = special
    t = np.arange(LC)
    f = np.arange(LC)
    th = 2 * np.pi * np.outer(t, f) / (2 * LC)
    re, im = np.cos(th), -np.sin(th)
    im[:, 0] = np.cos(np.pi * t)
    h, g = re.copy(), im.copy()
    h[:, 0] = im[:, 0]
    g[:, 0] = 0.0
    rows = lambda m: m.reshape(2, P, -1).transpose(1, 0, 2)
    c["cdft"] = np.stack([rows(re), rows(im)], 1)
    c["cdft_special"] = np.stack([rows(h)[:, :, :P], rows(g)[:, :, :P]], 1)
    w = np.full(LC, 2.0 / (2 * LC))
    w[0] = 1.0 / (2 * LC)
    c["cidft"] = np.stack([rows(re.T * w[:, None]), rows(im.T * w[:, None])], 1)
    px = (NR * np.arange(P)[None] + np.arange(NR)[:, None]).ravel()
    emb, dec = [], []
    for n, pos in ((L, px), (LC, np.arange(LC))):
        tn = np.linspace(0.0, 1.0, n).astype(np.float32).astype(np.float64)[pos][:, None]
        om = 2 * np.pi * pos[:, None] / n
        bands = np.linspace(1e-4, 7.0, 8).astype(np.float32).astype(np.float64)[None]
        emb.append(np.concatenate([tn, np.cos(bands * om), -np.sin(bands * om)], 1))
        deltas = np.abs(np.linspace(math.log(1e-2) / 1.5, math.log(1e-2) / 0.3, HW))
        dec.append(np.exp(-tn * deltas))
    c["emb"] = np.concatenate(emb, 0).T
    c["decay"] = np.concatenate(dec, 0).reshape(TILES, P, HW).transpose(1, 0, 2)
    tok = np.arange(L)
    fr = 10000.0 ** (-np.arange(16) / 16.0)
    ang = np.stack([tok // GRID, tok % GRID], 1)[:, :, None] * fr
    rope = np.zeros((TOK, 2, 2, 16))
    rope[:LC, 0] = 1.0
    rope[LC:, 0] = np.cos(ang)
    rope[LC:, 1] = np.sin(ang)
    c["rope"] = rope.reshape(TILES, P, 64).transpose(1, 0, 2)
    l, j = np.arange(P)[:, None], np.arange(P)[None]
    c["dist"] = np.stack([np.maximum(j - l, 0), np.maximum(l - j, 0), (j >= l) * 0.125, (l >= j) * 0.125], 1)
    c["age"] = np.broadcast_to(np.stack([np.arange(P) + 1, P - np.arange(P)])[None], (P, 2, P))
    c["rest"] = np.stack([P - 1 - np.arange(P), np.arange(P)], 1)[:, :, None].repeat(RH, 2)
    cq, ck = np.arange(GRID)[:, None], np.arange(GRID)[None]
    cs = np.clip(cq - KW // 2, 0, GRID - KW)
    ok = (ck >= cs) & (ck < cs + KW)
    c["colmask"] = np.concatenate([np.where(ok, 0.0, NEG)] * 2, 0)
    return {k: np.ascontiguousarray(v, np.float32) for k, v in c.items()}


class Ring:

    def __init__(self, name, banks, sem):
        self.banks, self.full, self.free = banks, sem(name + "_full"), sem(name + "_free")
        self.put, self.got = 0, 0

    def fill(self, pe):
        if self.put >= len(self.banks):
            pe.wait_ge(self.free, self.put - len(self.banks) + 1)
        self.put += 1
        return self.banks[(self.put - 1) % len(self.banks)]

    def read(self, eng):
        eng.wait_ge(self.full, self.got + 1)
        self.got += 1
        return self.banks[(self.got - 1) % len(self.banks)]


class Chain:

    def __init__(self, sem, eng=None):
        self.sem, self.n, self.eng = sem, 0, eng

    def __call__(self, ins):
        self.n += 1
        ins.then_inc(self.sem, 1)
        self.eng.wait_ge(self.sem, self.n)


class Build:

    def __init__(self, nc, a, out, ctx):
        self.nc, self.a, self.out, self.ctx = nc, a, out, ctx
        self.sems = []
        self.all_psum = ctx.enter_context(nc.psum_tensor("psum", [P, 8 * 512], F32))
        self.psum = [self.all_psum[:, i * 512:(i + 1) * 512] for i in range(8)]

    def sem(self, name):
        s = self.ctx.enter_context(self.nc.semaphore(name))
        self.sems.append(s)
        return s

    def of_layer(self, ap):
        return ap[bass.ds(self.layer, 1)]


def R32(ap):
    return ap.bitcast(mybir.dt.float32r)


def sbuf(ctx, nc, name, shape, side="left"):
    return ctx.enter_context(nc.sbuf_tensor(name, shape, F32, side=side))


def weight_chunk(k, n):
    def cols(w, c0, width=WCH, at=0):
        v = k.of_layer(w)[:, :, c0:c0 + width].rearrange("a (k p) n -> p (a k) n", p=P)
        return (slice(at, at + width), v)

    a = k.a
    if n < 6:
        return [cols(a["ada_w"], n * WCH)]
    n -= 6
    if n < 2:
        return [cols(a["w_in"], HY0 + n * WCH)]
    n -= 2
    if n < 4:
        return [cols(a["w_in"], m * NA_W + n * P, P, m * P) for m in range(4)]
    n -= 4
    if n < 2:
        return [cols(a["w_in"], RE0 + n * WCH)]
    return [cols(a["w_out"], (n - 2) * WCH)]


def load_weights(k, eng, n):
    for where, view in weight_chunk(k, n):
        eng.dma_start(k.wbuf[n % 2][:, :, where], view).then_inc(k.w_here[n % 2], 16)


def wait_weights(k, eng, n):
    parts = sum(4 if 8 <= m < 12 else 1 for m in range(n % 2, n + 1, 2))
    eng.wait_ge(k.w_here[n % 2], 16 * parts)
    return k.wbuf[n % 2]


class Split:

    def __init__(self, k, name, w_high, buffers):
        self.k, self.w_high, self.buffers = k, w_high, buffers
        self.s_wh, self.s_w, self.s_xh, self.s_x = (k.sem(name + n) for n in ("_w_high", "_w_split", "_x_high", "_x_split"))
        self.n = {s: 0 for s in ("wh", "wl", "w", "xh", "xl", "x")}

    def weights_high(self, act, n, chunks=range(KC)):
        w = wait_weights(self.k, act, n)
        for kc in chunks:
            act.activation(R32(self.w_high[:, kc, :]), w[:, kc, :], ACT.Copy).then_inc(self.s_wh, 1)

    def weights_low(self, dve, n, chunks=range(KC)):
        w = wait_weights(self.k, dve, n)
        for kc in chunks:
            self.n["wl"] += 1
            dve.wait_ge(self.s_wh, self.n["wl"])
            dve.tensor_tensor(R32(self.k.w_low[:, n % 2, kc, :]), w[:, kc, :], self.w_high[:, kc, :], ALU.subtract).then_inc(self.s_w, 1)

    def x_high(self, act, pieces):
        high, _ = self.buffers[self.n["xh"] % len(self.buffers)]
        self.n["xh"] += 1
        for chunks, src in pieces:
            ins = act.activation(R32(high[:, chunks, :]), src, ACT.Copy)
        ins.then_inc(self.s_xh, 1)

    def x_low(self, dve, pieces):
        high, low = self.buffers[self.n["xl"] % len(self.buffers)]
        self.n["xl"] += 1
        dve.wait_ge(self.s_xh, self.n["xl"])
        for chunks, src in pieces:
            ins = dve.tensor_tensor(R32(low[:, chunks, :]), src, high[:, chunks, :], ALU.subtract)
        ins.then_inc(self.s_x, 1)

    def tile(self, pe):
        self.n["x"] += 1
        pe.wait_ge(self.s_x, self.n["x"])
        return self.buffers[(self.n["x"] - 1) % len(self.buffers)]

    def product(self, pe, bank, x, w_low, first=False):
        high = self.w_high
        for kc in range(KC):
            if first:
                self.n["w"] += 1
                pe.wait_ge(self.s_w, self.n["w"])
            xh, xl = (part[:, kc, :] for part in x)
            pe.matmul(bank, R32(xh), R32(high[:, kc, :]), start=(kc == 0), stop=False)
            pe.matmul(bank, R32(xh), R32(w_low[:, kc, :]), start=False, stop=False)
            mm = pe.matmul(bank, R32(xl), R32(high[:, kc, :]), start=False, stop=(kc == KC - 1))
        return mm


def weights_stage(k):
    nc, a = k.nc, k.a
    with ExitStack() as mem:
        sb = lambda name, shape: sbuf(mem, nc, name, shape)
        time = sb("s1_time", [P, 2, P])
        fine = sb("s1_fine", [P, 2, GROUPS, 64])
        special = sb("s1_special", [P, 2, 64])
        cdft = sb("s1_cdft", [P, 2, 2, LC])
        cspecial = sb("s1_cspecial", [P, 2, 2, P])
        emb = sb("s1_emb", [EMB, TOK])
        decay = sb("s1_decay", [P, TILES, HW])
        w1, w2 = sb("s1_w1", [EMB, FFN]), sb("s1_w2", [FFN, FFN])
        w3 = sb("s1_w3", [FFN, 4 * HW])
        vec = sb("s1_vec", [FFN, 4])
        arg, turns, hid = sb("s1_arg", [FFN, TOK]), sb("s1_turns", [FFN, TOK]), sb("s1_hid", [FFN, TOK])
        taps = sb("s1_taps", [P, TILES, 2, HW])
        even, odd = sb("s1_even", [P, TILES, HW]), sb("s1_odd", [P, TILES, HW])
        mag = taps[:, :, 0, :]
        ones = sb("s1_ones", [P, P])
        part1, part2 = sb("s1_part1", [P, T2, HW]), sb("s1_part2", [P, GROUPS, HW])
        spec = sb("s1_spec", [P, 22, HW])
        cond = sb("s1_cond", [P, KC, 2])
        condb = sb("s1_condb", [P, 2, KC, P])
        gate_b, gate = sb("s1_gate_b", [P, D]), sb("s1_gate", [P, 2, D])
        ada_b = sb("s1_ada_b", [P, 2 * KC])
        normw = sb("s1_normw", [P, KC])

        s_tab, s_mod, s_w = k.sem("s1_tables_here"), k.sem("s1_mod_inputs_here"), k.sem("s1_mlp_weights_here")
        ra, rv = Ring("s1_act", k.psum[0:4], k.sem), Ring("s1_dve", k.psum[4:8], k.sem)
        s_arg, s_sin = k.sem("s1_arg"), k.sem("s1_sin")
        s_step, s_taps = k.sem("s1_dve_step"), k.sem("s1_magnitudes")
        s_both, s_even, s_odd = k.sem("s1_taps_ready"), k.sem("s1_even"), k.sem("s1_odd")
        s_shuf, s_spill = [k.sem(f"s1_shuffled{T}") for T in range(HT)], k.sem("s1_spilled")
        s_silu, s_condb = k.sem("s1_silu"), k.sem("s1_cond_spread")
        base = [0, 19, 36, 55, 72]
        used = [4, 8, 21, 22, 36, 38]

        with nc.Block() as block:
            @block.tensor
            def _(pe):
                def mlp(w, x):
                    for c0 in range(0, TOK, 512):
                        n = min(512, TOK - c0)
                        bank = rv.fill(pe)
                        pe.matmul(bank[0:FFN, 0:n], w[:, :], x[:, c0:c0 + n], start=True, stop=True).then_inc(rv.full, 1)

                def modulation(n):
                    w = wait_weights(k, pe, n)
                    if n < 4:
                        bank = rv.fill(pe)
                        for m in range(4):
                            for kc in range(KC):
                                mm = pe.matmul(bank[:, 2 * m:2 * m + 2], w[:, kc, m * P:(m + 1) * P], cond[:, kc, :],
                                               start=(kc == 0), stop=(kc == KC - 1))
                        mm.then_inc(rv.full, 1)
                    else:
                        pe.wait_ge(s_condb, 2)
                        for c in range(2):
                            bank = rv.fill(pe)
                            for kc in range(KC):
                                mm = pe.matmul(bank[:, :], condb[:, c, kc, :], w[:, kc, :], start=(kc == 0), stop=(kc == KC - 1))
                            mm.then_inc(rv.full, 1)
                    assert rv.put == used[n]

                pe.wait_ge(s_w, 7 * 16)
                mlp(w1, emb)
                pe.wait_ge(s_silu, 1)
                modulation(0)
                pe.wait_ge(s_sin, 1)
                mlp(w2, hid)
                modulation(1)
                pe.wait_ge(s_sin, 2)
                pe.wait_ge(s_tab, 6 * 16)
                for o in range(2):
                    for i in range(TILES):
                        bank = rv.fill(pe)
                        pe.matmul(bank[:, :], hid[:, i * P:(i + 1) * P], w3[:, o * 512:(o + 1) * 512],
                                  start=True, stop=True).then_inc(rv.full, 1)
                    for part, x in enumerate((even, odd)):
                        n = 2 * o + part
                        pe.wait_ge((s_even, s_odd)[part], o + 1)
                        assert ra.put == base[n]
                        for b in range(2):
                            for q in range(4):
                                bank = ra.fill(pe)
                                pe.matmul(bank[:, :], time[:, b, :], x[:, 2 * q:2 * q + 2, :],
                                          start=True, stop=True).then_inc(ra.full, 1)
                        if part == 0:
                            pe.wait_ge(s_taps, o + 1)
                            for tiles in (range(0, 8), range(8, 10)):
                                bank = rv.fill(pe)
                                for i in tiles:
                                    mm = pe.matmul(bank[:, 0:HW], ones[:, :], mag[:, i, :], start=(i == tiles[0]), stop=(i == tiles[-1]))
                                mm.then_inc(rv.full, 1)
                        bank = ra.fill(pe)
                        for T in range(2):
                            for kk in range(2):
                                table = cspecial[:, 1, kk, :] if part and T == 0 else cdft[:, part, kk, T * P:(T + 1) * P]
                                mm = pe.matmul(bank[:, T * HW:(T + 1) * HW], table, x[:, 8 + kk, :], start=(kk == 0), stop=(kk == 1))
                        mm.then_inc(ra.full, 1)
                        if part == 0:
                            bank = ra.fill(pe)
                            for kk in range(2):
                                mm = pe.matmul(bank[:, 0:HW], cspecial[:, 0, kk, :], x[:, 8 + kk, :], start=(kk == 0), stop=(kk == 1))
                            mm.then_inc(ra.full, 1)
                        modulation(n + 2)
                        for T in range(HT):
                            pe.wait_ge(s_shuf[T], 32 * (n + 1))
                            bank = ra.fill(pe)
                            for h in range(2):
                                g = 2 * T + h
                                lhs = special[:, 1, :] if part and g == 0 else fine[:, part, g, :]
                                mm = pe.matmul(bank[64 * h:64 * h + 64, 0:HW], lhs, part2[:, g, :], start=True, stop=True)
                            mm.then_inc(ra.full, 1)
                        if part == 0:
                            bank = ra.fill(pe)
                            pe.matmul(bank[0:64, 0:HW], special[:, 0, :], part2[:, 0, :], start=True, stop=True)
                            pe.matmul(bank[64:128, 0:HW], fine[:, 0, 1, :], part2[:, 1, :], start=True, stop=True).then_inc(ra.full, 1)

            @block.sync
            def _(sp):
                this = k.of_layer
                sp.dma_start(w1[:, :], this(a["hy_w1"]).rearrange("a k n -> (a k) n")).then_inc(s_w, 16)
                sp.dma_start(emb[:, :], a["emb"]).then_inc(s_w, 16)
                sp.dma_start(w2[:, :], this(a["hy_w2"]).rearrange("a k n -> (a k) n")).then_inc(s_w, 16)
                sp.dma_start(vec[:, 0:1], this(a["hy_b1"]).rearrange("a n -> n a")).then_inc(s_w, 16)
                sp.dma_start(vec[:, 1:2], this(a["hy_b2"]).rearrange("a n -> n a")).then_inc(s_w, 16)
                sp.dma_start(vec[:, 2:4], this(a["hy_sin_freq"]).rearrange("a f n -> n (a f)")).then_inc(s_w, 16)
                sp.dma_start(w3[:, :], this(a["hy_w3"]).rearrange("a k n -> (a k) n")).then_inc(s_w, 16)
                sp.dma_start(cond[:, :, 0], a["c_ctx"].rearrange("(k p) -> p k", p=P)).then_inc(s_mod, 16)
                sp.dma_start(cond[:, :, 1], a["c"].rearrange("a (k p) -> p (a k)", p=P)).then_inc(s_mod, 16)
                sp.dma_start(ada_b[:, :], this(a["ada_b"])[:, 0:2 * D].rearrange("a (k p) -> p (a k)", p=P)).then_inc(s_mod, 16)
                sp.dma_start(normw[:, :], this(a["norm_w"]).rearrange("a (k p) -> p (a k)", p=P)).then_inc(s_mod, 16)
                load_weights(k, sp, 0)
                sp.dma_start(gate_b[:, :], this(a["ada_b"])[:, 2 * D:3 * D].to_broadcast((P, D))).then_inc(s_mod, 16)
                sp.dma_start(decay[:, :, :], a["decay"]).then_inc(s_tab, 16)
                sp.dma_start(time[:, :, :], a["dft_time"]).then_inc(s_tab, 16)
                sp.dma_start(fine[:, :, :, :], a["dft_fine"]).then_inc(s_tab, 16)
                sp.dma_start(special[:, :, :], a["fine_special"]).then_inc(s_tab, 16)
                sp.dma_start(cdft[:, :, :, :], a["cdft"]).then_inc(s_tab, 16)
                sp.dma_start(cspecial[:, :, :, :], a["cdft_special"]).then_inc(s_tab, 16)
                load_weights(k, sp, 1)
                for m in (2, 3):
                    sp.wait_ge(rv.full, used[m - 2])
                    load_weights(k, sp, m)
                for n in range(4):
                    sp.wait_ge(ra.free, base[n] + 8)
                    if n >= 1:
                        sp.wait_ge(ra.full, base[n])
                    for g in range(GROUPS):
                        sp.dma_start(part2[:, g, :], part1[8 * g:8 * g + 8, :, :]).then_inc(s_shuf[g // 2], 16)
                    sp.wait_ge(rv.full, used[n + 2])
                    load_weights(k, sp, n + 4)
                    if n % 2 == 1:
                        sp.wait_ge(ra.free, base[n + 1])
                        sp.dma_start(k.spectra[n // 2], spec[:, :, :]).then_inc(s_spill, 16)
                sp.wait_ge(rv.free, used[5])
                sp.dma_start(k.gates, gate[0:1, :, :]).then_inc(s_spill, 16)
                sp.wait_ge(s_spill, 48)

            @block.gpsimd
            def _(pool):
                for o in range(2):
                    pool.wait_ge(s_both, o + 1)
                    pool.tensor_tensor(odd[:, :, :], taps[:, :, 0, :], taps[:, :, 1, :], ALU.subtract).then_inc(s_odd, 1)

            @block.scalar
            def _(act):
                act.wait_ge(s_mod, 5 * 16)
                act.activation(cond[:, :, :], cond[:, :, :], ACT.Silu).then_inc(s_silu, 1)
                for n in range(2):
                    act.wait_ge(s_arg, n + 1)
                    if n == 1:
                        act.wait_ge(rv.full, 7)
                    act.activation(hid[:, :], arg[:, :], ACT.Sin).then_inc(s_sin, 1)
                for n in range(4):
                    part = n % 2
                    if n >= 1:
                        for T in range(HT):
                            act.wait_ge(s_shuf[T], 32 * n)
                    for b in range(2):
                        for q in range(4):
                            bank = ra.read(act)
                            dst = part1[:, 8 * b + 2 * q:8 * b + 2 * q + 2, :]
                            act.activation(dst, bank[:, :].rearrange("p (a c) -> p a c", a=2), ACT.Copy).then_inc(ra.free, 1)
                    if n == 2:
                        act.wait_ge(s_spill, 16)
                    first = (17, 19)[part]
                    act.activation(spec[:, first:first + 2, :], ra.read(act)[:, :].rearrange("p (a c) -> p a c", a=2), ACT.Copy).then_inc(ra.free, 1)
                    if part == 0:
                        act.activation(spec[:, 21, :], ra.read(act)[:, 0:HW], ACT.Copy).then_inc(ra.free, 1)
                    for T in range(HT):
                        act.activation(spec[:, 8 * part + T, :], ra.read(act)[:, 0:HW], ACT.Copy).then_inc(ra.free, 1)
                    if part == 0:
                        act.activation(spec[:, 16, :], ra.read(act)[:, 0:HW], ACT.Copy).then_inc(ra.free, 1)

            @block.vector
            def _(dve):
                step = Chain(s_step, dve)

                def sin_argument(n):
                    for c0 in range(0, TOK, 512):
                        w = min(512, TOK - c0)
                        bank = rv.read(dve)
                        dve.tensor_scalar(arg[:, c0:c0 + w], bank[0:FFN, 0:w], vec[:, n:n + 1], vec[:, 2 + n:3 + n],
                                          ALU.add, ALU.mult).then_inc(rv.free, 1)
                    dve.wait_ge(rv.free, rv.got)
                    step(dve.tensor_scalar(turns[:, :], arg[:, :], 1.0 / (2 * math.pi), MAGIC, ALU.mult, ALU.add))
                    step(dve.tensor_scalar(turns[:, :], turns[:, :], MAGIC, None, ALU.subtract))
                    step(dve.scalar_tensor_tensor(out=arg[:, :], in0=turns[:, :], scalar=-TWO_PI_HI, in1=arg[:, :], op0=ALU.mult, op1=ALU.add))
                    step(dve.scalar_tensor_tensor(out=arg[:, :], in0=turns[:, :], scalar=-TWO_PI_LO, in1=arg[:, :], op0=ALU.mult, op1=ALU.add))
                    dve.tensor_scalar(arg[:, :], arg[:, :], PI_F, -PI_F, ALU.min, ALU.max).then_inc(s_arg, 1)

                def modulation(n):
                    if n < 4:
                        dst = (k.shift if n < 2 else k.scale)[:, 4 * (n % 2):4 * (n % 2) + 4, :]
                        both = lambda x, c0: x[:, c0:c0 + 4].unsqueeze(2).to_broadcast((P, 4, 2))
                        bank = rv.read(dve)
                        dve.tensor_tensor(dst, bank[:, 0:8].rearrange("p (m c) -> p m c", c=2), both(ada_b, 4 * n), ALU.add).then_inc(rv.free, 1)
                        if n >= 2:
                            dve.wait_ge(rv.free, rv.got)
                            step(dve.scalar_tensor_tensor(out=dst, in0=dst, scalar=1.0, in1=both(normw, 4 * (n - 2)), op0=ALU.add, op1=ALU.mult))
                    else:
                        c0 = (n - 4) * 512
                        for c in range(2):
                            bank = rv.read(dve)
                            dve.tensor_tensor(gate[:, c, c0:c0 + 512], bank[:, :], gate_b[:, c0:c0 + 512], ALU.add).then_inc(rv.free, 1)

                dve.memset(ones[:, :], 1.0).then_inc(s_step, 1)
                step.n += 1
                dve.wait_ge(s_w, 7 * 16)
                dve.wait_ge(s_mod, 5 * 16)
                sin_argument(0)
                dve.wait_ge(s_silu, 1)
                for c in range(2):
                    dve.tensor_copy(condb[:, c, :, :], cond[:, :, c].unsqueeze(2).to_broadcast((P, KC, P))).then_inc(s_condb, 1)
                modulation(0)
                dve.wait_ge(s_sin, 1)
                sin_argument(1)
                modulation(1)
                dve.wait_ge(s_tab, 6 * 16)
                for o in range(2):
                    for i in range(TILES):
                        bank = rv.read(dve)
                        dve.tensor_tensor(taps[:, i, :, :], bank[:, :].rearrange("p (w c) -> p w c", w=2),
                                          decay[:, i, :].unsqueeze(1).to_broadcast((P, 2, HW)), ALU.mult).then_inc(rv.free, 1)
                    dve.wait_ge(rv.free, rv.got)
                    step(dve.memset(taps[0:1, 0, 1, :], 0.0))
                    if o == 1:
                        dve.wait_ge(ra.full, base[2])
                    dve.memset(taps[0:1, 8, 1, :], 0.0).then_inc(s_both, 1)
                    dve.wait_ge(s_both, o + 1)
                    fwd, bwd = taps[:, :, 0, :], taps[:, :, 1, :]
                    dve.tensor_tensor(even[:, :, :], fwd, bwd, ALU.add).then_inc(s_even, 1)
                    dve.wait_ge(s_even, o + 1)
                    dve.wait_ge(s_odd, o + 1)
                    for x in (fwd, bwd):
                        step(dve.scalar_tensor_tensor(out=x, in0=x, scalar=-1.0, in1=x, op0=ALU.mult, op1=ALU.max))
                    dve.tensor_tensor(mag, fwd, bwd, ALU.add).then_inc(s_taps, 1)
                    for which in range(2):
                        bank = rv.read(dve)
                        dve.reciprocal(k.inv_sum[:, o, which, :], bank[:, 0:HW]).then_inc(rv.free, 1)
                    modulation(2 + 2 * o)
                    modulation(3 + 2 * o)


def stream_tile(k, i):
    return k.context[i * P:(i + 1) * P, :] if i < TC else k.out[0, (i - TC) * P:(i - TC + 1) * P, :]


def norm_stage(k):
    nc = k.nc
    BUFS = 3
    with ExitStack() as mem:
        x = sbuf(mem, nc, "s2_x", [P, BUFS, D])
        square = sbuf(mem, nc, "s2_square", [P, D])
        rms = sbuf(mem, nc, "s2_rms", [P, 2, TILES])
        inv = sbuf(mem, nc, "s2_inv", [P, TILES])
        eps = sbuf(mem, nc, "s2_eps", [P, 1])
        tmp = sbuf(mem, nc, "s2_scaled", [P, 2, 512])
        s_x = [k.sem(f"s2_x{b}_here") for b in range(BUFS)]
        s_sum, s_rms, s_inv, s_scaled = k.sem("s2_squares"), k.sem("s2_rms"), k.sem("s2_inverse"), k.sem("s2_x_scaled")
        s_eps, s_step = k.sem("s2_eps"), k.sem("s2_dve_step")
        ra, rv = Ring("s2_act", k.psum[0:4], k.sem), Ring("s2_dve", k.psum[4:8], k.sem)
        with nc.Block() as block:
            @block.sync
            def _(sp):
                for i in range(TILES):
                    if i >= BUFS:
                        sp.wait_ge(ra.full, i - BUFS + 1)
                    sp.dma_start(x[:, i % BUFS, :], stream_tile(k, i)).then_inc(s_x[i % BUFS], 16)

            @block.scalar
            def _(act):
                def transposed(i):
                    bank = ra.read(act)
                    c = int(i >= TC)
                    for m in range(4):
                        ins = act.activation(k.hxT[:, 4 + m, i * P:(i + 1) * P], bank[:, m * P:(m + 1) * P], ACT.Identity,
                                             bias=k.shift[:, 4 + m, c:c + 1], scale=k.scale[:, 4 + m, c:c + 1])
                    ins.then_inc(ra.free, 1)

                act.wait_ge(s_eps, 1)
                for i in range(TILES):
                    act.wait_ge(s_x[i % BUFS], 16 * (i // BUFS + 1))
                    if i >= 1:
                        act.wait_ge(s_sum, i)
                    act.activation(square[:, :], x[:, i % BUFS, :], ACT.Square, accum_out=rms[:, 0, i:i + 1]).then_inc(s_sum, 1)
                    act.wait_ge(s_sum, i + 1)
                    act.activation(rms[:, 1, i:i + 1], rms[:, 0, i:i + 1], ACT.Sqrt, bias=eps[:, 0:1], scale=1.0 / D).then_inc(s_rms, 1)
                    if i >= 1:
                        transposed(i - 1)
                transposed(TILES - 1)

            @block.vector
            def _(dve):
                dve.memset(eps[:, :], EPS).then_inc(s_eps, 1)
                step = Chain(s_step, dve)

                def transposed(i):
                    bank = rv.read(dve)
                    c = int(i >= TC)
                    per = lambda v: v[:, 0:4, c].unsqueeze(2).to_broadcast((P, 4, P))
                    four = lambda v: v.rearrange("p (m t) -> p m t", m=4)
                    dve.tensor_tensor(four(tmp[:, i % 2, :]), four(bank[:, :]), per(k.scale), ALU.mult).then_inc(rv.free, 1)
                    dve.wait_ge(rv.free, rv.got)
                    dve.tensor_tensor(k.hxT[:, 0:4, i * P:(i + 1) * P], four(tmp[:, i % 2, :]), per(k.shift), ALU.add).then_inc(s_step, 1)

                for i in range(TILES):
                    dve.wait_ge(s_rms, i + 1)
                    dve.reciprocal(inv[:, i:i + 1], rms[:, 1, i:i + 1]).then_inc(s_inv, 1)
                    dve.wait_ge(s_inv, i + 1)
                    dve.tensor_scalar(x[:, i % BUFS, :], x[:, i % BUFS, :], inv[:, i:i + 1], None, ALU.mult).then_inc(s_scaled, 1)
                    if i >= 1:
                        transposed(i - 1)
                transposed(TILES - 1)

            @block.tensor
            def _(pe):
                for i in range(TILES):
                    pe.wait_ge(s_scaled, i + 1)
                    for half, ring in enumerate((rv, ra)):
                        bank = ring.fill(pe)
                        for m in range(4):
                            c0 = (4 * half + m) * P
                            ins = pe.transpose(bank[:, m * P:(m + 1) * P], x[:, i % BUFS, c0:c0 + P], k.ident[:, :])
                        ins.then_inc(ring.full, 1)


def hyena_stage(k):
    nc, a_in = k.nc, k.a
    with ExitStack() as mem:
        sb = lambda name, shape: sbuf(mem, nc, name, shape)
        time, itime = sb("s3_time", [P, 2, P]), sb("s3_itime", [P, 2, P])
        fine, ifine = sb("s3_fine", [P, 2, GROUPS, 64]), sb("s3_ifine", [P, HT, 2, P])
        aux = sb("s3_aux", [P, 17, HW])
        tmp = sb("s3_tmp", [P, 4, HW])
        v = sb("s3_v", [P, NR, 3 * HW])
        gh = sb("s3_gate", [P, NR, HW])
        uc = sb("s3_context_columns", [P, TC, 4 * HW])
        parts = sb("s3_parts", [P, 2, T2, HW])
        part1, part2 = parts[:, 0], parts[:, 1]
        raw = parts[:, :, :, :].rearrange("p n t c -> p (n t c)")[:, 0:(NR + 2) * 3 * HW].rearrange("p (r c) -> p r c", r=NR + 2)
        convw = aux[:, 0:9, :].rearrange("p (j g) c -> p j (g c)", j=3)
        convb = tmp[:, 0:3, :].rearrange("p g c -> p (g c)")

        ra, rv = Ring("s3_act", k.psum[0:4], k.sem), Ring("s3_dve", k.psum[4:8], k.sem)
        s_tab, s_conv, s_zero, s_shift = k.sem("s3_tables_here"), k.sem("s3_conv_weights_here"), k.sem("s3_zeroed"), [k.sem(f"s3_shifted{n}") for n in range(2)]
        s_scaled, s_step, s_ready = k.sem("s3_neighbours_scaled"), k.sem("s3_dve_step"), k.sem("s3_conv_done")
        s_there, s_back = [k.sem(f"s3_shuffled{T}") for T in range(HT)], k.sem("s3_shuffled_back")
        s_spec, s_prod = k.sem("s3_spectrum_here"), k.sem("s3_products")
        s_spill = k.sem("s3_context_columns_stored")
        s_skip, s_y = k.sem("s3_skip_applied"), k.sem("s3_y_ready")
        PROJECTIONS = [(n, i) for n in (6, 7) for i in range(NR)] + [(n, NR + i) for n in (6, 7) for i in range(TC)]
        A = [20, 36]
        with nc.Block() as block:
            @block.tensor
            def _(pe):
                for n, i in PROJECTIONS:
                    w = wait_weights(k, pe, n)
                    bank = ra.fill(pe)
                    for kc in range(KC):
                        lhs = k.hxT[:, kc, LC + i:TOK:NR] if i < NR else k.hxT[:, kc, (i - NR) * P:(i - NR + 1) * P]
                        mm = pe.matmul(bank[:, :], lhs, w[:, kc, :], start=(kc == 0), stop=(kc == KC - 1))
                    mm.then_inc(ra.full, 1)
                pe.wait_ge(s_tab, 4 * 16)
                for o in range(2):
                    pe.wait_ge(s_ready if o == 0 else s_y, 1)
                    for b in range(2):
                        for q in range(4):
                            bank = ra.fill(pe)
                            pe.matmul(bank[:, :], time[:, b, :], v[:, 2 * q:2 * q + 2, 0:HW],
                                      start=True, stop=True).then_inc(ra.full, 1)
                    for T in range(HT):
                        pe.wait_ge(s_there[T], 32 * (o + 1))
                        bank = rv.fill(pe)
                        for h in range(2):
                            for ri in range(2):
                                mm = pe.matmul(bank[64 * h:64 * h + 64, ri * HW:(ri + 1) * HW], fine[:, ri, 2 * T + h, :],
                                               part2[:, 2 * T + h, :], start=True, stop=True)
                        mm.then_inc(rv.full, 1)
                    for T in range(0, HT, 2):
                        pe.wait_ge(s_prod, HT * o + T + 2)
                        banks = [ra.fill(pe), ra.fill(pe)]
                        for t in range(2):
                            for ri in range(2):
                                for h in range(2):
                                    y = part1[64 * h:64 * h + 64, 2 * (T + t) + ri, :]
                                    mm = pe.matmul(banks[h][:, t * HW:(t + 1) * HW], ifine[64 * h:64 * h + 64, T + t, ri, :], y,
                                                   start=(ri == 0), stop=(ri == 1))
                                    if t == 1 and ri == 1:
                                        mm.then_inc(ra.full, 1)
                    pe.wait_ge(s_back, 16 * GROUPS * (o + 1))
                    for q in range(4):
                        bank = rv.fill(pe)
                        for b in range(2):
                            y = part1[:, 8 * b + 2 * q:8 * b + 2 * q + 2, :]
                            mm = pe.matmul(bank[:, :], itime[:, b, :], y, start=(b == 0), stop=(b == 1))
                        mm.then_inc(rv.full, 1)
                pe.wait_ge(s_y, 2)
                for half in range(2):
                    for q in range(2):
                        bank = ra.fill(pe)
                        for m in range(4):
                            mm = pe.transpose(bank[:, m * P:(m + 1) * P], v[:, 4 * q + m, half * P:(half + 1) * P], k.ident[:, :])
                        mm.then_inc(ra.full, 1)

            @block.sync
            def _(sp):
                this = k.of_layer
                sp.dma_start(convw, this(a_in["hy_conv_w"]).rearrange("a j c -> a (j c)").to_broadcast((P, 9 * HW))).then_inc(s_conv, 16)
                sp.dma_start(convb, this(a_in["hy_conv_b"]).to_broadcast((P, 3 * HW))).then_inc(s_conv, 16)
                sp.dma_start(k.skip[:, :, :], this(a_in["hy_skip"]).rearrange("a o c -> a (o c)").to_broadcast((P, 2 * HW))).then_inc(s_conv, 16)
                sp.dma_start(time[:, :, :], a_in["dft_time"]).then_inc(s_tab, 16)
                sp.dma_start(itime[:, :, :], a_in["idft_time"]).then_inc(s_tab, 16)
                sp.dma_start(fine[:, :, :, :], a_in["dft_fine"]).then_inc(s_tab, 16)
                sp.dma_start(ifine[:, :, :, :], a_in["idft_fine"]).then_inc(s_tab, 16)
                for n, c in enumerate((slice(0, 2 * HW), slice(2 * HW, 3 * HW))):
                    sp.wait_ge(ra.free, (n + 1) * NR)
                    sp.wait_ge(s_zero, 1)
                    sp.dma_start(raw[1:P, 0, c], raw[0:P - 1, NR, c]).then_inc(s_shift[n], 16)
                    sp.dma_start(raw[0:P - 1, NR + 1, c], raw[1:P, 1, c]).then_inc(s_shift[n], 16)
                sp.wait_ge(ra.free, 20)
                sp.dma_start(k.context_columns, uc[:, :, :]).then_inc(s_spill, 16)
                sp.wait_ge(s_ready, 1)
                for o in range(2):
                    if o == 1:
                        sp.wait_ge(s_prod, HT)
                    sp.dma_start(aux[:, :, :], k.spectra[o, :, 0:17, :]).then_inc(s_spec, 16)
                    sp.wait_ge(ra.free, A[o] + 8)
                    if o == 1:
                        sp.wait_ge(ra.full, A[1] + 8)
                    for g in range(GROUPS):
                        sp.dma_start(part2[:, g, :], part1[8 * g:8 * g + 8, :, :]).then_inc(s_there[g // 2], 16)
                    for m in range(4):
                        sp.wait_ge(ra.free, A[o] + 8 + 2 * (m + 1))
                        if m == 0:
                            sp.wait_ge(ra.full, A[o] + 16)
                        for g in range(4 * m, 4 * m + 4):
                            sp.dma_start(part1[8 * g:8 * g + 8, :, :], part2[:, g, :]).then_inc(s_back, 16)
                    load_weights(k, sp, 8 + o)
                sp.wait_ge(s_back, 32 * GROUPS)
                sp.wait_ge(s_spill, 16)

            @block.scalar
            def _(act):
                for n, i in PROJECTIONS:
                    bank = ra.read(act)
                    dst = raw[:, i + 1, :] if i < NR else uc[:, i - NR, :]
                    if n == 6:
                        act.activation(dst[:, 0:2 * HW], bank[:, :], ACT.Copy).then_inc(ra.free, 1)
                    else:
                        gate = gh[:, i, :] if i < NR else dst[:, 3 * HW:4 * HW]
                        act.activation(gate, bank[:, HW:2 * HW], ACT.Silu)
                        act.activation(dst[:, 2 * HW:3 * HW], bank[:, 0:HW], ACT.Copy).then_inc(ra.free, 1)
                for o in range(2):
                    if o == 0:
                        act.wait_ge(s_ready, 1)
                    else:
                        act.wait_ge(rv.full, 12)
                    for b in range(2):
                        for q in range(4):
                            bank = ra.read(act)
                            dst = part1[:, 8 * b + 2 * q:8 * b + 2 * q + 2, :]
                            act.activation(dst, bank[:, :].rearrange("p (a c) -> p a c", a=2), ACT.Copy).then_inc(ra.free, 1)
                    for n in range(HT):
                        bank = ra.read(act)
                        g = 4 * (n // 2) + n % 2
                        act.activation(part2[:, g:g + 3:2, :], bank[:, :].rearrange("p (a c) -> p a c", a=2), ACT.Copy).then_inc(ra.free, 1)
                for half in range(2):
                    for q in range(2):
                        bank = ra.read(act)
                        dst = k.z_hy[:, half, LC:].rearrange("p (m r) -> p r m", r=NR)[:, 4 * q:4 * q + 4, :]
                        act.activation(dst, bank[:, :].rearrange("p (r m) -> p r m", r=4), ACT.Copy).then_inc(ra.free, 1)

            @block.gpsimd
            def _(pool):
                pool.memset(raw[0:1, 0, :], 0.0)
                pool.memset(raw[96:P, NR + 1, :], 0.0).then_inc(s_zero, 1)
                for o in range(2):
                    pool.wait_ge(ra.full, A[o] + 8)
                    pool.tensor_tensor(v[:, :, 0:HW], v[:, :, 0:HW], k.skip[:, o, :].unsqueeze(1).to_broadcast((P, NR, HW)),
                                       ALU.mult).then_inc(s_skip, 1)

            @block.vector
            def _(dve):
                step = Chain(s_step, dve)
                row = lambda r: r.unsqueeze(1).to_broadcast((P, NR, HW))
                dve.wait_ge(s_conv, 3 * 16)
                prod = aux[:, 9:17, :]
                for g in range(3):
                    dve.wait_ge(s_shift[g // 2], 32)
                    c = slice(g * HW, (g + 1) * HW)
                    x = v[:, :, c]
                    step(dve.tensor_tensor(x, raw[:, 1:NR + 1, c], row(convw[:, 1, c]), ALU.mult))
                    step(dve.tensor_tensor(x, x, row(convb[:, c]), ALU.add))
                    for j, r0 in ((0, 0), (2, 2)):
                        step(dve.tensor_tensor(prod, raw[:, r0:r0 + NR, c], row(convw[:, j, c]), ALU.mult))
                        step(dve.tensor_tensor(x, x, prod, ALU.add))
                dve.memset(tmp[:, 0, 0:1], 0.0).then_inc(s_ready, 1)
                dve.wait_ge(s_ready, 1)
                for o in range(2):
                    dve.wait_ge(s_spec, 16 * (o + 1))
                    for T in range(HT):
                        dve.wait_ge(s_there[T], 32 * (o + 1))
                    for T in range(HT):
                        bank = rv.read(dve)
                        x = bank[:, :].rearrange("p (r c) -> p r c", r=2)
                        y = part1[:, 2 * T:2 * T + 2, :]
                        t = tmp[:, 2 * (T % 2):2 * (T % 2) + 2, :]
                        f = aux[:, T, :].unsqueeze(1).to_broadcast((P, 2, HW)) if T else aux[:, 0:17:16, :]
                        dve.tensor_tensor(y, x, f, ALU.mult).then_inc(s_step, 1)
                        step.n += 1
                        dve.tensor_tensor(t, x, aux[:, 8 + T, :].unsqueeze(1).to_broadcast((P, 2, HW)), ALU.mult).then_inc(rv.free, 1)
                        dve.wait_ge(rv.free, rv.got)
                        dve.tensor_tensor(y[:, 0, :], y[:, 0, :], t[:, 1, :], ALU.subtract)
                        dve.tensor_tensor(y[:, 1, :], y[:, 1, :], t[:, 0, :], ALU.add).then_inc(s_prod, 1)
                    dve.wait_ge(s_prod, HT * (o + 1))
                    dve.wait_ge(s_skip, o + 1)
                    for q in range(4):
                        bank = rv.read(dve)
                        t = tmp[:, 2 * (q % 2):2 * (q % 2) + 2, :]
                        x = v[:, 2 * q:2 * q + 2, 0:HW]
                        dve.tensor_tensor(t, bank[:, :].rearrange("p (a c) -> p a c", a=2),
                                          k.inv_sum[:, o, 0, :].unsqueeze(1).to_broadcast((P, 2, HW)), ALU.mult).then_inc(rv.free, 1)
                        dve.wait_ge(rv.free, rv.got)
                        step(dve.tensor_tensor(x, x, t, ALU.add))
                        ins = dve.tensor_tensor(x, x, v[:, 2 * q:2 * q + 2, (1 + o) * HW:(2 + o) * HW], ALU.mult)
                        if o == 1:
                            step(ins)
                            ins = dve.tensor_tensor(x, x, gh[:, 2 * q:2 * q + 2, :], ALU.mult)
                        if q < 3:
                            step(ins)
                    ins.then_inc(s_y, 1)


ROWS = L // GRID


def window(i):
    if i < TC:
        return None
    r = 2 * (i - TC)
    s = min(max(r - KH // 2, 0), ROWS - KH)
    inner = r - KH // 2 == s and r + 1 - KH // 2 <= ROWS - KH and r - KH // 2 >= 0
    return s, KH + (1 if inner and r + 1 - KH // 2 == s + 1 else 0), s - r + KH - 1


def attention_stage(k):
    nc, a_in = k.nc, k.a
    PAIRS = NA_HEADS // 2
    UNITS = 2 * TILES
    NW = (KH + 1) * GRID
    BLOCKS = TC + (NW + P - 1) // P
    with ExitStack() as mem:
        sb = lambda name, shape: sbuf(mem, nc, name, shape)
        q, k_hi, k_lo = sb("s4_q", [P, 2, TOK]), sb("s4_k_high", [P, 2, TOK]), sb("s4_k_low", [P, 2, TOK])
        vg = sb("s4_v_and_gate", [P, TILES, 4 * HD])
        v, g = vg[:, :, 0:2 * HD], vg[:, :, 2 * HD:4 * HD]
        qk, square = sb("s4_qk", [P, 2, 512]), sb("s4_square", [P, 4 * HD])
        norm = sb("s4_norm", [P, 2, 3, 4])
        gains = sb("s4_gains", [P, 2])
        eps = sb("s4_eps", [P, 1])
        mask = sb("s4_mask", [P, GRID])
        table = sb("s4_bias", [P, 2, 2 * KH, GRID])
        raw = sb("s4_raw_bias", [P, 2 * KH, GRID])
        inner = sb("s4_inner_bias", [P, 2, KH + 1, GRID])
        w_high = sb("s4_w_high", [P, KC, WCH])
        with nc.sbuf_tensor("s4_x_parts", [P, 2, 2, KC, P], F32) as x_parts:
            pass
        p_sb = sb("s4_probs", [P, 4, LC + NW])
        pT = sb("s4_probsT", [P, 2, BLOCKS * P])
        top, total = sb("s4_max", [P, 4, 3]), sb("s4_sum", [P, 8, 4])

        ring, rz = Ring("s4_qkv", k.psum[4:8], k.sem), Ring("s4_zT", k.psum[0:4], k.sem)
        s_in, s_bias, s_zero = k.sem("s4_gains_here"), k.sem("s4_bias_ready"), k.sem("s4_eps")
        s_raw = k.sem("s4_raw_bias_here")
        s_sq, s_ss, s_rt, s_vg, s_hi, s_silu = (k.sem("s4_" + n) for n in ("squares", "square_sums", "roots", "v_and_gate", "high_parts", "gates"))
        s_scores, s_max, s_exp = k.sem("s4_scores"), k.sem("s4_max_ready"), k.sem("s4_exp_done")
        s_t0, s_t1, s_c0, s_c1 = (k.sem("s4_" + n) for n in ("probsT_low", "probsT_high", "probsT_low_copied", "probsT_high_copied"))
        s_o, s_z, s_step, s_pool = k.sem("s4_o"), k.sem("s4_z"), k.sem("s4_dve_step"), k.sem("s4_pool_step")
        split = Split(k, "s4_split", w_high, [(x_parts[:, b, 0], x_parts[:, b, 1]) for b in range(2)])
        RU = 2 * TILES
        ZU = (TILES + 3) // 4

        def unit(n):
            return n // UNITS, n % 2, n % UNITS // 2

        def scores_of(n):
            return k.all_psum[:, (n % 2) * 1024:(n % 2) * 1024 + 1024]

        def blocks(i):
            out = [(0, P), (1, P)]
            if window(i):
                s, rows, _ = window(i)
                keys = rows * GRID
                out += [(TC + s // 2 + b, min(P, keys - b * P)) for b in range((keys + P - 1) // P)]
            return out

        def projected(pair, i):
            return RU * pair + max(2 * i, 1)

        def turned_at(pair, i):
            return RU * pair + min(2 * i + 3, RU)

        def columns(i):
            return [(slice(0, KC), k.hxT[:, :, i * P:(i + 1) * P])]

        def bank_at(count):
            return ring.banks[(count - 1) % len(ring.banks)]

        def place(i, b):
            return 4 if i < TC and b == 1 else b

        with nc.Block() as block:
            @block.sync
            def _(sp):
                this = k.of_layer
                for c, name in enumerate(("na_q_gain", "na_k_gain")):
                    for h in range(2):
                        sp.dma_start(gains[64 * h:64 * h + 64, c:c + 1], this(a_in[name]).rearrange("a n -> n a")).then_inc(s_in, 16)
                sp.dma_start(mask[:, :], a_in["colmask"]).then_inc(s_in, 16)
                for h in range(NA_HEADS):
                    if h >= 1:
                        sp.wait_ge(s_bias, h)
                    rpb = this(a_in["na_rpb"])[:, h]
                    for part in range(2):
                        src = bass.AP(rpb.tensor, rpb.offset + (1 - part) * P, [[1, GRID], [P, 2 * KH], [1, GRID]])
                        sp.dma_start(raw[64 * part:64 * part + 64], src).then_inc(s_raw, 16)
                    if h % 2 == 0 and h >= 2:
                        pair = h // 2 - 1
                        sp.wait_ge(ring.full, projected(pair, TILES - 1))
                        load_weights(k, sp, 10 + pair)
                sp.wait_ge(ring.full, projected(PAIRS - 1, TILES - 1))
                load_weights(k, sp, 10 + PAIRS - 1)

            @block.gpsimd
            def _(pool):
                pool.wait_ge(s_in, 5 * 16)
                for h in range(NA_HEADS):
                    pool.wait_ge(s_raw, 32 * (h + 1))
                    t = table[:, h % 2]
                    if h >= 1:
                        pool.wait_ge(s_bias, h)
                    if h >= 2:
                        pool.wait_ge(s_max, UNITS * (h // 2) - 1 + h % 2)
                    pool.tensor_tensor(t, raw[:, :, ::-1], mask[:, :].unsqueeze(1).to_broadcast((P, 2 * KH, GRID)), ALU.add).then_inc(s_pool, 1)
                    pool.wait_ge(s_pool, 3 * h + 1)
                    pool.tensor_copy(inner[:, h % 2], t[:, 3:4 + KH, :]).then_inc(s_pool, 1)
                    pool.wait_ge(s_pool, 3 * h + 2)
                    pool.memset(inner[0:64, h % 2, KH, :], NEG).then_inc(s_pool, 1)
                    pool.wait_ge(s_pool, 3 * h + 3)
                    pool.memset(inner[64:128, h % 2, 0, :], NEG).then_inc(s_bias, 1)

            @block.tensor
            def _(pe):
                def projections(pair):
                    w = k.w_low[:, pair % 2]

                    def turn(i):
                        pe.wait_ge(ring.free, projected(pair, i))
                        bank = ring.fill(pe)
                        for m in range(4):
                            mm = pe.transpose(bank[:, m * P:(m + 1) * P], qk[:, i % 2, m * P:(m + 1) * P], k.ident[:, :])
                        mm.then_inc(ring.full, 1)

                    for i in range(TILES):
                        bank, x = ring.fill(pe), split.tile(pe)
                        split.product(pe, bank[:, :], x, w, first=(i == 0)).then_inc(ring.full, 1)
                        if i >= 1:
                            turn(i - 1)
                    turn(TILES - 1)

                def scores(n):
                    _, _, i = unit(n)
                    if n >= 2:
                        pe.wait_ge(s_exp, n)
                    parts = [(0, 0, LC)]
                    if window(i):
                        s, n_rows, _ = window(i)
                        k0 = LC + s * GRID
                        parts += [(LC, k0, 256), (512, k0 + 256, n_rows * GRID - 256)]
                    for h in range(2):
                        for c0, key, keys in parts:
                            for kk in (k_hi, k_lo):
                                mm = pe.matmul(scores_of(h)[:, c0:c0 + keys], R32(q[:, h, i * P:(i + 1) * P]), R32(kk[:, h, key:key + keys]),
                                               start=(kk is k_hi), stop=(kk is k_lo))
                        mm.then_inc(s_scores, 1)

                def turn_probs(n):
                    _, _, i = unit(n)
                    pe.wait_ge(s_exp, n + 1)
                    if n >= 1:
                        pe.wait_ge(s_c0, n)
                    for b, (_, keys) in enumerate(blocks(i)):
                        at = place(i, b)
                        if at == 4 and n >= 1:
                            pe.wait_ge(s_c1, n)
                        mm = pe.transpose(k.all_psum[0:keys, 2048 + at * P:2048 + (at + 1) * P], p_sb[:, n % 4, b * P:b * P + keys], k.ident[:, :])
                        if place(i, b + 1) == 4:
                            mm.then_inc(s_t0, 1)
                    mm.then_inc(s_t1, 1)

                def outputs(n):
                    _, h, i = unit(n)
                    pe.wait_ge(s_c0, n + 1)
                    pe.wait_ge(s_c1, n + 1)
                    if n >= 2:
                        pe.wait_ge(s_z, n - 1)
                    bank = k.psum[6 + n % 2]
                    last = len(blocks(i)) - 1
                    for b, (tile, keys) in enumerate(blocks(i)):
                        mm = pe.matmul(bank[:, 0:HD], pT[0:keys, n % 2, place(i, b) * P:(place(i, b) + 1) * P], v[0:keys, tile, h * HD:(h + 1) * HD],
                                       start=(b == 0), stop=(b == last))
                    mm.then_inc(s_o, 1)

                for pair in range(PAIRS):
                    n0, n1 = pair * UNITS, (pair + 1) * UNITS
                    projections(pair)
                    pe.wait_ge(ring.free, RU * (pair + 1))
                    if pair >= 1:
                        pe.wait_ge(rz.free, ZU * pair)
                    for n in range(n0, n1 + 4, 2):
                        if n < n1:
                            scores(n)
                        for h in range(2):
                            if n0 <= n - 4:
                                outputs(n - 4 + h)
                            if n0 <= n - 2 < n1:
                                turn_probs(n - 2 + h)
                    pe.wait_ge(s_z, n1)
                    for t in range(0, TILES, 4):
                        bank = rz.fill(pe)
                        for i in range(t, min(t + 4, TILES)):
                            mm = pe.transpose(bank[:, (i - t) * P:(i - t + 1) * P], g[:, i, :], k.ident[:, :])
                        mm.then_inc(rz.full, 1)

            @block.scalar
            def _(act):
                def high_parts(pair, i):
                    bank = bank_at(turned_at(pair, i))
                    act.wait_ge(ring.full, turned_at(pair, i))
                    for c, dst in enumerate((q, k_hi)):
                        ins = act.activation(R32(dst[:, :, i * P:(i + 1) * P]), bank[:, c * 256:(c + 1) * 256].rearrange("p (m t) -> p m t", m=2),
                                             ACT.Copy, scale=gains[:, c:c + 1])
                    ins.then_inc(s_hi, 1)

                def probs(n):
                    i = unit(n)[2]
                    act.wait_ge(s_max, n + 1)
                    bias = top[:, n % 4, 2:3]
                    if window(i):
                        p = p_sb[:, n % 4, LC:LC + window(i)[1] * GRID]
                        act.activation(p, p, ACT.Exp, bias=bias, accum_out=total[:, n % 8, 1:2])
                    act.activation(p_sb[:, n % 4, 0:LC], scores_of(n)[:, 0:LC], ACT.Exp, bias=bias,
                                   accum_out=total[:, n % 8, 0:1]).then_inc(s_exp, 1)

                def copy_low(n):
                    cols = (4 if window(unit(n)[2]) else 1) * P
                    act.wait_ge(s_t0, n + 1)
                    if n >= 2:
                        act.wait_ge(s_o, n - 1)
                    act.activation(pT[:, n % 2, 0:cols], k.all_psum[:, 2048:2048 + cols], ACT.Copy).then_inc(s_c0, 1)

                act.wait_ge(s_zero, 1)
                for pair in range(PAIRS):
                    if pair >= 1:
                        act.wait_ge(s_o, UNITS * pair)
                    split.x_high(act, columns(0))
                    if pair == 0:
                        split.weights_high(act, 8)
                    split.x_high(act, columns(1))
                    if pair >= 1:
                        act.wait_ge(rz.full, ZU * pair)
                    for i in range(TILES):
                        n = TILES * pair + i
                        bank = bank_at(projected(pair, i))
                        act.wait_ge(ring.full, projected(pair, i))
                        if n >= 1:
                            act.wait_ge(s_ss, n)
                        act.activation(square[:, :], bank[:, 0:256], ACT.Square).then_inc(s_sq, 1)
                        act.activation(vg[:, i, :], bank[:, 256:512], ACT.Copy).then_inc(s_vg, 1)
                        if i + 2 < TILES:
                            split.x_high(act, columns(i + 2))
                        act.wait_ge(s_ss, n + 1)
                        act.activation(norm[:, i % 2, 1, :], norm[:, i % 2, 0, :], ACT.Sqrt, bias=eps[:, 0:1], scale=1.0 / HD).then_inc(s_rt, 1)
                        if i >= 1:
                            high_parts(pair, i - 1)
                    high_parts(pair, TILES - 1)
                    act.wait_ge(s_vg, TILES * (pair + 1))
                    act.activation(g, g, ACT.Silu).then_inc(s_silu, 1)
                    n0, n1 = pair * UNITS, (pair + 1) * UNITS
                    for n in range(n0, n1 + 2, 2):
                        for h in range(2):
                            if n < n1:
                                probs(n + h)
                            if n > n0:
                                copy_low(n - 2 + h)
                        if pair + 1 < PAIRS and 1 <= (n - n0) // 2 <= KC:
                            split.weights_high(act, 9 + pair, [(n - n0) // 2 - 1])
                    for t in range(0, TILES, 4):
                        tiles = min(4, TILES - t)
                        bank = rz.read(act)
                        act.activation(k.z_na[:, pair, t * P:(t + tiles) * P], bank[:, 0:tiles * P], ACT.Copy).then_inc(rz.free, 1)

            @block.vector
            def _(dve):
                step = Chain(s_step, dve)
                dve.memset(eps[:, :], EPS).then_inc(s_zero, 1)
                dve.wait_ge(s_in, 5 * 16)
                step(dve.tensor_scalar(gains[:, 0:1], gains[:, 0:1], HD ** -0.5, None, ALU.mult))

                def low_parts(pair, i):
                    bank = ring.read(dve)
                    dve.wait_ge(s_hi, TILES * pair + i + 1)
                    cols = slice(i * P, (i + 1) * P)
                    two = lambda x: x.rearrange("p (m t) -> p m t", m=2)
                    dve.scalar_tensor_tensor(out=R32(k_lo[:, :, cols]), in0=two(bank[:, 256:512]), scalar=gains[:, 1:2], in1=k_hi[:, :, cols],
                                             op0=ALU.mult, op1=ALU.subtract)
                    dve.scalar_tensor_tensor(out=R32(q[64:128, :, cols]), in0=two(bank[64:128, 0:256]), scalar=gains[64:128, 0:1],
                                             in1=q[64:128, :, cols], op0=ALU.mult, op1=ALU.subtract).then_inc(ring.free, 1)

                def maximum(n):
                    pair, h, i = unit(n)
                    dve.wait_ge(s_scores, n + 1)
                    if n >= 4:
                        dve.wait_ge(s_t1, n - 3)
                    slot = top[:, n % 4]
                    bank = scores_of(n)
                    best = slot[:, 0:1]
                    dve.tensor_reduce(best, bank[:, 0:LC], AX.X, ALU.max).then_inc(s_step, 1)
                    step.n += 1
                    if window(i):
                        s, rows, first = window(i)
                        if i == TC:
                            dve.wait_ge(s_bias, 2 * pair + h + 1)
                        bias = inner[:, h] if rows > KH else table[:, h, first:first + KH, :]
                        keys = rows * GRID
                        step(dve.tensor_tensor_reduce(p_sb[:, n % 4, LC:LC + keys], bank[:, LC:LC + keys], bias.rearrange("p j c -> p (j c)"),
                                                      1.0, -3e38, ALU.add, ALU.max, slot[:, 1:2]))
                        dve.tensor_scalar(slot[:, 2:3], best, slot[:, 1:2], -1.0, ALU.max, ALU.mult).then_inc(s_max, 1)
                    else:
                        dve.wait_ge(s_step, step.n)
                        dve.tensor_scalar(slot[:, 2:3], best, -1.0, None, ALU.mult).then_inc(s_max, 1)

                def copy_high(n):
                    i = unit(n)[2]
                    dve.wait_ge(s_t1, n + 1)
                    if n >= 2:
                        dve.wait_ge(s_o, n - 1)
                    parts = [(place(i, b), keys) for b, (_, keys) in enumerate(blocks(i)) if place(i, b) >= 4]
                    full = sum(keys == P for _, keys in parts)
                    at = 4 * P
                    cols = full * P
                    ins = dve.tensor_copy(pT[:, n % 2, at:at + cols], k.all_psum[:, 2048 + at:2048 + at + cols])
                    if full < len(parts):
                        at += cols
                        ins = dve.tensor_copy(pT[0:64, n % 2, at:at + P], k.all_psum[0:64, 2048 + at:2048 + at + P])
                    ins.then_inc(s_c1, 1)

                def gated(n):
                    pair, h, i = unit(n)
                    slot = total[:, n % 8]
                    if i < TC:
                        step(dve.reciprocal(slot[:, 3:4], slot[:, 0:1]))
                    else:
                        step(dve.tensor_tensor(slot[:, 2:3], slot[:, 0:1], slot[:, 1:2], ALU.add))
                        step(dve.reciprocal(slot[:, 3:4], slot[:, 2:3]))
                    dve.wait_ge(s_silu, pair + 1)
                    dve.wait_ge(s_o, n + 1)
                    z = g[:, i, h * HD:(h + 1) * HD]
                    dve.scalar_tensor_tensor(out=z, in0=k.psum[6 + n % 2][:, 0:HD], scalar=slot[:, 3:4], in1=z, op0=ALU.mult, op1=ALU.mult).then_inc(s_z, 1)

                for pair in range(PAIRS):
                    if pair >= 1:
                        dve.wait_ge(s_o, UNITS * pair)
                    split.x_low(dve, columns(0))
                    if pair == 0:
                        split.weights_low(dve, 8)
                    split.x_low(dve, columns(1))
                    for i in range(TILES):
                        n = TILES * pair + i
                        dve.wait_ge(s_sq, n + 1)
                        dve.tensor_reduce(norm[:, i % 2, 0, :], square[:, :].rearrange("p (h d) -> p h d", d=HD), AX.X, ALU.add).then_inc(s_ss, 1)
                        dve.wait_ge(s_rt, n + 1)
                        step(dve.reciprocal(norm[:, i % 2, 2, :], norm[:, i % 2, 1, :]))
                        if n >= 2:
                            dve.wait_ge(ring.full, turned_at((n - 2) // TILES, (n - 2) % TILES))
                        bank = ring.read(dve)
                        dve.wait_ge(s_vg, n + 1)
                        twice = lambda x: x.unsqueeze(2).to_broadcast((P, 4, 2, HD))
                        dve.tensor_tensor(qk[:, i % 2, :].rearrange("p (h w d) -> p h w d", w=2, d=HD), twice(bank[:, 0:256].rearrange("p (h d) -> p h d", d=HD)),
                                          twice(norm[:, i % 2, 2, :].unsqueeze(2).to_broadcast((P, 4, HD))), ALU.mult).then_inc(ring.free, 1)
                        if i + 2 < TILES:
                            split.x_low(dve, columns(i + 2))
                        if i >= 1:
                            low_parts(pair, i - 1)
                    low_parts(pair, TILES - 1)
                    n0, n1 = pair * UNITS, (pair + 1) * UNITS
                    for n in range(n0, n1 + 4, 2):
                        if n < n1:
                            maximum(n)
                            maximum(n + 1)
                        for h in range(2):
                            if n0 <= n - 4:
                                gated(n - 4 + h)
                            if n0 <= n - 2 < n1:
                                copy_high(n - 2 + h)
                        if pair + 1 < PAIRS and 1 <= (n - n0) // 2 <= KC:
                            split.weights_low(dve, 9 + pair, [(n - n0) // 2 - 1])


CHAINS = (list(range(TILES)), [1, 0] + list(range(TILES - 1, TC - 1, -1)))


def retention_stage(k):
    nc, a_in = k.nc, k.a
    with ExitStack() as mem:
        sb = lambda name, shape: sbuf(mem, nc, name, shape)
        qk, vg = sb("s5_qk", [P, TILES, 512]), sb("s5_vg", [P, TILES, 512])
        rope, tmp = sb("s5_rope", [P, TILES, 64]), sb("s5_tmp", [P, 512])
        dist, age, rest = sb("s5_dist", [P, 4, P]), sb("s5_age", [P, 2, P]), sb("s5_rest", [P, 8])
        rate, zeta = sb("s5_log_gamma", [P, 8]), sb("s5_zeta", [P, 8])
        rate_p, power = sb("s5_log_gamma_turned", [P, 4]), sb("s5_chunk_decay", [P, 4])
        decay = sb("s5_decay", [P, 2, 2, P])
        fade = sb("s5_fade", [P, 2, 2, P])
        stat, eps = sb("s5_stat", [P, 2, 3, RH]), sb("s5_eps", [P, 1])
        with nc.sbuf_tensor("s5_w_high", [P, KC, WCH], F32) as w_high, nc.sbuf_tensor("s5_x_parts", [P, 2, 2, KC, P], F32) as x_parts:
            pass
        state = sb("s5_state", [P, TILES, 2, P])
        kz = sb("s5_k_weighted", [P, 2, 2, RW])
        qkT, qx = sb("s5_qkT", [P, 2, 512]), sb("s5_q_faded", [P, 2, 2, RW])
        sT, r = sb("s5_scoresT", [P, 2, 2, RW]), sb("s5_r", [P, 2, RW])
        square = sb("s5_square", [P, 2, RW])

        ra, rv = Ring("s5_act", k.psum[0:4], k.sem), Ring("s5_dve", k.psum[4:8], k.sem)
        rt = Ring("s5_turned", k.psum[0:2], k.sem)
        split = Split(k, "s5_split", w_high, [(x_parts[:, b, 0], x_parts[:, b, 1]) for b in range(2)])
        columns = lambda t: [(slice(0, KC), k.hxT[:, :, t % TILES * P:(t % TILES + 1) * P])]
        scores_bank = lambda i, h2: k.psum[(4, 2)[i % 2] + h2]
        names = ("tables_here", "rates", "tables", "dve_step", "act_step", "roped", "k_weighted", "squares",
                 "q_faded", "scores", "scores_weighted", "o", "o_copied", "square_sums", "roots", "z", "eps", "pool_step")
        (s_tab, s_rate, s_table, s_step, s_act, s_rope, s_kz, s_sq, s_qx, s_sc, s_sw, s_o, s_oc, s_ss, s_rt, s_z,
         s_eps, s_pool) = (k.sem("s5_" + n) for n in names)

        with nc.Block() as block:
            @block.sync
            def _(sp):
                rates = k.of_layer(a_in["ret_log_rate"])
                sp.dma_start(rate[:, :], rates.rearrange("a d h -> a (d h)").to_broadcast((P, 8))).then_inc(s_tab, 16)
                for h2 in range(2):
                    src = rates.rearrange("a d (p h) -> a (d p) h", h=2)[:, :, h2]
                    sp.dma_start(rate_p[64 * h2:64 * h2 + 64, :], src.to_broadcast((64, 4))).then_inc(s_tab, 16)
                sp.dma_start(rest[:, :], a_in["rest"].rearrange("p d h -> p (d h)")).then_inc(s_tab, 16)
                sp.dma_start(dist[:, :, :], a_in["dist"]).then_inc(s_tab, 16)
                sp.dma_start(age[:, :, :], a_in["age"]).then_inc(s_tab, 16)
                sp.dma_start(rope[:, :, :], a_in["rope"]).then_inc(s_tab, 16)
                sp.wait_ge(rv.full, TILES)
                load_weights(k, sp, 14)
                sp.wait_ge(ra.full, TILES)
                load_weights(k, sp, 15)

            @block.tensor
            def _(pe):
                for ring, n in ((rv, 12), (ra, 13)):
                    for i in range(TILES):
                        bank, x = ring.fill(pe), split.tile(pe)
                        split.product(pe, bank[:, :], x, k.w_low[:, n % 2], first=(i == 0)).then_inc(ring.full, 1)
                pe.wait_ge(ra.free, TILES)
                for j in range(TILES - 1):
                    pe.wait_ge(s_kz, 2 * j + 2)
                    bank = rv.fill(pe)
                    for d in range(2):
                        t = CHAINS[d][j]
                        for h in range(RH):
                            mm = pe.matmul(bank[64 * (h % 2):64 * (h % 2) + 64, d * P + (h // 2) * HD:d * P + (h // 2 + 1) * HD],
                                           kz[:, j % 2, d, h * HD:(h + 1) * HD], vg[:, t, h * HD:(h + 1) * HD], start=True, stop=True)
                    mm.then_inc(rv.full, 1)

                def turn(i):
                    bank = rt.fill(pe)
                    for m in range(4):
                        mm = pe.transpose(bank[:, m * P:(m + 1) * P], qk[:, i, m * P:(m + 1) * P], k.ident[:, :])
                    mm.then_inc(rt.full, 1)

                pe.wait_ge(rv.free, 2 * TILES - 1)
                def scores(i):
                    pe.wait_ge(rt.free, i + 1)
                    if i >= 2:
                        pe.wait_ge(s_sw, i - 1)
                    for h in (0, 2, 1, 3):
                        rows = slice(64 * (h % 2), 64 * (h % 2) + 64)
                        pair = h // 2
                        mm = pe.matmul(scores_bank(i, h % 2)[:, pair * P:(pair + 1) * P], qkT[rows, i % 2, (2 + pair) * P:(3 + pair) * P],
                                       qkT[rows, i % 2, pair * P:(pair + 1) * P], start=True, stop=True)
                    mm.then_inc(s_sc, 1)

                def outputs(i):
                    pe.wait_ge(s_sw, i + 1)
                    pe.wait_ge(s_qx, i + 1)
                    if i >= 1:
                        pe.wait_ge(s_oc, i)
                    for h in (0, 2, 1, 3):
                        rows = slice(64 * (h % 2), 64 * (h % 2) + 64)
                        pair = h // 2
                        out = k.psum[6 + h % 2][:, pair * HD:(pair + 1) * HD]
                        pe.matmul(out, sT[:, i % 2, h % 2, pair * P:(pair + 1) * P], vg[:, i, h * HD:(h + 1) * HD], start=True, stop=False)
                        for d in range(2):
                            mm = pe.matmul(out, qx[rows, i % 2, d, pair * P:(pair + 1) * P], state[rows, i, d, pair * HD:(pair + 1) * HD],
                                           start=False, stop=(d == 1))
                    mm.then_inc(s_o, 1)

                turn(0)
                turn(1)
                scores(0)
                for i in range(TILES):
                    if i + 2 < TILES:
                        turn(i + 2)
                    if i + 1 < TILES:
                        scores(i + 1)
                    outputs(i)
                pe.wait_ge(s_z, TILES)
                for t in range(TILES // 2):
                    bank = rt.fill(pe)
                    for m in range(4):
                        mm = pe.transpose(bank[:, m * P:(m + 1) * P], qk[:, 2 * t + m % 2, (m // 2) * P:(m // 2 + 1) * P], k.ident[:, :])
                    mm.then_inc(rt.full, 1)

            @block.scalar
            def _(act):
                def x_high(t):
                    if t >= 2:
                        act.wait_ge(*((rv.full, t - 1) if t - 2 < TILES else (ra.full, t - 1 - TILES)))
                    split.x_high(act, columns(t))

                x_high(0)
                split.weights_high(act, 12)
                x_high(1)
                act.wait_ge(s_tab, 7 * 16)
                act.activation(rate[:, :], rate[:, :], ACT.Exp)
                act.activation(rate_p[:, :], rate_p[:, :], ACT.Exp).then_inc(s_rate, 1)
                act.wait_ge(s_table, 1)
                act.activation(zeta[:, :], zeta[:, :], ACT.Exp).then_inc(s_act, 1)
                act.activation(power[:, :], rate_p[:, :], ACT.Exp, scale=float(P)).then_inc(s_act, 1)
                for d in range(2):
                    for pair in range(2):
                        act.activation(fade[:, d, pair, :], age[:, d, :], ACT.Exp, scale=rate_p[:, 2 * d + pair:2 * d + pair + 1]).then_inc(s_act, 1)
                for h in range(RH):
                    if h >= 1:
                        act.wait_ge(s_table, 1 + h)
                    for d in range(2):
                        act.activation(tmp[:, d * P:(d + 1) * P], dist[:, d, :], ACT.Exp, scale=rate[:, RH * d + h:RH * d + h + 1]).then_inc(s_act, 1)
                for t in range(2, TILES + 1):
                    x_high(t)
                act.wait_ge(rv.full, TILES)
                split.weights_high(act, 13)
                x_high(TILES + 1)
                for i in range(TILES):
                    if i + 2 < TILES:
                        x_high(TILES + i + 2)
                    bank = ra.read(act)
                    act.activation(vg[:, i, RW:2 * RW], bank[:, RW:2 * RW], ACT.Silu)
                    act.activation(vg[:, i, 0:RW], bank[:, 0:RW], ACT.Copy).then_inc(ra.free, 1)
                act.wait_ge(s_eps, 1)

                def root(i):
                    act.wait_ge(s_ss, i + 1)
                    act.activation(stat[:, i % 2, 1, :], stat[:, i % 2, 0, :], ACT.Sqrt, bias=eps[:, 0:1], scale=1.0 / HD).then_inc(s_rt, 1)

                def copy_turned(i):
                    if i >= 2:
                        act.wait_ge(s_qx, i - 1)
                        act.wait_ge(s_sc, i - 1)
                    bank = rt.read(act)
                    act.activation(qkT[:, i % 2, :], bank[:, :], ACT.Copy).then_inc(rt.free, 1)

                copy_turned(0)
                copy_turned(1)
                for i in range(TILES):
                    if i + 2 < TILES:
                        copy_turned(i + 2)
                    if i >= 1:
                        root(i - 1)
                    act.wait_ge(s_o, i + 1)
                    if i >= 2:
                        act.wait_ge(s_z, i - 1)
                    for h2 in range(2):
                        ins = act.activation(r[:, i % 2, :].rearrange("p (a h e) -> p h a e", h=2, e=HD)[:, h2],
                                             k.psum[6 + h2][:, 0:P].rearrange("p (a e) -> p a e", a=2), ACT.Copy)
                    ins.then_inc(s_oc, 1)
                    act.wait_ge(s_oc, i + 1)
                    act.activation(square[:, i % 2, :], r[:, i % 2, :], ACT.Square).then_inc(s_sq, 1)
                root(TILES - 1)
                for t in range(TILES // 2):
                    bank = rt.read(act)
                    act.activation(k.z_re[:, :, 2 * t * P:(2 * t + 2) * P], bank[:, :].rearrange("p (c t) -> p c t", c=2), ACT.Copy).then_inc(rt.free, 1)

            @block.gpsimd
            def _(pool):
                pool.wait_ge(ra.full, TILES)
                pool.memset(state[:, 0, 0, :], 0.0).then_inc(s_pool, 1)
                pool.memset(state[:, 1, 1, :], 0.0).then_inc(s_pool, 1)
                pool.wait_ge(s_pool, 2)
                pool.wait_ge(s_table, 6)
                pool.wait_ge(s_rope, TILES)
                for j in range(TILES - 1):
                    if j >= 2:
                        pool.wait_ge(rv.full, TILES + j - 1)
                    for d in range(2):
                        t = CHAINS[d][j]
                        if j or d:
                            pool.wait_ge(s_kz, 2 * j + d)
                        pool.tensor_tensor(kz[:, j % 2, d, :].rearrange("p (h e) -> p h e", h=RH),
                                           qk[:, t, RW:2 * RW].rearrange("p (h e) -> p h e", h=RH),
                                           zeta[:, RH * d:RH * d + RH].unsqueeze(2).to_broadcast((P, RH, HD)), ALU.mult).then_inc(s_kz, 1)

            @block.vector
            def _(dve):
                step = Chain(s_step, dve)
                dve.memset(eps[:, :], EPS).then_inc(s_eps, 1)
                split.x_low(dve, columns(0))
                split.weights_low(dve, 12)
                split.x_low(dve, columns(1))
                dve.wait_ge(s_rate, 1)
                step(dve.tensor_scalar(rate[:, :], rate[:, :], -1.0, None, ALU.mult))
                dve.tensor_scalar(rate_p[:, :], rate_p[:, :], -1.0, None, ALU.mult).then_inc(s_step, 1)
                step.n += 1
                dve.tensor_tensor(zeta[:, :], rest[:, :], rate[:, :], ALU.mult).then_inc(s_table, 1)
                for h in range(RH):
                    dve.wait_ge(s_act, 6 + 2 * h + 2)
                    dst = decay[:, h % 2, h // 2, :]
                    step(dve.tensor_tensor(dst, tmp[:, 0:P], dist[:, 2, :], ALU.mult))
                    step(dve.tensor_tensor(tmp[:, P:2 * P], tmp[:, P:2 * P], dist[:, 3, :], ALU.mult))
                    dve.tensor_tensor(dst, dst, tmp[:, P:2 * P], ALU.add).then_inc(s_table, 1)
                dve.wait_ge(s_table, 1 + RH)
                dve.tensor_scalar(zeta[:, :], zeta[:, :], HD ** -0.5, None, ALU.mult).then_inc(s_table, 1)

                for i in range(TILES):
                    if i == TILES - 1:
                        split.weights_low(dve, 13)
                    split.x_low(dve, columns(i + 2))
                    bank = rv.read(dve)
                    halves = lambda x, n: x.rearrange("p (g n c) -> p g n c", n=2, c=16)[:, :, n, :].rearrange("p (h a) c -> p h a c", a=2)
                    x1, x2 = halves(bank[:, :], 0), halves(bank[:, :], 1)
                    o1, o2 = halves(qk[:, i, :], 0), halves(qk[:, i, :], 1)
                    cos, sin = (rope[:, i, 32 * n:32 * n + 32].rearrange("p (a c) -> p a c", a=2).unsqueeze(1).to_broadcast((P, 8, 2, 16)) for n in range(2))
                    t1 = tmp[:, 0:256].rearrange("p (h a c) -> p h a c", a=2, c=16)
                    t2 = tmp[:, 256:512].rearrange("p (h a c) -> p h a c", a=2, c=16)
                    dve.tensor_tensor(o1, x1, cos, ALU.mult)
                    step(dve.tensor_tensor(t1, x2, sin, ALU.mult))
                    step(dve.tensor_tensor(o1, o1, t1, ALU.subtract))
                    dve.tensor_tensor(o2, x1, sin, ALU.mult)
                    dve.tensor_tensor(t2, x2, cos, ALU.mult).then_inc(rv.free, 1)
                    dve.wait_ge(rv.free, rv.got)
                    dve.tensor_tensor(o2, o2, t2, ALU.add).then_inc(s_rope, 1)
                for t in range(TILES + 2, 2 * TILES):
                    split.x_low(dve, columns(t))
                dve.wait_ge(s_rope, TILES)
                dve.wait_ge(s_pool, 2)
                for j in range(TILES - 1):
                    bank = rv.read(dve)
                    for d in range(2):
                        a, b = CHAINS[d][j], CHAINS[d][j + 1]
                        for pair in range(2):
                            c = slice(pair * HD, (pair + 1) * HD)
                            ins = dve.scalar_tensor_tensor(out=state[:, b, d, c], in0=state[:, a, d, c], scalar=power[:, 2 * d + pair:2 * d + pair + 1],
                                                           in1=bank[:, d * P + pair * HD:d * P + (pair + 1) * HD], op0=ALU.mult, op1=ALU.add)
                    ins.then_inc(rv.free, 1)
                    dve.wait_ge(rv.free, rv.got)

                def normed(i):
                    dve.wait_ge(s_rt, i + 1)
                    st = stat[:, i % 2]
                    step(dve.reciprocal(st[:, 2, :], st[:, 1, :]))
                    rr = r[:, i % 2, :]
                    heads = lambda x: x.rearrange("p (h e) -> p h e", h=RH)
                    step(dve.tensor_tensor(heads(rr), heads(rr), st[:, 2, :].unsqueeze(2).to_broadcast((P, RH, HD)), ALU.mult))
                    dve.tensor_tensor(qk[:, i, 0:RW], rr, vg[:, i, RW:2 * RW], ALU.mult).then_inc(s_z, 1)

                def weighted(i):
                    dve.wait_ge(rt.free, i + 1)
                    if i >= 2:
                        dve.wait_ge(s_o, i - 1)
                    for d in range(2):
                        ins = dve.tensor_tensor(qx[:, i % 2, d, :], qkT[:, i % 2, 0:RW], fade[:, d, :, :].rearrange("p a j -> p (a j)"), ALU.mult)
                    ins.then_inc(s_qx, 1)
                    dve.wait_ge(s_sc, i + 1)
                    for h2 in range(2):
                        ins = dve.tensor_tensor(sT[:, i % 2, h2, :], scores_bank(i, h2)[:, 0:RW],
                                                decay[:, h2, :, :].rearrange("p a j -> p (a j)"), ALU.mult)
                    ins.then_inc(s_sw, 1)

                weighted(0)
                for i in range(TILES):
                    if i + 1 < TILES:
                        weighted(i + 1)
                    if i >= 1:
                        normed(i - 1)
                    dve.wait_ge(s_sq, i + 1)
                    dve.tensor_reduce(stat[:, i % 2, 0, :], square[:, i % 2, :].rearrange("p (h e) -> p h e", h=RH), AX.X, ALU.add).then_inc(s_ss, 1)
                normed(TILES - 1)


def output_stage(k):
    nc, a_in = k.nc, k.a
    BUFS = 3
    ORDER = list(range(TC, TILES)) + list(range(TC))
    IMAGE = TILES - TC
    CONTEXT_UNITS = 7
    with ExitStack() as mem:
        sb = lambda name, shape: sbuf(mem, nc, name, shape)
        x, y = sb("s6_x", [P, BUFS, D]), sb("s6_y", [P, 2, WCH])
        gate = sb("s6_gate", [P, 2, D])
        z_parts, w_high = sb("s6_z_parts", [P, 2, 2, KC, P]), sb("s6_w_high", [P, 2, KC, WCH])
        u = sb("s6_context_columns", [P, TC, 4 * HW])
        cdft, cidft = sb("s6_cdft", [P, 2, 2, LC]), sb("s6_cidft", [P, 2, 2, LC])
        spec = sb("s6_spectra", [P, 2, 5, HW])
        convw, convb = sb("s6_conv_w", [P, 3, 3 * HW]), sb("s6_conv_b", [P, 3 * HW])
        before, after = sb("s6_before", [P, TC, 3 * HW]), sb("s6_after", [P, TC, 3 * HW])
        yf, tmp = sb("s6_product", [P, 2 * TC, HW]), sb("s6_tmp", [P, 2, HW])

        ring, cring = Ring("s6_out", k.psum[0:4], k.sem), Ring("s6_context", k.psum[4:8], k.sem)
        s_x = [k.sem(f"s6_x{b}_here") for b in range(BUFS)]
        s_out = [k.sem(f"s6_x{b}_stored") for b in range(BUFS)]
        s_new, s_gate = k.sem("s6_x_new"), k.sem("s6_gate_here")
        s_tab, s_zero = k.sem("s6_tables_here"), k.sem("s6_zeroed")
        s_step, s_v, s_prod = k.sem("s6_dve_step"), k.sem("s6_v_ready"), k.sem("s6_products")
        split = [Split(k, f"s6_split{h}", w_high[:, h], [(z_parts[:, b, 0], z_parts[:, b, 1]) for b in range(2)]) for h in range(2)]

        def pieces(i):
            c = slice(i * P, (i + 1) * P)
            return [(slice(0, 4), k.z_na[:, :, c]), (slice(4, 6), k.z_hy[:, :, c]), (slice(6, 8), k.z_re[:, :, c])]

        def not_last(eng):
            return eng.If(k.layer < DEPTH - 1)

        with nc.Block() as block:
            @block.sync
            def _(sp):
                this = k.of_layer
                uc = k.context_columns

                def load(n):
                    sp.dma_start(x[:, n % BUFS, :], stream_tile(k, ORDER[n])).then_inc(s_x[n % BUFS], 16)

                def store(n):
                    sp.wait_ge(s_new, n + 1)
                    sp.dma_start(stream_tile(k, ORDER[n]), x[:, n % BUFS, :]).then_inc(s_out[n % BUFS], 16)

                def reload(n):
                    sp.wait_ge(s_out[n % BUFS], 16 * (n // BUFS))
                    load(n)

                for n in range(BUFS):
                    load(n)
                sp.dma_start(gate[:, :, :], k.gates.to_broadcast((P, 2, D))).then_inc(s_gate, 16)
                with not_last(sp):
                    sp.dma_start(u[:, :, :], uc).then_inc(s_tab, 16)
                    sp.wait_ge(s_zero, 1)
                    sp.dma_start(before[1:P, :, :], uc[0:P - 1, :, 0:3 * HW]).then_inc(s_tab, 16)
                    sp.dma_start(before[0:1, 1, :], uc[P - 1:P, 0, 0:3 * HW]).then_inc(s_tab, 16)
                    sp.dma_start(after[0:P - 1, :, :], uc[1:P, :, 0:3 * HW]).then_inc(s_tab, 16)
                    sp.dma_start(after[P - 1:P, 0, :], uc[0:1, 1, 0:3 * HW]).then_inc(s_tab, 16)
                    sp.dma_start(convw[:, :, :], this(a_in["hy_conv_w"]).rearrange("a j c -> a (j c)").to_broadcast((P, 9 * HW))).then_inc(s_tab, 16)
                    sp.dma_start(convb[:, :], this(a_in["hy_conv_b"]).to_broadcast((P, 3 * HW))).then_inc(s_tab, 16)
                    sp.dma_start(cdft[:, :, :, :], a_in["cdft"]).then_inc(s_tab, 16)
                    sp.dma_start(cidft[:, :, :, :], a_in["cidft"]).then_inc(s_tab, 16)
                    for o in range(2):
                        sp.dma_start(spec[:, o], k.spectra[o, :, 17:22, :]).then_inc(s_tab, 16)
                for n in range(IMAGE):
                    store(n)
                    if n + BUFS < IMAGE:
                        reload(n + BUFS)
                for n in range(IMAGE - BUFS, IMAGE):
                    sp.wait_ge(s_out[n % BUFS], 16 * (n // BUFS + 1))
                with not_last(sp):
                    for n in range(IMAGE, TILES):
                        reload(n)
                    for n in range(IMAGE, TILES):
                        store(n)
                    for n in range(IMAGE, TILES):
                        sp.wait_ge(s_out[n % BUFS], 16 * (n // BUFS + 1))

            @block.gpsimd
            def _(pool):
                pool.memset(before[0:1, 0, :], 0.0)
                pool.memset(after[96:P, :, :], 0.0).then_inc(s_zero, 1)

            @block.tensor
            def _(pe):
                def tile(n):
                    x = split[0].tile(pe)
                    for h in range(2):
                        split[h].product(pe, ring.fill(pe)[:, :], x, k.w_low[:, h], first=(n == 0)).then_inc(ring.full, 1)

                def forward(o):
                    pe.wait_ge(s_v, o + 1)
                    for T in range(2):
                        bank = cring.fill(pe)
                        for ri in range(2):
                            for kk in range(TC):
                                mm = pe.matmul(bank[:, ri * HW:(ri + 1) * HW], cdft[:, ri, kk, T * P:(T + 1) * P], u[:, kk, 0:HW],
                                               start=(kk == 0), stop=(kk == TC - 1))
                        mm.then_inc(cring.full, 1)

                def back(o):
                    pe.wait_ge(s_prod, o + 1)
                    bank = cring.fill(pe)
                    for kk in range(TC):
                        for n in range(4):
                            T, ri = n // 2, n % 2
                            mm = pe.matmul(bank[:, kk * HW:(kk + 1) * HW], cidft[:, ri, T, kk * P:(kk + 1) * P], yf[:, n, :],
                                           start=(n == 0), stop=(n == 3))
                    mm.then_inc(cring.full, 1)

                def turn():
                    pe.wait_ge(s_v, 3)
                    bank = cring.fill(pe)
                    for half in range(2):
                        for kk in range(TC):
                            c0 = (2 * half + kk) * P
                            mm = pe.transpose(bank[:, c0:c0 + P], u[:, kk, half * P:(half + 1) * P], k.ident[:, :])
                    mm.then_inc(cring.full, 1)

                steps = {2: lambda: forward(0), 3: lambda: back(0), 4: lambda: forward(1), 5: lambda: back(1), 6: turn}
                for n in range(IMAGE):
                    tile(n)
                    if n in steps:
                        with not_last(pe):
                            steps[n]()
                with not_last(pe):
                    pe.wait_ge(cring.free, CONTEXT_UNITS)
                    for n in range(IMAGE, TILES):
                        tile(n)

            @block.scalar
            def _(act):
                def tile(n):
                    if n >= 2:
                        act.wait_ge(ring.full, 2 * (n - 1))
                    split[0].x_high(act, pieces(ORDER[n]))

                tile(0)
                split[0].weights_high(act, 14)
                split[1].weights_high(act, 15)
                for n in range(1, IMAGE):
                    tile(n)
                with not_last(act):
                    act.wait_ge(cring.free, CONTEXT_UNITS)
                    for n in range(IMAGE, TILES):
                        tile(n)

            @block.vector
            def _(dve):
                step = Chain(s_step, dve)
                wide = lambda r: r.unsqueeze(1).to_broadcast((P, TC, r.shape[-1]))
                v = u[:, :, 0:HW]

                def tile(n):
                    i = ORDER[n]
                    dve.wait_ge(s_x[n % BUFS], 16 * (n // BUFS + 1))
                    for h in range(2):
                        c = slice(h * WCH, (h + 1) * WCH)
                        bank = ring.read(dve)
                        dve.tensor_tensor(y[:, h, :], bank[:, :], gate[:, int(i >= TC), c], ALU.mult).then_inc(ring.free, 1)
                        dve.wait_ge(ring.free, ring.got)
                        ins = dve.tensor_tensor(x[:, n % BUFS, c], x[:, n % BUFS, c], y[:, h, :], ALU.add)
                    ins.then_inc(s_new, 1)

                def short_convolution():
                    xs = u[:, :, 0:3 * HW]
                    dve.wait_ge(s_zero, 1)
                    dve.wait_ge(s_tab, 11 * 16)
                    step(dve.tensor_tensor(xs, xs, wide(convw[:, 1, :]), ALU.mult))
                    step(dve.tensor_tensor(xs, xs, wide(convb[:, :]), ALU.add))
                    for buf, j in ((before, 0), (after, 2)):
                        step(dve.tensor_tensor(buf[:, :, :], buf[:, :, :], wide(convw[:, j, :]), ALU.mult))
                        ins = dve.tensor_tensor(xs, xs, buf[:, :, :], ALU.add)
                        if j == 0:
                            step(ins)
                    ins.then_inc(s_v, 1)

                def products(o):
                    for T in range(2):
                        bank = cring.read(dve)
                        xf = bank[:, :].rearrange("p (r c) -> p r c", r=2)
                        f = wide(spec[:, o, 1, :]) if T else spec[:, o, 0:5:4, :]
                        yy = yf[:, 2 * T:2 * T + 2, :]
                        step(dve.tensor_tensor(yy, xf, f, ALU.mult))
                        dve.tensor_tensor(tmp[:, :, :], xf, wide(spec[:, o, 2 + T, :]), ALU.mult).then_inc(cring.free, 1)
                        dve.wait_ge(cring.free, cring.got)
                        step(dve.tensor_tensor(yy[:, 0, :], yy[:, 0, :], tmp[:, 1, :], ALU.subtract))
                        ins = dve.tensor_tensor(yy[:, 1, :], yy[:, 1, :], tmp[:, 0, :], ALU.add)
                        if T == 0:
                            step(ins)
                    ins.then_inc(s_prod, 1)

                def gated(o):
                    bank = cring.read(dve)
                    dve.tensor_tensor(tmp[:, :, :], bank[:, :].rearrange("p (a c) -> p a c", a=2), wide(k.inv_sum[:, o, 1, :]), ALU.mult).then_inc(cring.free, 1)
                    dve.wait_ge(cring.free, cring.got)
                    step(dve.tensor_tensor(v, v, wide(k.skip[:, o, :]), ALU.mult))
                    step(dve.tensor_tensor(v, v, tmp[:, :, :], ALU.add))
                    ins = dve.tensor_tensor(v, v, u[:, :, (1 + o) * HW:(2 + o) * HW], ALU.mult)
                    if o == 1:
                        step(ins)
                        ins = dve.tensor_tensor(v, v, u[:, :, 3 * HW:4 * HW], ALU.mult)
                    ins.then_inc(s_v, 1)

                def turned():
                    bank = cring.read(dve)
                    dve.tensor_copy(k.z_hy[:, :, 0:LC], bank[:, :].rearrange("p (h t) -> p h t", h=2)).then_inc(cring.free, 1)

                steps = {1: short_convolution, 3: lambda: products(0), 4: lambda: gated(0), 5: lambda: products(1),
                         6: lambda: gated(1), 7: turned}
                low = lambda n: split[0].x_low(dve, pieces(ORDER[n]))
                low(0)
                split[0].weights_low(dve, 14)
                split[1].weights_low(dve, 15)
                dve.wait_ge(s_gate, 16)
                for n in range(IMAGE):
                    if n + 1 < IMAGE:
                        low(n + 1)
                    if n in steps:
                        with not_last(dve):
                            steps[n]()
                    tile(n)
                with not_last(dve):
                    for n in range(IMAGE, TILES):
                        low(n)
                    for n in range(IMAGE, TILES):
                        tile(n)


CONST_SHAPES = {n: v.shape for n, v in constants().items()}
INPUTS = ("x", "c", "ctx", "c_ctx", "norm_w", "ada_w", "ada_b", "w_in", "w_out", "na_q_gain", "na_k_gain", "na_rpb",
          "hy_conv_w", "hy_conv_b", "hy_w1", "hy_b1", "hy_w2", "hy_b2", "hy_w3", "hy_sin_freq", "hy_skip", "ret_log_rate")


def program(nc, a, out, scratch, depth=DEPTH):
    with ExitStack() as ctx:
        k = Build(nc, a, out, ctx)
        ctx.enter_context(nc.allow_non_contiguous_dma(reason="vectors of a layer go down the partitions"))
        k.spectra, k.context, k.context_columns, k.gates = scratch
        sb = lambda name, shape: sbuf(ctx, nc, name, shape)
        k.ident = sb("ident", [P, P])
        with nc.sbuf_tensor("weights_low", [P, 2, KC, WCH], F32) as k.w_low:
            pass
        k.wbuf = [sb(f"weights{i}", [P, KC, WCH]) for i in range(2)]
        k.shift, k.scale = sb("mod_shift", [P, KC, 2]), sb("mod_scale", [P, KC, 2])
        k.inv_sum = sb("inv_sum", [P, 2, 2, HW])
        k.skip = sb("hy_skip_rows", [P, 2, HW])
        s_start = ctx.enter_context(nc.semaphore("start_copied"))
        k.w_here = [k.sem(f"weights{i}_here") for i in range(2)]

        with nc.Block() as block:
            @block.sync
            def _(sp):
                sp.dma_start(k.ident[:, :], a["ident"]).then_inc(s_start, 16)
                sp.dma_start(out[0], a["x"][0]).then_inc(s_start, 16)
                sp.dma_start(k.context, a["ctx"][0]).then_inc(s_start, 16)
                sp.wait_ge(s_start, 48)

        with nc.Fori(0, depth) as layer:
            k.layer = layer
            with ExitStack() as held:
                sb = lambda name, shape: sbuf(held, nc, name, shape, side="right")
                weights_stage(k)
                with nc.sbuf_tensor("hxT", [P, KC, TOK], F32) as k.hxT:
                    norm_stage(k)
                    k.z_hy = sb("z_hyena", [P, 2, TOK])
                    hyena_stage(k)
                    k.z_na = sb("z_attention", [P, 4, TOK])
                    attention_stage(k)
                    k.z_re = sb("z_retention", [P, 2, TOK])
                    retention_stage(k)
                output_stage(k)
            with nc.Block() as block:
                @block.vector
                def _(dve):
                    for s in k.sems:
                        dve.sem_clear(s)


def build(nc, arrays):
    a = {n: nc.dram_tensor("in_" + n, v.shape, F32, kind="ExternalInput").ap() for n, v in arrays.items()}
    out = nc.dram_tensor("out", (1, L, D), F32, kind="ExternalOutput").ap()
    spectra = nc.dram_tensor("filter_spectra", (2, P, 22, HW), F32, kind="Internal").ap()
    context = nc.dram_tensor("context_stream", (LC, D), F32, kind="Internal").ap()
    columns = nc.dram_tensor("context_hyena_columns", (P, TC, 4 * HW), F32, kind="Internal").ap()
    gates = nc.dram_tensor("gates", (1, 2, D), F32, kind="Internal").ap()
    return a, out, (spectra, context, columns, gates)


def laid_out(inputs):
    arrays = {n: np.ascontiguousarray(inputs[n]) for n in INPUTS}
    arrays["na_rpb"] = np.ascontiguousarray(np.pad(arrays["na_rpb"], ((0, 0), (0, 0), (1, 1), (GRID + 1 - KW, GRID - KW)))[..., ::-1])
    arrays.update(constants())
    return arrays


def kernel(**inputs):
    import concourse.bacc as bacc
    from concourse.bass_utils import run_bass_kernel_spmd

    arrays = laid_out(inputs)
    nc = bacc.Bacc("TRN2", target_bir_lowering=False, num_devices=1)
    a, out, scratch = build(nc, arrays)
    program(nc, a, out, scratch)
    r = run_bass_kernel_spmd(nc, [{"in_" + n: v for n, v in arrays.items()}], core_ids=[0])
    return r.results[0]["out"]
```
